# Optimizing a Trainium2 kernel written in Bass

```python
import jax, jax.numpy as jnp
from jax import lax
import numpy as np
import math

D_MODEL = 1024
BATCH = 1
SEQ = 256
DEPTH = 1

CHUNK = 64
Q_BLOCK = 128
SB_HEADS = 8
SB_HEAD_DIM = 64
SB_WIDTH = SB_HEADS * SB_HEAD_DIM
RW_HEADS = 8
RW_HEAD_DIM = 64
RW_WIDTH = RW_HEADS * RW_HEAD_DIM
W_LORA = 64
A_LORA = 64
G_LORA = 128
GN_EPS = RW_HEAD_DIM * 1e-5
N_BRANCH = 2
SB_COLS = 3 * SB_WIDTH
RW_COLS = 3 * RW_WIDTH + W_LORA + A_LORA + G_LORA
GATE_COLS = N_BRANCH * D_MODEL
IN_COLS = SB_COLS + RW_COLS + GATE_COLS
D_FF = ((8 * D_MODEL + 3 * 256 - 1) // (3 * 256)) * 256
RMS_EPS = 1e-6


def rms_norm(x, g):
    xf = x.astype(jnp.float32)
    y = xf * lax.rsqrt(jnp.mean(xf * xf, axis=-1, keepdims=True) + RMS_EPS)
    return (y * g).astype(x.dtype)

def token_shift(p):
    return jnp.pad(p, ((0, 0), (1, 0), (0, 0)))[:, :-1]

def stick_breaking_attention(q, k, v):
    B, S, H, Dh = q.shape
    scale = Dh ** -0.5
    outs = []
    for i in range(S // Q_BLOCK):
        q0 = i * Q_BLOCK
        kv_len = q0 + Q_BLOCK
        qb = q[:, q0:kv_len]
        kb = k[:, :kv_len]
        vb = v[:, :kv_len]
        z = jnp.einsum('bqhd,bkhd->bhqk', qb, kb).astype(jnp.float32) * scale
        t_idx = q0 + jnp.arange(Q_BLOCK)[:, None]
        s_idx = jnp.arange(kv_len)[None, :]
        strict = s_idx < t_idx
        log_fail = jnp.where(strict, jax.nn.log_sigmoid(-z), 0.0)
        after = lax.cumsum(log_fail, axis=3, reverse=True) - log_fail
        w = jnp.where(strict, jnp.exp(jax.nn.log_sigmoid(z) + after), 0.0)
        outs.append(jnp.einsum('bhqk,bkhd->bqhd', w.astype(vb.dtype), vb))
    return jnp.concatenate(outs, axis=1)

def wkv7_scan(r, decay, k, v, kk, a):
    B, S, H, N = r.shape

    def to_chunks(t):
        return t.astype(jnp.float32).transpose(1, 0, 2, 3).reshape(S // CHUNK, CHUNK, B, H, N)

    def step(state, inp):
        r_t, w_t, k_t, v_t, kk_t, a_t = inp
        sa = jnp.einsum('bhvk,bhk->bhv', state, -kk_t)
        state = (state * w_t[:, :, None, :]
                 + sa[..., None] * (kk_t * a_t)[:, :, None, :]
                 + v_t[..., None] * k_t[:, :, None, :])
        return state, jnp.einsum('bhvk,bhk->bhv', state, r_t)

    def chunk_step(state, chunk_inp):
        return lax.scan(step, state, chunk_inp)

    state0 = jnp.zeros((B, H, N, N), jnp.float32)
    _, y = lax.scan(chunk_step, state0, tuple(to_chunks(t) for t in (r, decay, k, v, kk, a)))
    return y.reshape(S, B, H, N).transpose(1, 0, 2, 3)

def rwkv7_time_mix(p, mu, w0, w_up, a0, a_up, g_up, k_k, k_a, r_k, lnx_w, lnx_b):
    B, S, _ = p.shape
    H, N = RW_HEADS, RW_HEAD_DIM
    p = p + (token_shift(p) - p) * mu
    o1, o2, o3 = RW_WIDTH, 2 * RW_WIDTH, 3 * RW_WIDTH
    r, k, v = p[..., :o1], p[..., o1:o2], p[..., o2:o3]
    xw = p[..., o3:o3 + W_LORA]
    xa = p[..., o3 + W_LORA:o3 + W_LORA + A_LORA]
    xg = p[..., o3 + W_LORA + A_LORA:]
    w_raw = (w0 + jnp.tanh(xw) @ w_up).astype(jnp.float32)
    decay = jnp.exp(-jnp.exp(-jax.nn.softplus(-w_raw) - 0.5))
    a = jax.nn.sigmoid((a0 + xa @ a_up).astype(jnp.float32))
    g = jax.nn.sigmoid(xg) @ g_up
    kk = (k * k_k).astype(jnp.float32).reshape(B, S, H, N)
    kk = kk / jnp.maximum(jnp.linalg.norm(kk, axis=-1, keepdims=True), 1e-12)
    k = k.astype(jnp.float32) * (1.0 + (a - 1.0) * k_a)
    heads = lambda t: t.astype(jnp.float32).reshape(B, S, H, N)
    r_h, k_h, v_h = heads(r), heads(k), heads(v)
    y = wkv7_scan(r_h, heads(decay), k_h, v_h, kk, heads(a))
    mean = jnp.mean(y, axis=-1, keepdims=True)
    var = jnp.mean(jnp.square(y - mean), axis=-1, keepdims=True)
    y = ((y - mean) * lax.rsqrt(var + GN_EPS)).reshape(B, S, RW_WIDTH) * lnx_w + lnx_b
    bonus = (jnp.sum(r_h * k_h * r_k, axis=-1, keepdims=True) * v_h).reshape(B, S, RW_WIDTH)
    return ((y + bonus) * g).astype(p.dtype)

def first_inputs(seed: int = 0) -> dict:
    key = jax.random.key(seed)
    ks = jax.random.split(key, 24)
    L, D = DEPTH, D_MODEL
    nrm = lambda k_, shape, s: jax.random.normal(k_, shape, jnp.float32) * s
    return {
        "x": nrm(ks[0], (BATCH, SEQ, D), 1.0),
        "norm_mix_pre": 1.0 + nrm(ks[1], (L, D), 0.1),
        "w_in": nrm(ks[2], (L, D, IN_COLS), D ** -0.5),
        "b_gate": nrm(ks[3], (L, GATE_COLS), 0.1),
        "mu_rw": jax.random.uniform(ks[4], (L, RW_COLS), jnp.float32),
        "w0": jax.random.uniform(ks[5], (L, RW_WIDTH), jnp.float32, -6.0, 0.0),
        "w_up": nrm(ks[6], (L, W_LORA, RW_WIDTH), 0.1),
        "a0": nrm(ks[7], (L, RW_WIDTH), 0.1),
        "a_up": nrm(ks[8], (L, A_LORA, RW_WIDTH), 0.5 * A_LORA ** -0.5),
        "g_up": nrm(ks[9], (L, G_LORA, RW_WIDTH), G_LORA ** -0.5),
        "k_k": 0.85 + nrm(ks[10], (L, RW_WIDTH), 0.05),
        "k_a": 1.0 + nrm(ks[11], (L, RW_WIDTH), 0.05),
        "r_k": nrm(ks[12], (L, RW_HEADS, RW_HEAD_DIM), 0.1),
        "lnx_w": 1.0 + nrm(ks[13], (L, RW_WIDTH), 0.1),
        "lnx_b": nrm(ks[14], (L, RW_WIDTH), 0.02),
        "w_sb_out": nrm(ks[15], (L, SB_WIDTH, D), SB_WIDTH ** -0.5),
        "w_rw_out": nrm(ks[16], (L, RW_WIDTH, D), RW_WIDTH ** -0.5),
        "w_o": nrm(ks[17], (L, D, D), D ** -0.5),
        "norm_mix_post": 1.0 + nrm(ks[18], (L, D), 0.1),
        "norm_ffn_pre": 1.0 + nrm(ks[19], (L, D), 0.1),
        "w_ffn_gate": nrm(ks[20], (L, D, D_FF), D ** -0.5),
        "w_ffn_up": nrm(ks[21], (L, D, D_FF), D ** -0.5),
        "w_ffn_down": nrm(ks[22], (L, D_FF, D), D_FF ** -0.5),
        "norm_ffn_post": 1.0 + nrm(ks[23], (L, D), 0.1),
    }

def first_block(x, norm_mix_pre, w_in, b_gate, mu_rw, w0, w_up, a0, a_up, g_up, k_k, k_a, r_k,
              lnx_w, lnx_b, w_sb_out, w_rw_out, w_o, norm_mix_post, norm_ffn_pre,
              w_ffn_gate, w_ffn_up, w_ffn_down, norm_ffn_post):
    B, S, D = x.shape
    for l in range(DEPTH):
        h = rms_norm(x, norm_mix_pre[l])
        proj = h @ w_in[l]
        p_sb = proj[..., :SB_COLS]
        p_rw = proj[..., SB_COLS:SB_COLS + RW_COLS]
        gates = jax.nn.sigmoid(proj[..., SB_COLS + RW_COLS:] + b_gate[l])
        q = p_sb[..., :SB_WIDTH].reshape(B, S, SB_HEADS, SB_HEAD_DIM)
        k = p_sb[..., SB_WIDTH:2 * SB_WIDTH].reshape(B, S, SB_HEADS, SB_HEAD_DIM)
        v = p_sb[..., 2 * SB_WIDTH:].reshape(B, S, SB_HEADS, SB_HEAD_DIM)
        o_sb = stick_breaking_attention(q, k, v).reshape(B, S, SB_WIDTH)
        o_rw = rwkv7_time_mix(p_rw, mu_rw[l], w0[l], w_up[l], a0[l], a_up[l], g_up[l],
                              k_k[l], k_a[l], r_k[l], lnx_w[l], lnx_b[l])
        merged = (gates[..., :D] * (o_sb @ w_sb_out[l])
                  + gates[..., D:] * (o_rw @ w_rw_out[l]))
        x = x + rms_norm(merged @ w_o[l], norm_mix_post[l])
        h = rms_norm(x, norm_ffn_pre[l])
        f = (jax.nn.silu(h @ w_ffn_gate[l]) * (h @ w_ffn_up[l])) @ w_ffn_down[l]
        x = x + rms_norm(f, norm_ffn_post[l])
    return x


MEM_LEN = 256
ATT_WIDTH = D_MODEL // 2
HEAD_DIM = 64
N_ATT_HEADS = ATT_WIDTH // HEAD_DIM
CONV_WIDTH = D_MODEL - ATT_WIDTH
CONV_K = 3
DILATED_PATTERNS = ((128, 1), (512, 4), (2048, 16))
N_MEM_HEADS = 4
MEM_HEAD_DIM = D_MODEL // N_MEM_HEADS
D_FF_2 = 4 * D_MODEL
NORM_EPS = 1e-6
NEG_INF = -1e30
IN_COLS_2 = 3 * ATT_WIDTH + 3 * CONV_WIDTH


def rms_norm_2(x, g):
    xf = x.astype(jnp.float32)
    y = xf * lax.rsqrt(jnp.mean(xf * xf, axis=-1, keepdims=True) + NORM_EPS)
    return (y * g.astype(jnp.float32)).astype(x.dtype)

def dilated_window_attention(q, k, v, window, dilation):
    b, s, h, e = q.shape
    steps = window // dilation
    span = steps * dilation
    s_pad = -(-s // span) * span
    nb = s_pad // span
    pad = ((0, 0), (0, s_pad - s), (0, 0), (0, 0))

    def blocks(t):
        return jnp.pad(t, pad).reshape(b, nb, steps, dilation, h, e)

    def with_prev(t):
        prev = jnp.pad(t, ((0, 0), (1, 0), (0, 0), (0, 0), (0, 0), (0, 0)))[:, :-1]
        return jnp.concatenate([prev, t], axis=2)

    qb = blocks(q)
    kk = with_prev(blocks(k))
    vv = with_prev(blocks(v))
    scale = 1.0 / math.sqrt(e)
    scores = jnp.einsum('bnqrhe,bnkrhe->bnrhqk', qb, kk).astype(jnp.float32) * scale
    i = jnp.arange(steps)[:, None]
    j = jnp.arange(2 * steps)[None, :]
    band = (j >= i) & (j <= i + steps)
    has_prev = (jnp.arange(nb) > 0)[:, None, None]
    valid = band[None] & (has_prev | (j[None] >= steps))
    scores = jnp.where(valid[None, :, None, None], scores, NEG_INF)
    lse = jax.nn.logsumexp(scores, axis=-1)
    p = jnp.exp(scores - lse[..., None]).astype(v.dtype)
    o = jnp.einsum('bnrhqk,bnkrhe->bnqrhe', p, vv)
    o = o.reshape(b, s_pad, h, e)[:, :s]
    lse = jnp.transpose(lse, (0, 1, 4, 2, 3)).reshape(b, s_pad, h)[:, :s]
    return o, lse

def short_gated_conv(bg, cg, xc, conv_w):
    u = cg * xc
    up = jnp.pad(u, ((0, 0), (CONV_K - 1, 0), (0, 0)))
    s = u.shape[1]
    conv = sum(up[:, tap:tap + s] * conv_w[tap] for tap in range(CONV_K))
    return bg * conv

def hybrid_mixer(h, w_in, conv_w, g_attn_out, g_conv_out, w_out):
    b, s, _ = h.shape
    proj = h @ w_in
    q, k, v, bg, cg, xc = jnp.split(proj, 6, axis=-1)
    q = q.reshape(b, s, N_ATT_HEADS, HEAD_DIM)
    k = k.reshape(b, s, N_ATT_HEADS, HEAD_DIM)
    v = v.reshape(b, s, N_ATT_HEADS, HEAD_DIM)
    outs, lses = [], []
    for window, dilation in DILATED_PATTERNS:
        o, lse = dilated_window_attention(q, k, v, window, dilation)
        outs.append(o)
        lses.append(lse)
    mix_w = jax.nn.softmax(jnp.stack(lses, axis=0), axis=0)
    attn = jnp.einsum('pbsh,pbshe->bshe', mix_w, jnp.stack(outs, axis=0).astype(jnp.float32))
    attn = attn.astype(h.dtype).reshape(b, s, ATT_WIDTH)
    conv = short_gated_conv(bg, cg, xc, conv_w)
    merged = jnp.concatenate([rms_norm_2(attn, g_attn_out), rms_norm_2(conv, g_conv_out)], axis=-1)
    return merged @ w_out

def memory_cross_attention(h, mem_n, w_q_mem, w_kv_mem, w_o_mem):
    b, s, _ = h.shape
    q = (h @ w_q_mem).reshape(b, s, N_MEM_HEADS, MEM_HEAD_DIM)
    kv = mem_n @ w_kv_mem
    k, v = jnp.split(kv, 2, axis=-1)
    k = k.reshape(b, MEM_LEN, N_MEM_HEADS, MEM_HEAD_DIM)
    v = v.reshape(b, MEM_LEN, N_MEM_HEADS, MEM_HEAD_DIM)
    scores = jnp.einsum('bshe,bmhe->bhsm', q, k).astype(jnp.float32) / math.sqrt(MEM_HEAD_DIM)
    p = jax.nn.softmax(scores, axis=-1).astype(v.dtype)
    o = jnp.einsum('bhsm,bmhe->bshe', p, v).reshape(b, s, D_MODEL)
    return o @ w_o_mem

def squared_relu_mlp(h, w_up, w_down):
    a = jax.nn.relu(h @ w_up)
    return (a * a) @ w_down

def second_inputs(seed: int = 0) -> dict:
    key = jax.random.key(seed)
    ks = jax.random.split(key, 17)
    f32 = jnp.float32

    def dense(k, fan_in, shape, gain=1.0):
        return jax.random.normal(k, shape, f32) * (gain * fan_in ** -0.5)

    def gain(k, n):
        return 1.0 + 0.02 * jax.random.normal(k, (n,), f32)

    return {
        "x": jax.random.normal(ks[0], (BATCH, SEQ, D_MODEL), f32),
        "mem": jax.random.normal(ks[1], (BATCH, MEM_LEN, D_MODEL), f32),
        "g_mix": gain(ks[2], D_MODEL),
        "w_in": dense(ks[3], D_MODEL, (D_MODEL, IN_COLS_2)),
        "conv_w": dense(ks[4], CONV_K, (CONV_K, CONV_WIDTH)),
        "g_attn_out": gain(ks[5], ATT_WIDTH),
        "g_conv_out": gain(ks[6], CONV_WIDTH),
        "w_out": dense(ks[7], D_MODEL, (D_MODEL, D_MODEL), 0.5),
        "g_xattn": gain(ks[8], D_MODEL),
        "g_mem": gain(ks[9], D_MODEL),
        "w_q_mem": dense(ks[10], D_MODEL, (D_MODEL, D_MODEL)),
        "w_kv_mem": dense(ks[11], D_MODEL, (D_MODEL, 2 * D_MODEL)),
        "w_o_mem": dense(ks[12], D_MODEL, (D_MODEL, D_MODEL), 0.5),
        "g_mlp": gain(ks[13], D_MODEL),
        "w_up": dense(ks[14], D_MODEL, (D_MODEL, D_FF_2)),
        "w_down": dense(ks[15], D_FF_2, (D_FF_2, D_MODEL), 0.5),
        "g_final": gain(ks[16], D_MODEL),
    }

def second_block(x, mem, g_mix, w_in, conv_w, g_attn_out, g_conv_out, w_out,
              g_xattn, g_mem, w_q_mem, w_kv_mem, w_o_mem,
              g_mlp, w_up, w_down, g_final):
    for _ in range(DEPTH):
        x = x + hybrid_mixer(rms_norm_2(x, g_mix), w_in, conv_w, g_attn_out, g_conv_out, w_out)
        x = x + memory_cross_attention(rms_norm_2(x, g_xattn), rms_norm_2(mem, g_mem),
                                       w_q_mem, w_kv_mem, w_o_mem)
        x = x + squared_relu_mlp(rms_norm_2(x, g_mlp), w_up, w_down)
    return rms_norm_2(x, g_final)


def setup_inputs(seed=0):
    out = dict(first_inputs(seed))
    for name, value in second_inputs(seed + 1).items():
        if name != "x":
            out[name + "_2"] = value
    return out


def reference(
    x, norm_mix_pre, w_in, b_gate, mu_rw, w0, w_up, a0, a_up, g_up, k_k, k_a, r_k, lnx_w, lnx_b,
    w_sb_out, w_rw_out, w_o, norm_mix_post, norm_ffn_pre, w_ffn_gate, w_ffn_up, w_ffn_down,
    norm_ffn_post, mem_2, g_mix_2, w_in_2, conv_w_2, g_attn_out_2, g_conv_out_2, w_out_2,
    g_xattn_2, g_mem_2, w_q_mem_2, w_kv_mem_2, w_o_mem_2, g_mlp_2, w_up_2, w_down_2, g_final_2,
):
    x = first_block(
        x, norm_mix_pre, w_in, b_gate, mu_rw, w0, w_up, a0, a_up, g_up, k_k, k_a, r_k, lnx_w,
        lnx_b, w_sb_out, w_rw_out, w_o, norm_mix_post, norm_ffn_pre, w_ffn_gate, w_ffn_up,
        w_ffn_down, norm_ffn_post,
    )
    return second_block(
        x, mem_2, g_mix_2, w_in_2, conv_w_2, g_attn_out_2, g_conv_out_2, w_out_2, g_xattn_2,
        g_mem_2, w_q_mem_2, w_kv_mem_2, w_o_mem_2, g_mlp_2, w_up_2, w_down_2, g_final_2,
    )


_drawn_inputs = setup_inputs


def setup_inputs(seed=0):
    import zlib

    import numpy as np

    out = dict(_drawn_inputs(seed))
    spreads = {}
    factors = {'lnx_b': 4.558,
     'g_mix_2': 6.088,
     'g_attn_out_2': 8.0,
     'g_conv_out_2': 8.0,
     'g_xattn_2': 8.0,
     'g_mem_2': 8.0,
     'g_mlp_2': 7.439,
     'g_final_2': 2.725}
    for name, (base, spread) in spreads.items():
        noise = np.random.default_rng([zlib.crc32(name.encode()), seed]).standard_normal(out[name].shape)
        drawn = base * np.exp(spread * noise) if base else spread * noise
        out[name] = __import__('jax').numpy.asarray(drawn.astype(out[name].dtype))
    for name, factor in factors.items():
        out[name] = (out[name] * factor).astype(out[name].dtype)
    return out
```

```python
import concourse.bass as bass
from concourse import mybir
from contextlib import ExitStack
import numpy as np

P = 128
SEQ = 256
NT = SEQ // P
D = 1024
KD = D // P
HW = 512
NPAIR = HW // P
HD = 64
NH = HW // HD
CHUNK = 64
RW0 = 3 * HW
GATE0 = RW0 + 3 * HW + 256
DFF = ((8 * D + 3 * 256 - 1) // (3 * 256)) * 256
DFF2 = 4 * D
FF_CHUNKS = DFF // 256
FF2_CHUNKS = DFF2 // 256
MEM_HEADS = 4
RING = 3
UNIT = 2048

PARAM_ROWS = [("norm_mix_pre", 8), ("b_gate", 16), ("mu_rw", 14), ("w0", 4), ("a0", 4), ("k_k", 4),
              ("k_a", 4), ("r_k", 4), ("lnx_w", 4), ("lnx_b", 4), ("norm_ffn_pre", 8), ("conv_w_2", 12),
              ("g_conv_out_2", 4), ("g_attn_out_2", 4), ("g_mix_2", 8), ("g_xattn_2", 8), ("g_mem_2", 8),
              ("g_mlp_2", 8)]
PCOL = {}
_at = 0
for _n, _k in PARAM_ROWS:
    PCOL[_n] = _at
    _at += _k
NPARAM = _at


def shape_constants():
    i = np.arange(P)[:, None]
    j = np.arange(P)[None, :]
    t = np.arange(SEQ)[None, :]
    parts, cols, at = [], {}, 0

    def put(name, a):
        nonlocal at
        a = np.broadcast_to(a, (P, a.shape[1])).astype(np.float32)
        cols[name] = (at, at + a.shape[1])
        parts.append(a)
        at += a.shape[1]

    same = (i // CHUNK) == (j // CHUNK)
    put("ident", (i == j) * 1.0)
    put("tri", (i >= j) * 1.0)
    put("ones", np.ones((P, P)))
    put("blockones", same * 1.0)
    put("incl", (same & (i <= j)) * 1.0)
    put("strict", (same & (i < j)) * 1.0)
    for m in (1, 2, 4, 8, 16, 32):
        two = (i // (2 * m)) == (j // (2 * m))
        put(f"level{m}", (two & (i % (2 * m) < m) & (j % (2 * m) >= m)) * 1.0)
    ks = np.concatenate([(i < t), (i + P < t[:, P:])], 1)
    put("sb_neg", ks * -1.0)
    put("sb_add", np.where(ks, 0.0, -1e30))

    def count(q, s):
        d = q - s
        c = ((d >= 0) & (d <= 128)) * 1 + ((d >= 0) & (d % 4 == 0)) * 1 + ((d >= 0) & (d % 16 == 0)) * 1
        return np.where(c > 0, np.log(np.maximum(c, 1)), -1e30)

    put("dil", np.concatenate([count(i, j), count(i + P, t)], 1))
    put("reset", (t % CHUNK != 0) * 1.0)
    return np.concatenate(parts, 1), cols


CONSTS, CCOL = shape_constants()
NCONST = CONSTS.shape[1]


def block_kernel(nc, A, out, dbg=None):
    f32 = mybir.dt.float32
    f32r = mybir.dt.float32r
    ALU = mybir.AluOpType
    ACT = mybir.ActivationFunctionType
    AX = mybir.AxisListType
    KB = 1024
    BASE = 16512

    ctx = ExitStack()
    with ctx:
        def at(name, kb, shape, dt=f32):
            return nc.alloc_sbuf_tensor_at(name, shape, dt, offset=BASE + int(kb * KB))

        sems = {}

        def sem(name):
            if name not in sems:
                sems[name] = ctx.enter_context(nc.semaphore(name))
            return sems[name]

        raw = [at(f"raw{i}", 8 * i, [P, UNIT]) for i in range(RING)]
        whi = [at(f"whi{i}", 24 + 16 * i, [P, UNIT], f32r) for i in range(RING)]
        wlo = [at(f"wlo{i}", 32 + 16 * i, [P, UNIT], f32r) for i in range(RING)]
        cst = at("cst", 72, [P, NCONST])
        par = at("par", 84, [P, NPARAM])
        small = at("small", 84.5, [P, 128])
        XR = 85
        xres = at("xres", XR, [P, NT, D])
        A0 = 93
        xh = at("xh", A0, [P, KD, SEQ], f32r)
        xl = at("xl", A0 + 8, [P, KD, SEQ], f32r)
        W = 109
        gates = at("gates", W, [P, 16, SEQ])
        sboh = at("sboh", W + 16, [P, NPAIR, SEQ], f32r)
        sbol = at("sbol", W + 20, [P, NPAIR, SEQ], f32r)
        xn = at("xn", W + 24, [P, NT, D])
        rw = at("rw", W + 24, [P, 14, SEQ])
        eP = at("eP", W + 38, [P, NPAIR, SEQ])
        eN = at("eN", W + 42, [P, NPAIR, SEQ])
        eX = at("eX", W + 46, [P, NPAIR, SEQ])
        kk = at("kk", W + 50, [P, NPAIR, SEQ])
        sg = at("sg", W + 54, [P, NPAIR, SEQ])
        cs = at("cs", W + 58, [P, NPAIR, SEQ])
        ag = at("ag", W + 62, [P, NPAIR, SEQ])
        kq = at("kq", W + 66, [P, NPAIR, SEQ])
        sq = at("sq", W + 70, [P, NPAIR, SEQ])
        sk = at("sk", W + 74, [P, NPAIR, SEQ])
        sv = at("sv", W + 78, [P, NT, HW])
        st1 = [at(f"st1{i}", W + 82 + 6 * i, [P, 384]) for i in range(2)]
        st2 = [at(f"st2{i}", W + 83.5 + 6 * i, [P, 384]) for i in range(2)]
        st3 = [at(f"st3{i}", W + 85 + 6 * i, [P, 384]) for i in range(2)]
        st4 = [at(f"st4{i}", W + 86.5 + 6 * i, [P, 384]) for i in range(2)]
        lora = at("lora", W + 94, [P, HW])
        gup = at("gup", W + 96, [P, HW])
        stg = [at(f"stg{i}", XR + 2.0625 * i, [P, 2, SEQ + 1]) for i in range(2)]
        diff = at("diff", XR + 4.25, [P, 2, SEQ])
        Tm = at("Tm", W + 54, [P, NH, P])
        TT = at("TT", W + 58, [P, NH, P])
        Gm = at("Gm", W + 62, [P, NH, P])
        Xm = at("Xm", W + 66, [P, NH, P])
        XT = at("XT", W + 70, [P, NH, P])
        AK = at("AK", W + 74, [P, NH, P])
        RB = at("RB", W + 78, [P, NH, P])
        RK = at("RK", W + 82, [P, NH, P])
        St = at("St", W + 86, [P, 4, NPAIR, P])
        yT = at("yT", XR, [P, NPAIR, SEQ])
        dS = at("dS", XR + 4, [P, NPAIR, P])
        at_ = at("a_tok", A0, [P, HW])
        bt_ = at("b_tok", A0 + 2, [P, HW])
        kt_ = at("k_tok", A0 + 4, [P, HW])
        vt_ = at("v_tok", A0 + 6, [P, HW])
        WT = at("WT", A0 + 8, [P, NPAIR, P])
        AV = at("AV", A0 + 10, [P, HW])
        U0 = at("U0", A0 + 12, [P, HW])
        Uc = at("Uc", A0 + 14, [P, HW])
        yc = at("yc", W + 54, [P, NPAIR, SEQ])
        yq = at("yq", W + 58, [P, NPAIR, SEQ])
        bon = at("bon", W + 62, [P, NPAIR, SEQ])
        orw = at("orw", W + 66, [P, NPAIR, SEQ])
        rwoh = at("rwoh", W + 70, [P, NPAIR, SEQ], f32r)
        rwol = at("rwol", W + 74, [P, NPAIR, SEQ], f32r)
        mh = at("mh", A0, [P, KD, SEQ], f32r)
        ml = at("ml", A0 + 8, [P, KD, SEQ], f32r)
        gmix = at("gmix", W + 38, [P, D])
        gffn = at("gffn", W + 42, [P, D])
        gfin = at("gfin", W + 46, [P, D])
        tmp = at("tmp", W + 16, [P, NT, D])
        junk = at("junk", W + 32, [P, D])
        fa = [at(f"fa{i}", W + 54 + 2 * i, [P, 2 * SEQ]) for i in range(2)]
        fb = [at(f"fb{i}", W + 58 + 2 * i, [P, 2 * SEQ]) for i in range(2)]
        fh = [at(f"fh{i}", W + 62 + 2 * i, [P, 2, SEQ], f32r) for i in range(2)]
        fl = [at(f"fl{i}", W + 66 + 2 * i, [P, 2, SEQ], f32r) for i in range(2)]
        q2 = at("q2", W, [P, NPAIR, SEQ])
        k2 = at("k2", W + 4, [P, NPAIR, SEQ])
        v2 = at("v2", W + 8, [P, NT, HW])
        att = at("att", W + 12, [P, NT, HW])
        cv = at("cv", W + 16, [P, 3, NPAIR, SEQ])
        m2h = at("m2h", W + 28, [P, KD, SEQ], f32r)
        m2l = at("m2l", W + 36, [P, KD, SEQ], f32r)
        dz = [at(f"dz{i}", W + 50 + 4.5 * i, [P, 384]) for i in range(2)]
        dp = [at(f"dp{i}", W + 51.5 + 4.5 * i, [P, 384]) for i in range(2)]
        dq = [at(f"dq{i}", W + 53 + 4.5 * i, [P, 384]) for i in range(2)]
        km = at("km", W + 59, [P, KD, SEQ])
        crs = at("crs", W + 67, [P, SEQ])
        memh = at("memh", W + 71, [P, KD, SEQ], f32r)
        meml = at("meml", W + 79, [P, KD, SEQ], f32r)
        mem = at("mem", W + 87, [P, NT, D])
        vm = at("vm", W + 87, [P, NT, D])
        qm = at("qm", W, [P, KD, SEQ])
        mp = [at(f"mp{i}", W + 8 + 4 * i, [P, NT, SEQ]) for i in range(2)]
        mq = [at(f"mq{i}", W + 10 + 4 * i, [P, NT, SEQ]) for i in range(2)]
        omh = at("omh", W + 16, [P, KD, SEQ], f32r)
        oml = at("oml", W + 24, [P, KD, SEQ], f32r)
        EVENTS = {"sq": (["n1", "p1", "n2", "p2", "n3", "mem", "att", "n4", "n5", "fin"], 2),
                  "sd": (["n1", "p1", "n2", "p2", "n3", "mem", "att", "n4", "n5", "fin"], 1),
                  "x": (["n2", "n3", "n4", "n5", "fin"], 2),
                  "xn": (["n1", "n2", "n3", "mem", "att", "n4", "n5", "fin"], 2),
                  "T": (["n1", "n2", "n3", "mem", "att", "n4", "n5"], KD),
                  "hi": (["n1", "n2", "n3", "mem", "att", "n4", "n5"], KD),
                  "xT": (["n1", "n2", "n3", "mem", "att", "n4", "n5"], KD)}

        def norm_sem(st, what):
            return sem("norm_" + what)

        def nth(st, what, n):
            order, each = EVENTS[what]
            before = order.index(st) * each
            if each == KD and "att" in order[:order.index(st)]:
                before -= KD - NPAIR
            return before + n

        PS = ctx.enter_context(nc.psum_tensor("PS", [P, 8 * 512], f32))

        def bank(b):
            return PS[:, b * 512:(b + 1) * 512]

        def C(name):
            a, b = CCOL[name]
            return cst[:, a:b]

        def par_col(name, i=0):
            c = PCOL[name] + i
            return par[:, c:c + 1]

        def col(i, n=1):
            return small[:, i:i + n]

        EPS, GEPS = 0, 1
        NORM = {n: 2 + 6 * i for i, n in enumerate(["n1", "p1", "n2", "p2", "n3", "mem", "att", "n4", "n5", "fin"])}
        DMX, DL, DRL = 62, 78, 94
        MMX, MSUM = 110, 118
        dec = at("dec", W + 98, [P, NPAIR, 4])

        units = []

        def cols_unit(w, c0, n=256):
            units.append((w[:, c0:c0 + n].rearrange("(k p) n -> p k n", p=P), n))
            return len(units) - 1

        def rows_unit(w, k0, k, c0=0, n=D):
            units.append((w[k0 * P:(k0 + k) * P, c0:c0 + n].rearrange("(k p) n -> p k n", p=P), n))
            return len(units) - 1

        w_in, w_in2, w_kv = A["w_in"][0], A["w_in_2"], A["w_kv_mem_2"]
        U_RW = [cols_unit(w_in, RW0 + c) for c in (1536, 512, 768, 0, 256, 1024, 1280)]
        RW_TILE = [12, 4, 6, 0, 2, 8, 10]
        U_QK = [cols_unit(w_in, 256 * c) for c in range(4)]
        U_V = [rows_unit(w_in, 4 * i, 4, 2 * HW, HW) for i in range(2)]
        U_G = [cols_unit(w_in, GATE0 + 256 * c) for c in range(8)]
        U_SO = [cols_unit(A["w_sb_out"][0], 512 * c, 512) for c in range(2)]
        U_RO = [cols_unit(A["w_rw_out"][0], 512 * c, 512) for c in range(2)]
        U_O = [rows_unit(A["w_o"][0], 2 * i, 2) for i in range(4)]
        U_F = {}
        for i in range(FF_CHUNKS + 1):
            if i < FF_CHUNKS:
                U_F["g", i] = cols_unit(A["w_ffn_gate"][0], 256 * i)
                U_F["u", i] = cols_unit(A["w_ffn_up"][0], 256 * i)
            if i:
                U_F["d", i - 1] = rows_unit(A["w_ffn_down"][0], 2 * (i - 1), 2)
        U_QK2 = [cols_unit(w_in2, 256 * c) for c in range(4)]
        U_V2 = [rows_unit(w_in2, 4 * i, 4, 2 * HW, HW) for i in range(2)]
        U_CV = [cols_unit(w_in2, 3 * HW + 256 * c) for c in range(6)]
        U_KM = [cols_unit(w_kv, 256 * c) for c in range(4)]
        U_VM = [rows_unit(w_kv, 2 * i, 2, D, D) for i in range(4)]
        U_O2 = [rows_unit(A["w_out_2"], 2 * i, 2) for i in range(4)]
        U_QM = [cols_unit(A["w_q_mem_2"], 256 * c) for c in range(4)]
        U_OM = [rows_unit(A["w_o_mem_2"], 2 * i, 2) for i in range(4)]
        U_M = {}
        for i in range(FF2_CHUNKS + 1):
            if i < FF2_CHUNKS:
                U_M["u", i] = cols_unit(A["w_up_2"], 256 * i)
            if i:
                U_M["d", i - 1] = rows_unit(A["w_down_2"], 2 * (i - 1), 2)
        NU = len(units)
        FILL2 = U_CV + U_KM

        raw_loaded = [sem(f"raw_loaded{i}") for i in range(RING)]

        block = ctx.enter_context(nc.Block())

        @block.sync
        def _(sp):
            sp.dma_start(xres[:], A["x"][0].rearrange("(t p) n -> p t n", p=P)).then_inc(sem("x_loaded"), 16)
            for u, (src, n) in enumerate(units):
                s = u % RING
                if u >= RING:
                    sp.wait_ge(sem("unit_split"), u - RING + 1)
                sp.dma_start(raw[s][:].rearrange("p (k n) -> p k n", n=n), src).then_inc(raw_loaded[s], 16)
                if u == U_O[0]:
                    sp.wait_ge(sem("yc_ready"), 2)
                    sp.dma_start(xres[:], A["x"][0].rearrange("(t p) n -> p t n", p=P)).then_inc(sem("x_loaded"), 16)
                    sp.dma_start(gmix[:], A["norm_mix_post"].rearrange("a n -> (a n)").partition_broadcast(P)).then_inc(sem("gmix_loaded"), 16)
                    sp.dma_start(gffn[:], A["norm_ffn_post"].rearrange("a n -> (a n)").partition_broadcast(P)).then_inc(sem("gffn_loaded"), 16)
                    sp.dma_start(gfin[:], A["g_final_2"].partition_broadcast(P)).then_inc(sem("gfin_loaded"), 16)
                    sp.dma_start(mem[:], A["mem_2"][0].rearrange("(t p) n -> p t n", p=P)).then_inc(sem("mem_loaded"), 16)
            for tt in range(NT):
                sp.wait_ge(norm_sem("fin", "xn"), nth("fin", "xn", tt + 1))
                sp.dma_start(out[0, tt * P:(tt + 1) * P, :], xn[:, tt, :]).then_inc(sem("stored"), 16)
            sp.wait_ge(sem("stored"), 16 * NT)

        @block.tensor
        def _(pe):
            def mm(o, l, r, start, stop, **kw):
                return nc.tensor.matmul(o, l, r, start=start, stop=stop, **kw)

            def slot(h):
                return 4 * (h % 2) + h // 2

            def split(u, n):
                pe.wait_ge(sem("unit_split"), u + 1)
                return (whi[u % RING][:].rearrange("p (k n) -> p k n", n=n),
                        wlo[u % RING][:].rearrange("p (k n) -> p k n", n=n))

            def by_feature(u, hi, lo, b):
                n = units[u][1]
                kt = UNIT // n
                wh, wl = split(u, n)
                for f in range(n // P):
                    o = PS[:, b * 512 + f * SEQ:b * 512 + (f + 1) * SEQ]
                    for k in range(kt):
                        fs = slice(f * P, (f + 1) * P)
                        mm(o, wh[:, k, fs], hi[:, k, :], k == 0, False)
                        mm(o, wh[:, k, fs], lo[:, k, :], False, False)
                        last = mm(o, wl[:, k, fs], hi[:, k, :], False, k == kt - 1)
                last.then_inc(sem("units_used"), 1)

            def by_token(u, hi, lo, k0, b, first, end):
                n = units[u][1]
                kt = UNIT // n
                wh, wl = split(u, n)
                for k in range(kt):
                    for t in range(NT):
                        ts = slice(t * P, (t + 1) * P)
                        for c in range(n // 512):
                            o = bank(b + t * (n // 512) + c)
                            ns = slice(c * 512, (c + 1) * 512)
                            mm(o, hi[:, k0 + k, ts], wh[:, k, ns], first and k == 0, False)
                            mm(o, hi[:, k0 + k, ts], wl[:, k, ns], False, False)
                            last = mm(o, lo[:, k0 + k, ts], wh[:, k, ns], False, end and k == kt - 1)
                last.then_inc(sem("units_used"), 1)

            def transpose_in(st, src, nf, b):
                for f in range(nf):
                    if f == 0:
                        pe.wait_ge(norm_sem(st, "xn"), nth(st, "xn", NT))
                    for t in range(NT):
                        last = nc.tensor.transpose(
                            PS[:, b * 512 + f * SEQ + t * P:b * 512 + f * SEQ + (t + 1) * P],
                            src[:, t, f * P:(f + 1) * P], C("ident"))
                    last.then_inc(norm_sem(st, "T"), 1)

            pe.wait_ge(sem("cst_loaded"), 16)
            transpose_in("n1", xn, KD, 4)
            pe.wait_ge(norm_sem("n1", "xT"), nth("n1", "xT", KD))
            for i, u in enumerate(U_RW):
                if i >= 2:
                    pe.wait_ge(sem("out_evac"), i - 1)
                by_feature(u, xh, xl, i % 2)
                if i == 1:
                    pe.wait_ge(sem("lora_in"), 1)
                    pe.wait_ge(sem("lora_loaded"), 48)
                    for j in range(NPAIR):
                        mm(PS[:, 4 * 512 + j * SEQ:4 * 512 + (j + 1) * SEQ], lora[0:HD, j * P:(j + 1) * P],
                           rw[0:HD, 12, :], True, True)
                    for j in range(NPAIR):
                        last = mm(PS[:, 6 * 512 + j * SEQ:6 * 512 + (j + 1) * SEQ], lora[HD:P, j * P:(j + 1) * P],
                                  rw[HD:P, 12, :], True, True)
                    last.then_inc(sem("lora_out"), 1)
                if i == 4:
                    pe.wait_ge(sem("kk_sq"), 1)
                    pe.wait_ge(sem("lora_evac"), 1)
                    for j in range(NPAIR):
                        last = mm(PS[:, 4 * 512 + j * SEQ:4 * 512 + (j + 1) * SEQ], C("blockones"), kq[:, j, :], True, True)
                    last.then_inc(sem("kk_ss"), 1)
            for i, u in enumerate(U_QK):
                pe.wait_ge(sem("out_evac"), i + 6)
                by_feature(u, xh, xl, (i + 7) % 2)
            for i, u in enumerate(U_V):
                by_token(u, xh, xl, 4 * i, 2, i == 0, i == 1)
            pe.wait_ge(sem("kk_sd"), 1)
            for i in range(NH + 1):
                r = slice(HD * (i % 2), HD * (i % 2) + HD)
                b = 4 + i % 2
                if i < NH:
                    if i == 0:
                        pe.wait_ge(sem("out_evac"), 11)
                    if i >= 2:
                        pe.wait_ge(sem("sb_arg_read"), i - 1)
                    mm(PS[:, b * 512:b * 512 + SEQ], sk[r, i // 2, 0:P], sq[r, i // 2, :], True, False, skip_group_check=True)
                    mm(PS[:, b * 512 + SEQ:b * 512 + 384], sk[r, i // 2, P:SEQ], sq[r, i // 2, P:SEQ], False, True, skip_group_check=True) \
                        .then_inc(sem("sb_z"), 1)
                    pe.wait_ge(sem("out_evac"), i + 10)
                    by_feature(U_G[i], xh, xl, (i + 11) % 2)
                    pe.wait_ge(sem("sb_lf"), i + 1)
                    mm(PS[:, b * 512:b * 512 + 384], C("tri"), st2[i % 2][:], False, False, skip_group_check=True)
                    mm(PS[:, b * 512 + P:b * 512 + SEQ], C("ones"), st2[i % 2][:, SEQ:384], False, True,
                       skip_group_check=True).then_inc(sem("sb_arg"), 1)
                if i >= 1:
                    h = i - 1
                    o = PS[HD * (h % 2):HD * (h % 2) + HD, (6 + h // 4) * 512 + (h // 2 % 2) * SEQ:
                           (6 + h // 4) * 512 + (h // 2 % 2) * SEQ + SEQ]
                    pe.wait_ge(sem("sb_w"), h + 1)
                    if h == 0:
                        pe.wait_ge(sem("sv_ready"), 2)
                    mm(o, sv[:, 0, h * HD:(h + 1) * HD], st4[h % 2][:, 0:SEQ], True, False, skip_group_check=True)
                    mm(o[:, P:SEQ], sv[:, 1, h * HD:(h + 1) * HD], st4[h % 2][:, SEQ:384], False, True,
                       skip_group_check=True).then_inc(sem("sb_o"), 1)

            pe.wait_ge(sem("rw_pre"), 1)
            for tt in range(NT):
                ts = slice(tt * P, (tt + 1) * P)
                if tt == 0:
                    pe.wait_ge(sem("sb_evac"), 4)
                else:
                    pe.wait_ge(sem("y_evac"), tt)
                    pe.wait_ge(sem("state"), 2 * tt + 1)
                for q, src in enumerate((eX, kk, eN, rw)):
                    for j in range(NPAIR):
                        s = src[:, 8 + j, ts] if q == 3 else src[:, j, ts]
                        last = nc.tensor.transpose(PS[:, (4 + q) * 512 + j * P:(4 + q) * 512 + (j + 1) * P], s, C("ident"))
                    last.then_inc(sem("tok_T"), 1)
                for q, (l, r) in enumerate(((kk, eX), (eN, eX), (kk, eP), (eN, eP))):
                    for g in range(2):
                        b = (2 * q + g) % 8
                        if q == 0 and g == 0:
                            pe.wait_ge(sem("out_evac"), 19)
                        if b >= 4:
                            pe.wait_ge(sem("tok_evac"), 4 * tt + b - 3)
                        p = slice(HD * g, HD * g + HD)
                        for e in range(4):
                            h = 2 * e + g
                            last = mm(PS[:, b * 512 + e * P:b * 512 + (e + 1) * P], l[p, h // 2, ts], r[p, h // 2, ts], True, True)
                        last.then_inc(sem("pair_mm"), 1)
                for g in range(2):
                    pe.wait_ge(sem("xm"), 12 * tt + g + 1)
                    pe.wait_ge(sem("pair_evac"), 8 * tt + 2)
                    for e in range(4):
                        last = nc.tensor.transpose(PS[:, g * 512 + e * P:g * 512 + (e + 1) * P], Xm[:, 4 * g + e, :], C("ident"))
                    last.then_inc(sem("inv_T1"), 1)
                for v in range(1, 6):
                    for g in range(2):
                        pe.wait_ge(sem("xm"), 12 * tt + 2 * v + g + 1)
                        pe.wait_ge(sem("inv_t"), 10 * tt + 2 * (v - 1) + g + 1)
                        if v == 1:
                            pe.wait_ge(sem("pair_evac"), 8 * tt + 8)
                        for e in range(4):
                            h = 4 * g + e
                            last = mm(PS[:, g * 512 + e * P:g * 512 + (e + 1) * P], Xm[:, h, :], Tm[:, h, :], True, True)
                        last.then_inc(sem("inv_g"), 1)
                    for g in range(2):
                        pe.wait_ge(sem("inv_g_evac"), 10 * tt + 2 * (v - 1) + g + 1)
                        pe.wait_ge(sem("inv_tt"), 12 * tt + 2 * (v - 1) + g + 1)
                        if v < 5:
                            for e in range(4):
                                h = 4 * g + e
                                mm(PS[:, (2 + g) * 512 + e * P:(2 + g) * 512 + (e + 1) * P], TT[:, h, :], Gm[:, h, :], True, True)
                        for e in range(4):
                            h = 4 * g + e
                            last = mm(PS[:, (4 + g) * 512 + e * P:(4 + g) * 512 + (e + 1) * P], Gm[:, h, :], TT[:, h, :], True, True)
                        last.then_inc(sem("inv_up"), 1)
                for h in range(NH):
                    o = PS[:, 7 * 512 + h * HD:7 * 512 + (h + 1) * HD]
                    last = mm(o, AK[:, slot(h), :], vt_[:, h * HD:(h + 1) * HD], True, True)
                last.then_inc(sem("av_mm"), 1)
                pe.wait_ge(sem("inv_tt"), 12 * tt + 12)
                for h in range(NH):
                    p = slice(HD * (h % 2), HD * (h % 2) + HD)
                    last = mm(PS[p, 6 * 512 + (h // 2) * P:6 * 512 + (h // 2 + 1) * P], at_[:, h * HD:(h + 1) * HD], TT[:, slot(h), :],
                              True, True, skip_group_check=True)
                last.then_inc(sem("wt_mm"), 1)
                pe.wait_ge(sem("av_evac"), tt + 1)
                for h in range(NH):
                    last = mm(PS[:, h * HD:(h + 1) * HD], TT[:, slot(h), :], AV[:, h * HD:(h + 1) * HD], True, True)
                last.then_inc(sem("u0_mm"), 1)
                pe.wait_ge(sem("wt_evac"), tt + 1)
                for c in range(2):
                    g = 2 * tt + c
                    rs_ = slice(CHUNK * c, CHUNK * c + CHUNK)
                    pe.wait_ge(sem("state"), g + 1)
                    for j in range(NPAIR):
                        last = mm(PS[rs_, 512 + j * P:512 + (j + 1) * P], WT[:, j, rs_], St[:, g, j, :], True, True,
                                  skip_group_check=True)
                    last.then_inc(sem("u_mm"), 1)
                    pe.wait_ge(sem("u_ready"), g + 1)
                    if g < 3:
                        for j in range(NPAIR):
                            o = PS[:, 2 * 512 + j * P:2 * 512 + (j + 1) * P]
                            js = slice(j * P, (j + 1) * P)
                            mm(o, bt_[rs_, js], Uc[rs_, js], True, False)
                            last = mm(o, kt_[rs_, js], vt_[rs_, js], False, True)
                        last.then_inc(sem("ds_mm"), 1)
                for j in range(NPAIR):
                    b0 = 3 * 512 + j * P
                    mm(PS[:, b0:b0 + CHUNK], St[:, 2 * tt, j, :], eP[:, j, tt * P:tt * P + CHUNK], True, False,
                       skip_group_check=True)
                    mm(PS[:, b0 + CHUNK:b0 + P], St[:, 2 * tt + 1, j, :], eP[:, j, tt * P + CHUNK:(tt + 1) * P], False, False,
                       skip_group_check=True)
                    for e in range(2):
                        h = 2 * j + e
                        o = PS[HD * e:HD * e + HD, b0:b0 + P]
                        mm(o, Uc[:, h * HD:(h + 1) * HD], RB[:, slot(h), :], False, False, skip_group_check=True)
                        last = mm(o, vt_[:, h * HD:(h + 1) * HD], RK[:, slot(h), :], False, True, skip_group_check=True)
                last.then_inc(sem("y_mm"), 1)

            pe.wait_ge(sem("y_evac"), 2)
            for j in range(NPAIR):
                last = mm(PS[:, 4 * 512 + j * SEQ:4 * 512 + (j + 1) * SEQ], C("blockones"), yT[:, j, :], True, True)
            last.then_inc(sem("y_sum"), 1)
            by_feature(U_SO[0], sboh, sbol, 0)
            pe.wait_ge(sem("y_sq"), 1)
            for j in range(NPAIR):
                last = mm(PS[:, 6 * 512 + j * SEQ:6 * 512 + (j + 1) * SEQ], C("blockones"), yq[:, j, :], True, True)
            last.then_inc(sem("y_ss"), 1)
            by_feature(U_SO[1], sboh, sbol, 2)
            pe.wait_ge(sem("rkk"), 1)
            for j in range(NPAIR):
                last = mm(PS[:, 4 * 512 + j * SEQ:4 * 512 + (j + 1) * SEQ], C("blockones"), bon[:, j, :], True, True)
            last.then_inc(sem("bonus_mm"), 1)
            pe.wait_ge(sem("y_sd"), 1)
            for j in range(NPAIR):
                last = mm(PS[:, 6 * 512 + j * SEQ:6 * 512 + (j + 1) * SEQ], gup[:, j * P:(j + 1) * P], rw[:, 13, :], True, True)
            last.then_inc(sem("g_mm"), 1)
            pe.wait_ge(sem("rwo"), 4)
            for i in range(2):
                pe.wait_ge(sem("merge_a"), i + 1)
                by_feature(U_RO[i], rwoh, rwol, 2 * i)
            for i, u in enumerate(U_O):
                pe.wait_ge(sem("merged"), 2 * i + 2)
                by_token(u, mh, ml, 2 * i, 4, i == 0, i == 3)

            transpose_in("n2", xn, KD, 0)
            pe.wait_ge(norm_sem("n2", "xT"), nth("n2", "xT", KD))
            for i in range(FF_CHUNKS + 1):
                if i < FF_CHUNKS:
                    if i >= 2:
                        pe.wait_ge(sem("ff_out"), i - 1)
                    by_feature(U_F["g", i], xh, xl, 2 * (i % 2))
                    by_feature(U_F["u", i], xh, xl, 2 * (i % 2) + 1)
                if i:
                    pe.wait_ge(sem("ff_h"), i)
                    by_token(U_F["d", i - 1], fh[(i - 1) % 2], fl[(i - 1) % 2], 0, 4, i == 1, i == FF_CHUNKS)

            transpose_in("n3", xn, KD, 0)
            pe.wait_ge(norm_sem("n3", "xT"), nth("n3", "xT", KD))
            for i, u in enumerate(U_QK2):
                if i >= 2:
                    pe.wait_ge(sem("out2_evac"), i - 1)
                by_feature(u, xh, xl, i % 2)
            for i, u in enumerate(U_V2):
                by_token(u, xh, xl, 4 * i, 2, i == 0, i == 1)
            transpose_in("mem", mem, KD, 4)
            pe.wait_ge(norm_sem("mem", "xT"), nth("mem", "xT", KD))
            for i in range(NH + 2):
                if i < NH:
                    r = slice(HD * (i % 2), HD * (i % 2) + HD)
                    b = (4 + i % 2) * 512
                    if i == 0:
                        pe.wait_ge(sem("out2_evac"), 4)
                    if i >= 2:
                        pe.wait_ge(sem("d_z_read"), i - 1)
                    mm(PS[:, b:b + P], q2[r, i // 2, 0:P], k2[r, i // 2, 0:P], True, True)
                    mm(PS[:, b + P:b + 384], q2[r, i // 2, P:SEQ], k2[r, i // 2, :], True, True).then_inc(sem("d_z"), 1)
                pe.wait_ge(sem("out2_evac"), i + 3)
                if i < 6:
                    by_feature(FILL2[i], xh, xl, i % 2)
                else:
                    by_feature(FILL2[i], memh, meml, i % 2)
                if 1 <= i <= NH:
                    h = i - 1
                    pe.wait_ge(sem("d_p"), 2 * h + 2)
                    if h < 2:
                        pe.wait_ge(sem("v2_ready"), 2)
                    else:
                        pe.wait_ge(sem("d_q"), h - 1)
                    for c in range(3):
                        b = (2 + h % 2) * 512 + c * P
                        last = nc.tensor.transpose(PS[:, b:b + P], dp[h % 2][:, c * P:(c + 1) * P], C("ident"))
                    last.then_inc(sem("d_T"), 1)
                if i >= 2:
                    h = i - 2
                    pe.wait_ge(sem("d_q"), h + 1)
                    hs = slice(h * HD, (h + 1) * HD)
                    mm(bank(6)[:, hs], dq[h % 2][:, 0:P], v2[:, 0, hs], True, True)
                    mm(bank(7)[:, hs], dq[h % 2][:, P:SEQ], v2[:, 0, hs], True, False)
                    mm(bank(7)[:, hs], dq[h % 2][:, SEQ:384], v2[:, 1, hs], False, True).then_inc(sem("d_o"), 1)
            for i, u in enumerate(U_VM):
                by_token(u, memh, meml, 2 * i, 2, i == 0, i == 3)
                if i == 1:
                    pe.wait_ge(sem("c_sq"), 1)
                    pe.wait_ge(sem("out2_evac"), 14)
                    for j in range(NPAIR):
                        last = mm(PS[:, 0:SEQ], C("ones"), cv[:, 1, j, :], j == 0, j == NPAIR - 1)
                    last.then_inc(sem("c_ss"), 1)
                if i == 2:
                    transpose_in("att", att, NPAIR, 6)
            for i, u in enumerate(U_O2):
                if i < 2:
                    pe.wait_ge(norm_sem("att", "xT"), nth("att", "xT", NPAIR))
                else:
                    pe.wait_ge(sem("conv_xT"), NPAIR)
                if i == 0:
                    pe.wait_ge(sem("vm_ready"), 4)
                    pe.wait_ge(sem("c_sd"), 1)
                by_token(u, m2h, m2l, 2 * i, 0, i == 0, i == 3)

            transpose_in("n4", xn, KD, 4)
            pe.wait_ge(norm_sem("n4", "xT"), nth("n4", "xT", KD))
            for i, u in enumerate(U_QM):
                if i >= 2:
                    pe.wait_ge(sem("qm_evac"), i - 1)
                by_feature(u, xh, xl, i % 2)
            for i in range(MEM_HEADS + 2):
                if i < MEM_HEADS:
                    pe.wait_ge(sem("qm_evac"), min(i + 1, 4))
                    if i >= 2:
                        pe.wait_ge(sem("m_exp"), 2 * (i - 1))
                    for t in range(NT):
                        for e in range(2):
                            last = mm(PS[:, (2 + i % 2) * 512 + t * SEQ:(2 + i % 2) * 512 + (t + 1) * SEQ],
                                      qm[:, 2 * i + e, t * P:(t + 1) * P], km[:, 2 * i + e, :], e == 0, e == 1)
                    last.then_inc(sem("m_z"), 1)
                if 1 <= i <= MEM_HEADS:
                    h = i - 1
                    pe.wait_ge(sem("m_p"), h + 1)
                    if h >= 2:
                        pe.wait_ge(sem("m_q"), h - 1)
                    for mt in range(NT):
                        for t in range(NT):
                            b = (4 + h % 2) * 512 + mt * SEQ + t * P
                            last = nc.tensor.transpose(PS[:, b:b + P], mp[h % 2][:, t, mt * P:(mt + 1) * P], C("ident"))
                    last.then_inc(sem("m_T"), 1)
                if i >= 2:
                    h = i - 2
                    pe.wait_ge(sem("m_q"), h + 1)
                    if h >= 2:
                        pe.wait_ge(sem("om"), 2 * (h - 1))
                    for e in range(2):
                        for mt in range(NT):
                            last = mm(PS[:, (6 + h % 2) * 512 + e * SEQ:(6 + h % 2) * 512 + (e + 1) * SEQ],
                                      vm[:, mt, (2 * h + e) * P:(2 * h + e + 1) * P], mq[h % 2][:, mt, :], mt == 0, mt == 1)
                    last.then_inc(sem("m_o"), 1)
            for i, u in enumerate(U_OM):
                pe.wait_ge(sem("om"), 2 * (i + 1))
                by_token(u, omh, oml, 2 * i, 0, i == 0, i == 3)

            transpose_in("n5", xn, KD, 4)
            pe.wait_ge(norm_sem("n5", "xT"), nth("n5", "xT", KD))
            for i in range(FF2_CHUNKS + 1):
                if i < FF2_CHUNKS:
                    if i >= 4:
                        pe.wait_ge(sem("mlp_out"), i - 3)
                    by_feature(U_M["u", i], xh, xl, i % 4)
                if i:
                    pe.wait_ge(sem("mlp_h"), i)
                    by_token(U_M["d", i - 1], fh[(i - 1) % 2], fl[(i - 1) % 2], 0, 4, i == 1, i == FF2_CHUNKS)

        @block.scalar
        def _(act):
            chain = [0]

            def A_(o, i, f, **kw):
                return nc.scalar.activation(o, i, f, **kw)

            def link(ins):
                chain[0] += 1
                ins.then_inc(sem("act_chain"), 1)
                act.wait_ge(sem("act_chain"), chain[0])

            def hi(u):
                if u >= NU:
                    return
                act.wait_ge(raw_loaded[u % RING], 16 * (u // RING + 1))
                if u >= RING:
                    act.wait_ge(sem("units_used"), u - RING + 1)
                A_(whi[u % RING][:], raw[u % RING][:], ACT.Copy).then_inc(sem("hi_done"), 1)

            def after(u):
                hi(u + RING)
                act.wait_ge(sem("units_used"), u + 1)

            def deviation(st, src, ready, width=D):
                c = NORM[st]
                for t in range(NT):
                    ready(t)
                    if t:
                        act.wait_ge(norm_sem(st, "sq"), nth(st, "sq", t))
                    A_(junk[:, 0:width], src(t), ACT.Square, accum_out=col(c + t)).then_inc(norm_sem(st, "sq"), 1)
                act.wait_ge(norm_sem(st, "sq"), nth(st, "sq", NT))
                A_(col(c + 2, 2), col(c, 2), ACT.Sqrt, scale=1.0 / width, bias=col(EPS)).then_inc(norm_sem(st, "sd"), 1)

            def round_T(st, g, dst, f0, nf, b):
                for f in range(nf):
                    act.wait_ge(norm_sem(st, "T"), nth(st, "T", f // 2 * 2 + 2))
                    A_(dst[:, f0 + f, :], PS[:, b * 512 + f * SEQ:b * 512 + (f + 1) * SEQ], ACT.Copy, scale=par_col(g, f)) \
                        .then_inc(norm_sem(st, "hi"), 1)

            act.dma_start(par[:], A["params"]).then_inc(sem("par_loaded"), 16)
            act.dma_start(cst[:], A["consts"]).then_inc(sem("cst_loaded"), 16)
            act.dma_start(lora[0:HD, :], A["w_up"][0]).then_inc(sem("lora_loaded"), 16)
            act.dma_start(lora[HD:P, :], A["a_up"][0]).then_inc(sem("lora_loaded"), 16)
            act.dma_start(gup[:], A["g_up"][0]).then_inc(sem("lora_loaded"), 16)
            act.wait_ge(sem("x_loaded"), 16)
            act.wait_ge(sem("eps_set"), 1)
            deviation("n1", lambda t: xres[:, t, :], lambda t: None)
            for u in range(RING):
                hi(u)
            act.wait_ge(sem("par_loaded"), 16)
            round_T("n1", "norm_mix_pre", xh, 0, KD, 4)
            for i, u in enumerate(U_RW):
                after(u)
                if i >= 2:
                    act.wait_ge(sem("mixed"), i - 1)
                else:
                    act.wait_ge(sem("stg_zero"), 1)
                A_(stg[i % 2][:, :, 1:SEQ + 1], bank(i % 2).rearrange("p (f t) -> p f t", f=2), ACT.Copy) \
                    .then_inc(sem("out_evac"), 1)
                if i == 1:
                    act.wait_ge(sem("mixed"), 1)
                    A_(rw[0:HD, 12, :], rw[0:HD, 12, :], ACT.Tanh)
                    A_(rw[:, 13, :], rw[:, 13, :], ACT.Sigmoid).then_inc(sem("lora_in"), 1)
                if i == 2:
                    act.wait_ge(sem("lora_out"), 1)
                    for j in range(NPAIR):
                        A_(sg[:, j, :], PS[:, 4 * 512 + j * SEQ:4 * 512 + (j + 1) * SEQ], ACT.Sigmoid, bias=par_col("w0", j))
                    for j in range(NPAIR):
                        last = A_(ag[:, j, :], PS[:, 6 * 512 + j * SEQ:6 * 512 + (j + 1) * SEQ], ACT.Sigmoid, bias=par_col("a0", j))
                    last.then_inc(sem("lora_evac"), 1)
                if i == 5:
                    act.wait_ge(sem("kk_ss"), 1)
                    A_(kq[:].rearrange("p j t -> p (j t)"), PS[:, 4 * 512:6 * 512], ACT.Sqrt).then_inc(sem("kk_sd"), 1)
            nc.scalar.preload_act_table_set("natural_log_exp_and_others")
            act.wait_ge(sem("cs"), 1)
            act.wait_ge(sem("k_mod"), 1)
            c0 = float(np.exp(-0.5))
            A_(eP[:], cs[:], ACT.Exp, scale=-c0)
            A_(eN[:], cs[:], ACT.Exp, scale=c0)
            A_(eX[:], sg[:], ACT.Exp, scale=-c0).then_inc(sem("decays"), 1)
            for i, u in enumerate(U_QK):
                after(u)
                dst = (sq, sk)[i // 2]
                A_(dst[:, 2 * (i % 2):2 * (i % 2) + 2, :], bank((i + 7) % 2).rearrange("p (f t) -> p f t", f=2), ACT.Copy,
                   scale=HD ** -0.5 if i < 2 else 1.0).then_inc(sem("out_evac"), 1)
            hi(U_V[0] + RING)
            after(U_V[1])
            for t in range(NT):
                A_(sv[:, t, :], bank(2 + t), ACT.Copy).then_inc(sem("sv_ready"), 1)
            for i in range(NH):
                b = (4 + i % 2) * 512
                s1, s2, s3, s4 = st1[i % 2], st2[i % 2], st3[i % 2], st4[i % 2]
                act.wait_ge(sem("sb_z"), i + 1)
                if i >= 2:
                    act.wait_ge(sem("sb_lf"), i - 1)
                link(A_(s1[:], PS[:, b:b + 384], ACT.Abs))
                link(A_(s1[:], s1[:], ACT.Exp, scale=-1.0))
                A_(s1[:], s1[:], ACT.Ln, bias=1.0).then_inc(sem("sb_ln"), 1)
                after(U_G[i])
                for f in range(2):
                    last = A_(gates[:, 2 * i + f, :], PS[:, ((i + 11) % 2) * 512 + f * SEQ:((i + 11) % 2) * 512 + (f + 1) * SEQ],
                              ACT.Identity, bias=par_col("b_gate", 2 * i + f))
                last.then_inc(sem("out_evac"), 1)
                act.wait_ge(sem("sb_arg_read"), i + 1)
                if i >= 2:
                    act.wait_ge(sem("sb_o"), i - 1)
                A_(s4[:], s3[:], ACT.Exp).then_inc(sem("sb_w"), 1)
            act.wait_ge(sem("sb_o"), NH)
            for j in range(2):
                A_(sboh[:, 2 * j:2 * j + 2, :], bank(6 + j).rearrange("p (f t) -> p f t", f=2), ACT.Copy).then_inc(sem("sbo_hi"), 1)
            act.wait_ge(sem("out_evac"), 19)
            A_(gates[:], gates[:], ACT.Sigmoid).then_inc(sem("gates_ready"), 1)
            for tt in range(NT):
                for q, dst in enumerate((at_, bt_, kt_, vt_)):
                    act.wait_ge(sem("tok_T"), 4 * tt + q + 1)
                    if q == 0 and tt == 0:
                        act.wait_ge(sem("units_used"), U_G[7] + 1)
                    A_(dst[:], bank(4 + q), ACT.Copy).then_inc(sem("tok_evac"), 1)
                for v in range(1, 6):
                    for g in range(2):
                        act.wait_ge(sem("inv_g"), 10 * tt + 2 * (v - 1) + g + 1)
                        A_(Gm[:, 4 * g:4 * g + 4, :], bank(g).rearrange("p (e t) -> p e t", e=4), ACT.Copy) \
                            .then_inc(sem("inv_g_evac"), 1)
                act.wait_ge(sem("av_mm"), tt + 1)
                A_(AV[:], bank(7), ACT.Copy).then_inc(sem("av_evac"), 1)
                act.wait_ge(sem("wt_mm"), tt + 1)
                A_(WT[:].rearrange("p j t -> p (j t)"), bank(6), ACT.Copy).then_inc(sem("wt_evac"), 1)
                act.wait_ge(sem("u0_mm"), tt + 1)
                A_(U0[:], bank(0), ACT.Copy).then_inc(sem("u0_evac"), 1)
                act.wait_ge(sem("y_mm"), tt + 1)
                A_(yT[:, :, tt * P:(tt + 1) * P], bank(3).rearrange("p (j t) -> p j t", j=NPAIR), ACT.Copy) \
                    .then_inc(sem("y_evac"), 1)
            act.wait_ge(sem("yc_ready"), 2)
            A_(yq[:], yc[:], ACT.Square).then_inc(sem("y_sq"), 1)
            hi(U_SO[0] + RING)
            act.wait_ge(sem("y_ss"), 1)
            A_(yq[:].rearrange("p j t -> p (j t)"), PS[:, 6 * 512:8 * 512], ACT.Sqrt, scale=1.0 / HD, bias=col(GEPS)) \
                .then_inc(sem("y_sd"), 1)
            hi(U_SO[1] + RING)
            for j in range(NPAIR):
                act.wait_ge(sem("orw"), j + 1)
                A_(rwoh[:, j, :], orw[:, j, :], ACT.Copy).then_inc(sem("rwo_hi"), 1)
            for i, u in enumerate(U_RO):
                hi(u + RING)
            for f in range(KD):
                act.wait_ge(sem("merge_sum"), f + 1)
                A_(mh[:, f, :], gates[:, f, :], ACT.Copy).then_inc(sem("merged_hi"), 1)
            for u in U_O:
                hi(u + RING)

            def post(st, u, b):
                act.wait_ge(sem("units_used"), u + 1)
                deviation(st, lambda t: PS[:, b * 512 + t * D:b * 512 + (t + 1) * D], lambda t: None)

            def pre(st, g, b):
                deviation(st, lambda t: xres[:, t, :], lambda t: act.wait_ge(norm_sem(st, "x"), nth(st, "x", t + 1)))
                round_T(st, g, xh, 0, KD, b)

            post("p1", U_O[3], 4)
            pre("n2", "norm_ffn_pre", 0)
            for i in range(FF_CHUNKS):
                hi(U_F["g", i] + RING)
                after(U_F["u", i])
                if i >= 2:
                    act.wait_ge(sem("ff_out"), i - 1)
                A_(fa[i % 2][:], bank(2 * (i % 2)), ACT.Silu).then_inc(sem("ff_silu"), 1)
                if i:
                    hi(U_F["d", i - 1] + RING)
                act.wait_ge(sem("ff_out"), i + 1)
                if i >= 2:
                    act.wait_ge(sem("units_used"), U_F["d", i - 2] + 1)
                A_(fh[i % 2][:].rearrange("p f t -> p (f t)"), fb[i % 2][:], ACT.Copy).then_inc(sem("ff_hi"), 1)
            hi(U_F["d", FF_CHUNKS - 1] + RING)
            post("p2", U_F["d", FF_CHUNKS - 1], 4)
            pre("n3", "g_mix_2", 0)
            act.wait_ge(sem("mem_loaded"), 16)
            deviation("mem", lambda t: mem[:, t, :], lambda t: None)
            for i, u in enumerate(U_QK2):
                after(u)
                dst = (q2, k2)[i // 2]
                A_(dst[:, 2 * (i % 2):2 * (i % 2) + 2, :], bank(i % 2).rearrange("p (f t) -> p f t", f=2), ACT.Copy) \
                    .then_inc(sem("out2_evac"), 1)
            hi(U_V2[0] + RING)
            after(U_V2[1])
            for t in range(NT):
                A_(v2[:, t, :], bank(2 + t), ACT.Copy).then_inc(sem("v2_ready"), 1)
            round_T("mem", "g_mem_2", memh, 0, KD, 4)
            for i in range(NH + 2):
                if i < NH:
                    if i >= 2:
                        act.wait_ge(sem("d_T"), i - 1)
                    act.wait_ge(sem("d_max"), i + 1)
                    A_(dp[i % 2][:, 0:P], dz[i % 2][:, 0:P], ACT.Exp, bias=col(DMX + i), accum_out=col(DL + i)) \
                        .then_inc(sem("d_p"), 1)
                    A_(dp[i % 2][:, P:384], dz[i % 2][:, P:384], ACT.Exp, bias=col(DMX + NH + i), accum_out=col(DL + NH + i)) \
                        .then_inc(sem("d_p"), 1)
                u = FILL2[i]
                after(u)
                dst = cv[:, i // 2, 2 * (i % 2):2 * (i % 2) + 2, :] if i < 6 else km[:, 2 * (i - 6):2 * (i - 6) + 2, :]
                A_(dst, bank(i % 2).rearrange("p (f t) -> p f t", f=2), ACT.Copy).then_inc(sem("out2_evac"), 1)
                if 1 <= i <= NH:
                    h = i - 1
                    act.wait_ge(sem("d_T"), h + 1)
                    if h >= 2:
                        act.wait_ge(sem("d_o"), h - 1)
                    A_(dq[h % 2][:], PS[:, (2 + h % 2) * 512:(2 + h % 2) * 512 + 384], ACT.Copy).then_inc(sem("d_q"), 1)
            act.wait_ge(sem("c_gated"), 1)
            A_(cv[:, 1], cv[:, 0], ACT.Square).then_inc(sem("c_sq"), 1)
            deviation("att", lambda t: att[:, t, :], lambda t: act.wait_ge(sem("att_raw"), t + 1), HW)
            for i in range(2):
                hi(U_VM[i] + RING)
            act.wait_ge(sem("c_ss"), 1)
            A_(crs[:], PS[:, 0:SEQ], ACT.Sqrt, scale=1.0 / HW, bias=col(EPS)).then_inc(sem("c_sd"), 1)
            hi(U_VM[2] + RING)
            for j in range(NPAIR):
                act.wait_ge(sem("conv_n"), j + 1)
                A_(m2h[:, 4 + j, :], cv[:, 0, j, :], ACT.Copy).then_inc(sem("conv_hi"), 1)
            round_T("att", "g_attn_out_2", m2h, 0, NPAIR, 6)
            after(U_VM[3])
            for t in range(NT):
                for c in range(2):
                    A_(vm[:, t, c * 512:(c + 1) * 512], bank(2 + 2 * t + c), ACT.Copy).then_inc(sem("vm_ready"), 1)
            for u in U_O2:
                hi(u + RING)
            pre("n4", "g_xattn_2", 4)
            for i, u in enumerate(U_QM):
                after(u)
                A_(qm[:, 2 * i:2 * i + 2, :], bank(i % 2).rearrange("p (f t) -> p f t", f=2), ACT.Copy).then_inc(sem("qm_evac"), 1)
            for i in range(MEM_HEADS + 2):
                if i < MEM_HEADS:
                    act.wait_ge(sem("m_max"), i + 1)
                    if i >= 2:
                        act.wait_ge(sem("m_T"), i - 1)
                    for t in range(NT):
                        A_(mp[i % 2][:, t, :], PS[:, (2 + i % 2) * 512 + t * SEQ:(2 + i % 2) * 512 + (t + 1) * SEQ], ACT.Exp,
                           bias=col(MMX + 2 * i + t), scale=256 ** -0.5, accum_out=col(MSUM + 2 * i + t)) \
                            .then_inc(sem("m_exp"), 1)
                if 1 <= i <= MEM_HEADS:
                    h = i - 1
                    act.wait_ge(sem("m_T"), h + 1)
                    if h >= 2:
                        act.wait_ge(sem("m_o"), h - 1)
                    A_(mq[h % 2][:].rearrange("p m t -> p (m t)"), bank(4 + h % 2), ACT.Copy).then_inc(sem("m_q"), 1)
                if i >= 2:
                    h = i - 2
                    act.wait_ge(sem("m_o"), h + 1)
                    A_(omh[:, 2 * h:2 * h + 2, :], bank(6 + h % 2).rearrange("p (e t) -> p e t", e=2), ACT.Copy) \
                        .then_inc(sem("om_hi"), 1)
            for u in U_OM:
                hi(u + RING)
            pre("n5", "g_mlp_2", 4)
            for i in range(FF2_CHUNKS):
                after(U_M["u", i])
                if i >= 2:
                    act.wait_ge(sem("mlp_sq"), i - 1)
                A_(fa[i % 2][:], bank(i % 4), ACT.Relu).then_inc(sem("mlp_out"), 1)
                if i:
                    hi(U_M["d", i - 1] + RING)
                act.wait_ge(sem("mlp_sq"), i + 1)
                if i >= 2:
                    act.wait_ge(sem("units_used"), U_M["d", i - 2] + 1)
                A_(fh[i % 2][:].rearrange("p f t -> p (f t)"), fb[i % 2][:], ACT.Copy).then_inc(sem("mlp_hi"), 1)
            deviation("fin", lambda t: xres[:, t, :], lambda t: act.wait_ge(norm_sem("fin", "x"), nth("fin", "x", t + 1)))

        @block.vector
        def _(dve):
            V = nc.vector
            chain = [0]

            def link(ins):
                chain[0] += 1
                ins.then_inc(sem("dve_chain"), 1)
                dve.wait_ge(sem("dve_chain"), chain[0])

            def lo(u):
                if u >= NU:
                    return
                dve.wait_ge(sem("hi_done"), u + 1)
                V.tensor_tensor(wlo[u % RING][:], raw[u % RING][:], whi[u % RING][:].bitcast(f32), ALU.subtract) \
                    .then_inc(sem("unit_split"), 1)

            def normalise(st, src, dst, width=D):
                c = NORM[st]
                dve.wait_ge(norm_sem(st, "sd"), nth(st, "sd", 1))
                link(V.reciprocal(col(c + 4, 2), col(c + 2, 2)))
                for t in range(NT):
                    V.tensor_scalar(dst[:, t, :], src[:, t, :], col(c + 4 + t), None, ALU.mult).then_inc(norm_sem(st, "xn"), 1)

            def rest_T(st, g, hi_, lo_, f0, nf, b):
                for f in range(nf):
                    dve.wait_ge(norm_sem(st, "hi"), nth(st, "hi", f // 2 * 2 + 2))
                    V.scalar_tensor_tensor(out=lo_[:, f0 + f, :], in0=PS[:, b * 512 + f * SEQ:b * 512 + (f + 1) * SEQ],
                                           scalar=par_col(g, f), in1=hi_[:, f0 + f, :].bitcast(f32),
                                           op0=ALU.mult, op1=ALU.subtract).then_inc(norm_sem(st, "xT"), 1)

            V.memset(col(EPS), 1e-6)
            V.memset(col(GEPS), HD * 1e-5).then_inc(sem("eps_set"), 1)
            dve.wait_ge(sem("x_loaded"), 16)
            normalise("n1", xres, xn)
            for u in range(RING):
                lo(u)
            dve.wait_ge(sem("par_loaded"), 16)
            rest_T("n1", "norm_mix_pre", xh, xl, 0, KD, 4)
            for i in range(2):
                last = V.memset(stg[i][:, :, 0:1], 0.0)
            last.then_inc(sem("stg_zero"), 1)
            for i, u in enumerate(U_RW):
                lo(u + RING)
                dve.wait_ge(sem("out_evac"), i + 1)
                s = stg[i % 2]
                if i:
                    dve.wait_ge(sem("mixed"), i)
                link(V.tensor_tensor(diff[:], s[:, :, 0:SEQ], s[:, :, 1:SEQ + 1], ALU.subtract))
                for f in range(2):
                    r = RW_TILE[i] + f
                    last = V.scalar_tensor_tensor(out=rw[:, r, :], in0=diff[:, f, :], scalar=par_col("mu_rw", r),
                                                  in1=s[:, f, 1:SEQ + 1], op0=ALU.mult, op1=ALU.add)
                last.then_inc(sem("mixed"), 1)
                if i == 2:
                    dve.wait_ge(sem("mixed"), 3)
                    for j in range(NPAIR):
                        last = V.tensor_scalar(kk[:, j, :], rw[:, 4 + j, :], par_col("k_k", j), None, ALU.mult)
                    link(last)
                    V.tensor_tensor(kq[:], kk[:], kk[:], ALU.mult).then_inc(sem("kk_sq"), 1)
                if i == 3:
                    dve.wait_ge(sem("lora_evac"), 1)
                    dve.wait_ge(sem("cst_loaded"), 16)
                    for j in range(NPAIR):
                        last = V.tensor_tensor_scan(cs[:, j, :], C("reset"), sg[:, j, :], 0.0, ALU.mult, ALU.add)
                    link(last)
                    V.tensor_tensor(sg[:], cs[:], sg[:], ALU.subtract).then_inc(sem("cs"), 1)
                if i == 4:
                    for j in range(NPAIR):
                        link(V.tensor_scalar(eP[:, j, :], ag[:, j, :], 1.0, par_col("k_a", j), ALU.subtract, ALU.mult))
                        last = V.scalar_tensor_tensor(out=rw[:, 4 + j, :], in0=eP[:, j, :], scalar=1.0, in1=rw[:, 4 + j, :],
                                                      op0=ALU.add, op1=ALU.mult)
                    last.then_inc(sem("k_mod"), 1)
            dve.wait_ge(sem("kk_sd"), 1)
            lo(U_QK[0] + RING)
            link(V.tensor_scalar(kq[:], kq[:], 1e-12, None, ALU.max))
            link(V.reciprocal(kq[:], kq[:]))
            link(V.tensor_tensor(kk[:], kk[:], kq[:], ALU.mult))
            lo(U_QK[1] + RING)
            dve.wait_ge(sem("decays"), 1)
            V.tensor_copy(dec[:], eP[:].rearrange("p j (g c) -> p j g c", c=CHUNK)[:, :, :, CHUNK - 1])
            link(V.scalar_tensor_tensor(out=eX[:].rearrange("p j t -> p (j t)"), in0=kk[:].rearrange("p j t -> p (j t)"), scalar=-1.0,
                                        in1=eX[:].rearrange("p j t -> p (j t)"), op0=ALU.mult, op1=ALU.mult))
            link(V.tensor_tensor(kk[:], kk[:], ag[:], ALU.mult))
            lo(U_QK[2] + RING)
            link(V.tensor_tensor(kk[:], kk[:], eN[:], ALU.mult))
            dve.wait_ge(sem("mixed"), 7)
            V.tensor_tensor(eN[:], rw[:, 4:8, :], eN[:], ALU.mult)
            V.tensor_tensor(eP[:], rw[:, 0:4, :], eP[:], ALU.mult).then_inc(sem("rw_pre"), 1)
            lo(U_QK[3] + RING)
            for u in U_V:
                lo(u + RING)
            for i in range(NH):
                b = (4 + i % 2) * 512
                s1, s2, s3 = st1[i % 2], st2[i % 2], st3[i % 2]
                dve.wait_ge(sem("sb_ln"), i + 1)
                if i >= 2:
                    dve.wait_ge(sem("sb_arg"), i - 1)
                link(V.scalar_tensor_tensor(out=s2[:], in0=PS[:, b:b + 384], scalar=0.0, in1=s1[:], op0=ALU.max, op1=ALU.add))
                V.tensor_tensor(s2[:], s2[:], C("sb_neg"), ALU.mult).then_inc(sem("sb_lf"), 1)
                lo(U_G[i] + RING)
                dve.wait_ge(sem("sb_arg"), i + 1)
                if i >= 2:
                    dve.wait_ge(sem("sb_w"), i - 1)
                V.scalar_tensor_tensor(out=s3[:], in0=PS[:, b:b + 384], scalar=0.0, in1=C("sb_add"), op0=ALU.min, op1=ALU.add) \
                    .then_inc(sem("sb_arg_read"), 1)
            for j in range(2):
                dve.wait_ge(sem("sbo_hi"), j + 1)
                V.tensor_tensor(sbol[:, 2 * j:2 * j + 2, :], bank(6 + j).rearrange("p (f t) -> p f t", f=2),
                                sboh[:, 2 * j:2 * j + 2, :].bitcast(f32), ALU.subtract).then_inc(sem("sb_evac"), 2)

            def mask4(name):
                return C(name).unsqueeze(1).broadcast_to([P, 4, P])

            V.memset(St[:, 0], 0.0).then_inc(sem("state"), 1)
            for tt in range(NT):
                for q, (dst, m) in enumerate(((XT, "strict"), (AK, "strict"), (RB, "incl"), (RK, "incl"))):
                    for g in range(2):
                        dve.wait_ge(sem("pair_mm"), 8 * tt + 2 * q + g + 1)
                        V.tensor_tensor(dst[:, 4 * g:4 * g + 4, :], bank(2 * q + g).rearrange("p (e t) -> p e t", e=4), mask4(m),
                                        ALU.mult).then_inc(sem("pair_evac"), 1)
                        if q == 0 and g == 1:
                            dve.wait_ge(sem("pair_evac"), 8 * tt + 2)
                            for gg in range(2):
                                gs = slice(4 * gg, 4 * gg + 4)
                                if tt:
                                    dve.wait_ge(sem("inv_g"), 10 * tt)
                                V.tensor_tensor(Xm[:, gs, :], XT[:, gs, :], mask4("level1"), ALU.mult).then_inc(sem("xm"), 1)
                for g in range(2):
                    gs = slice(4 * g, 4 * g + 4)
                    dve.wait_ge(sem("xm"), 12 * tt + 2)
                    V.tensor_tensor(TT[:, gs, :], Xm[:, gs, :], mask4("ident"), ALU.add).then_inc(sem("inv_tt"), 1)
                for g in range(2):
                    gs = slice(4 * g, 4 * g + 4)
                    dve.wait_ge(sem("inv_T1"), 2 * tt + g + 1)
                    V.tensor_tensor(Tm[:, gs, :], bank(g).rearrange("p (e t) -> p e t", e=4), mask4("ident"), ALU.add) \
                        .then_inc(sem("inv_t"), 1)
                for v in range(1, 6):
                    for g in range(2):
                        gs = slice(4 * g, 4 * g + 4)
                        if v == 1:
                            dve.wait_ge(sem("inv_T1"), 2 * tt + g + 1)
                            dve.wait_ge(sem("inv_tt"), 12 * tt + 2)
                        else:
                            dve.wait_ge(sem("inv_g"), 10 * tt + 2 * (v - 2) + g + 1)
                        V.tensor_tensor(Xm[:, gs, :], XT[:, gs, :], mask4(f"level{2 ** v}"), ALU.mult).then_inc(sem("xm"), 1)
                    for g in range(2):
                        gs = slice(4 * g, 4 * g + 4)
                        dve.wait_ge(sem("inv_up"), 10 * tt + 2 * (v - 1) + g + 1)
                        if v < 5:
                            V.tensor_tensor(Tm[:, gs, :], Tm[:, gs, :], bank(2 + g).rearrange("p (e t) -> p e t", e=4), ALU.add) \
                                .then_inc(sem("inv_t"), 1)
                        V.tensor_tensor(TT[:, gs, :], TT[:, gs, :], bank(4 + g).rearrange("p (e t) -> p e t", e=4), ALU.add) \
                            .then_inc(sem("inv_tt"), 1)
                for c in range(2):
                    g = 2 * tt + c
                    r = slice(CHUNK * c, CHUNK * c + CHUNK)
                    dve.wait_ge(sem("u_mm"), g + 1)
                    dve.wait_ge(sem("u0_evac"), tt + 1)
                    V.tensor_tensor(Uc[r, :], PS[r, 512:1024], U0[r, :], ALU.add).then_inc(sem("u_ready"), 1)
                    if g < 3:
                        dve.wait_ge(sem("ds_mm"), g + 1)
                        link(V.tensor_tensor(dS[:], bank(2).rearrange("p (j t) -> p j t", j=NPAIR), St[:, g], ALU.add))
                        for j in range(NPAIR):
                            last = V.scalar_tensor_tensor(out=St[:, g + 1, j, :], in0=dS[:, j, :], scalar=dec[:, j, g:g + 1],
                                                          in1=C("blockones"), op0=ALU.mult, op1=ALU.mult)
                        last.then_inc(sem("state"), 1)
            dve.wait_ge(sem("y_sum"), 1)
            for j in range(2):
                V.scalar_tensor_tensor(out=yc[:, 2 * j:2 * j + 2, :].rearrange("p j t -> p (j t)"), in0=bank(4 + j), scalar=-1.0 / HD,
                                       in1=yT[:, 2 * j:2 * j + 2, :].rearrange("p j t -> p (j t)"), op0=ALU.mult, op1=ALU.add) \
                    .then_inc(sem("yc_ready"), 1)
            for j in range(NPAIR):
                last = V.scalar_tensor_tensor(out=bon[:, j, :], in0=rw[:, j, :], scalar=par_col("r_k", j), in1=rw[:, 4 + j, :],
                                              op0=ALU.mult, op1=ALU.mult)
            last.then_inc(sem("rkk"), 1)
            lo(U_SO[0] + RING)
            dve.wait_ge(sem("gates_ready"), 1)

            def gate(i, u, base):
                dve.wait_ge(sem("units_used"), u + 1)
                for c in range(2):
                    g = gates[:, base + 4 * i + 2 * c:base + 4 * i + 2 * c + 2, :].rearrange("p f t -> p (f t)")
                    last = V.tensor_tensor(g, bank(2 * i + c), g, ALU.mult)
                return last

            gate(0, U_SO[0], 0).then_inc(sem("merge_a"), 1)
            dve.wait_ge(sem("y_sd"), 1)
            link(V.reciprocal(yq[:], yq[:]))
            link(V.tensor_tensor(yc[:], yc[:], yq[:], ALU.mult))
            lo(U_SO[1] + RING)
            gate(1, U_SO[1], 0).then_inc(sem("merge_a"), 1)
            for j in range(NPAIR):
                link(V.tensor_scalar(yc[:, j, :], yc[:, j, :], par_col("lnx_w", j), par_col("lnx_b", j), ALU.mult, ALU.add))
            dve.wait_ge(sem("bonus_mm"), 1)
            for j in range(2):
                last = V.tensor_tensor(bon[:, 2 * j:2 * j + 2, :], bank(4 + j).rearrange("p (j t) -> p j t", j=2),
                                       rw[:, 8 + 2 * j:10 + 2 * j, :], ALU.mult)
            link(last)
            link(V.tensor_tensor(yc[:], yc[:], bon[:], ALU.add))
            dve.wait_ge(sem("g_mm"), 1)
            for j in range(NPAIR):
                V.tensor_tensor(orw[:, j, :], yc[:, j, :], PS[:, 6 * 512 + j * SEQ:6 * 512 + (j + 1) * SEQ], ALU.mult) \
                    .then_inc(sem("orw"), 1)
            for j in range(NPAIR):
                dve.wait_ge(sem("rwo_hi"), j + 1)
                V.tensor_tensor(rwol[:, j, :], orw[:, j, :], rwoh[:, j, :].bitcast(f32), ALU.subtract).then_inc(sem("rwo"), 1)
            for i, u in enumerate(U_RO):
                lo(u + RING)
                link(gate(i, u, 8))
                for f in range(4):
                    V.tensor_tensor(gates[:, 4 * i + f, :], gates[:, 4 * i + f, :], gates[:, 8 + 4 * i + f, :], ALU.add) \
                        .then_inc(sem("merge_sum"), 1)
            for f in range(KD):
                dve.wait_ge(sem("merged_hi"), f + 1)
                V.tensor_tensor(ml[:, f, :], gates[:, f, :], mh[:, f, :].bitcast(f32), ALU.subtract).then_inc(sem("merged"), 1)
            for u in U_O:
                lo(u + RING)

            def post(st, gain, loaded, b, then):
                c = NORM[st]
                dve.wait_ge(sem(loaded), 16)
                dve.wait_ge(sem("x_loaded"), 32)
                dve.wait_ge(norm_sem(st, "sd"), nth(st, "sd", 1))
                link(V.reciprocal(col(c + 4, 2), col(c + 2, 2)))
                for t in range(NT):
                    link(V.scalar_tensor_tensor(out=tmp[:, t, :], in0=PS[:, b * 512 + t * D:b * 512 + (t + 1) * D],
                                                scalar=col(c + 4 + t), in1=gain[:], op0=ALU.mult, op1=ALU.mult))
                    V.tensor_tensor(xres[:, t, :], xres[:, t, :], tmp[:, t, :], ALU.add).then_inc(norm_sem(then, "x"), 1)

            def residual(u, b, then):
                dve.wait_ge(sem("units_used"), u + 1)
                for t in range(NT):
                    V.tensor_tensor(xres[:, t, :], xres[:, t, :], PS[:, b * 512 + t * D:b * 512 + (t + 1) * D], ALU.add) \
                        .then_inc(norm_sem(then, "x"), 1)

            def pre(st, g, b):
                dve.wait_ge(norm_sem(st, "x"), nth(st, "x", NT))
                normalise(st, xres, xn)
                rest_T(st, g, xh, xl, 0, KD, b)

            post("p1", gmix, "gmix_loaded", 4, "n2")
            pre("n2", "norm_ffn_pre", 0)
            for i in range(FF_CHUNKS):
                lo(U_F["g", i] + RING)
                lo(U_F["u", i] + RING)
                dve.wait_ge(sem("ff_silu"), i + 1)
                if i >= 2:
                    dve.wait_ge(sem("ff_hi"), i - 1)
                V.tensor_tensor(fb[i % 2][:], fa[i % 2][:], bank(2 * (i % 2) + 1), ALU.mult).then_inc(sem("ff_out"), 1)
                if i:
                    lo(U_F["d", i - 1] + RING)
                dve.wait_ge(sem("ff_hi"), i + 1)
                V.tensor_tensor(fl[i % 2][:].rearrange("p f t -> p (f t)"), fb[i % 2][:],
                                fh[i % 2][:].rearrange("p f t -> p (f t)").bitcast(f32), ALU.subtract).then_inc(sem("ff_h"), 1)
            lo(U_F["d", FF_CHUNKS - 1] + RING)
            post("p2", gffn, "gffn_loaded", 4, "n3")
            pre("n3", "g_mix_2", 0)
            normalise("mem", mem, mem)
            for u in U_QK2 + U_V2:
                lo(u + RING)
            rest_T("mem", "g_mem_2", memh, meml, 0, KD, 4)
            for i in range(NH + 2):
                if i < NH:
                    b = (4 + i % 2) * 512
                    z = dz[i % 2]
                    dve.wait_ge(sem("d_z"), i + 1)
                    if i >= 2:
                        dve.wait_ge(sem("d_p"), 2 * (i - 1))
                    V.scalar_tensor_tensor(out=z[:], in0=PS[:, b:b + 384], scalar=HD ** -0.5, in1=C("dil"), op0=ALU.mult, op1=ALU.add) \
                        .then_inc(sem("d_z_read"), 1)
                    dve.wait_ge(sem("d_z_read"), i + 1)
                    V.tensor_reduce(out=col(DMX + i), in_=z[:, 0:P], axis=AX.X, op=ALU.max, negate=True)
                    V.tensor_reduce(out=col(DMX + NH + i), in_=z[:, P:384], axis=AX.X, op=ALU.max, negate=True) \
                        .then_inc(sem("d_max"), 1)
                lo(FILL2[i] + RING)
                if i == 6:
                    dve.wait_ge(sem("out2_evac"), 10)
                    link(V.tensor_tensor(cv[:, 1], cv[:, 1], cv[:, 2], ALU.mult))
                    for j in range(NPAIR):
                        last = V.tensor_scalar(cv[:, 2, j, :], cv[:, 1, j, :], par_col("conv_w_2", 8 + j), None, ALU.mult)
                    link(last)
                    for tap in (1, 0):
                        sh = 2 - tap
                        for j in range(NPAIR):
                            last = V.scalar_tensor_tensor(out=cv[:, 2, j, sh:SEQ], in0=cv[:, 1, j, 0:SEQ - sh],
                                                          scalar=par_col("conv_w_2", 4 * tap + j), in1=cv[:, 2, j, sh:SEQ],
                                                          op0=ALU.mult, op1=ALU.add)
                        link(last)
                    V.tensor_tensor(cv[:, 0], cv[:, 0], cv[:, 2], ALU.mult).then_inc(sem("c_gated"), 1)
            dve.wait_ge(sem("d_o"), NH)
            dve.wait_ge(sem("d_p"), 2 * NH)
            link(V.reciprocal(col(DRL, 16), col(DL, 16)))
            for t in range(NT):
                V.tensor_tensor(att[:, t, :].rearrange("p (h e) -> p h e", h=NH), bank(6 + t).rearrange("p (h e) -> p h e", h=NH),
                                col(DRL + NH * t, NH).unsqueeze(2).broadcast_to([P, NH, HD]), ALU.mult).then_inc(sem("att_raw"), 1)
            dve.wait_ge(sem("att_raw"), 2)
            normalise("att", att, att)
            for i in range(2):
                lo(U_VM[i] + RING)
            dve.wait_ge(sem("c_sd"), 1)
            link(V.reciprocal(crs[:], crs[:]))
            lo(U_VM[2] + RING)
            for j in range(NPAIR):
                V.scalar_tensor_tensor(out=cv[:, 0, j, :], in0=cv[:, 0, j, :], scalar=par_col("g_conv_out_2", j), in1=crs[:],
                                       op0=ALU.mult, op1=ALU.mult).then_inc(sem("conv_n"), 1)
            for j in range(NPAIR):
                dve.wait_ge(sem("conv_hi"), j + 1)
                V.tensor_tensor(m2l[:, 4 + j, :], cv[:, 0, j, :], m2h[:, 4 + j, :].bitcast(f32), ALU.subtract) \
                    .then_inc(sem("conv_xT"), 1)
            rest_T("att", "g_attn_out_2", m2h, m2l, 0, NPAIR, 6)
            lo(U_VM[3] + RING)
            for u in U_O2:
                lo(u + RING)
            residual(U_O2[3], 0, "n4")
            pre("n4", "g_xattn_2", 4)
            for u in U_QM:
                lo(u + RING)
            for i in range(MEM_HEADS + 2):
                if i < MEM_HEADS:
                    dve.wait_ge(sem("m_z"), i + 1)
                    link(V.tensor_reduce(out=col(MMX + 2 * i, 2), in_=bank(2 + i % 2).rearrange("p (t m) -> p t m", t=2), axis=AX.X,
                                         op=ALU.max, negate=True))
                    V.tensor_scalar(col(MMX + 2 * i, 2), col(MMX + 2 * i, 2), 256 ** -0.5, None, ALU.mult).then_inc(sem("m_max"), 1)
                    dve.wait_ge(sem("m_exp"), 2 * i + 2)
                    link(V.reciprocal(col(MSUM + 2 * i, 2), col(MSUM + 2 * i, 2)))
                    for t in range(NT):
                        last = V.tensor_scalar(mp[i % 2][:, t, :], mp[i % 2][:, t, :], col(MSUM + 2 * i + t), None, ALU.mult)
                    last.then_inc(sem("m_p"), 1)
                if i >= 2:
                    h = i - 2
                    dve.wait_ge(sem("om_hi"), h + 1)
                    V.tensor_tensor(oml[:, 2 * h:2 * h + 2, :], bank(6 + h % 2).rearrange("p (e t) -> p e t", e=2),
                                    omh[:, 2 * h:2 * h + 2, :].bitcast(f32), ALU.subtract).then_inc(sem("om"), 2)
            for u in U_OM:
                lo(u + RING)
            residual(U_OM[3], 0, "n5")
            pre("n5", "g_mlp_2", 4)
            for i in range(FF2_CHUNKS):
                lo(U_M["u", i] + RING)
                dve.wait_ge(sem("mlp_out"), i + 1)
                if i >= 2:
                    dve.wait_ge(sem("mlp_hi"), i - 1)
                V.tensor_tensor(fb[i % 2][:], fa[i % 2][:], fa[i % 2][:], ALU.mult).then_inc(sem("mlp_sq"), 1)
                if i:
                    lo(U_M["d", i - 1] + RING)
                dve.wait_ge(sem("mlp_hi"), i + 1)
                V.tensor_tensor(fl[i % 2][:].rearrange("p f t -> p (f t)"), fb[i % 2][:],
                                fh[i % 2][:].rearrange("p f t -> p (f t)").bitcast(f32), ALU.subtract).then_inc(sem("mlp_h"), 1)
            residual(U_M["d", FF2_CHUNKS - 1], 4, "fin")
            dve.wait_ge(norm_sem("fin", "x"), nth("fin", "x", NT))
            c = NORM["fin"]
            dve.wait_ge(sem("gfin_loaded"), 16)
            dve.wait_ge(norm_sem("fin", "sd"), nth("fin", "sd", 1))
            link(V.reciprocal(col(c + 4, 2), col(c + 2, 2)))
            for t in range(NT):
                V.scalar_tensor_tensor(out=xn[:, t, :], in0=xres[:, t, :], scalar=col(c + 4 + t), in1=gfin[:],
                                       op0=ALU.mult, op1=ALU.mult).then_inc(norm_sem("fin", "xn"), 1)


_INS = ["x", "w_in", "w_up", "a_up", "g_up", "w_sb_out", "w_rw_out", "w_o", "norm_mix_post", "w_ffn_gate", "w_ffn_up",
        "w_ffn_down", "norm_ffn_post", "mem_2", "w_in_2", "w_out_2", "w_q_mem_2", "w_kv_mem_2", "w_o_mem_2", "w_up_2",
        "w_down_2", "g_final_2"]


def kernel(**inputs):
    import numpy as _np
    import concourse.bacc as _bacc
    from concourse import mybir as _mybir
    from concourse.bass_utils import run_bass_kernel_spmd as _run

    nc = _bacc.Bacc("TRN2", target_bir_lowering=False, num_devices=1)
    arrays, A = {}, {}
    given = {n: _np.ascontiguousarray(inputs[n]) for n in _INS}
    rows = [_np.ascontiguousarray(inputs[n]).reshape(k, P) for n, k in PARAM_ROWS]
    given["params"] = _np.ascontiguousarray(_np.concatenate(rows, 0).T)
    given["consts"] = CONSTS
    for name, a in given.items():
        arrays[f"in_{name}_dram"] = a
        A[name] = nc.dram_tensor(f"in_{name}_dram", a.shape, _mybir.dt.from_np(a.dtype), kind="ExternalInput").ap()
    out = nc.dram_tensor("out_0_dram", (1, SEQ, D), _mybir.dt.float32, kind="ExternalOutput").ap()
    block_kernel(nc, A, out)
    r = _run(nc, [arrays], core_ids=[0])
    return r.results[0]["out_0_dram"]
```

```python
import concourse.bass as bass
from concourse import mybir
from contextlib import ExitStack
import numpy as np

P = 128
SEQ = 256
NT = SEQ // P
D = 1024
KD = D // P
HW = 512
NPAIR = HW // P
HD = 64
NH = HW // HD
CHUNK = 64
RW0 = 3 * HW
GATE0 = RW0 + 3 * HW + 256
DFF = ((8 * D + 3 * 256 - 1) // (3 * 256)) * 256
DFF2 = 4 * D
FF_CHUNKS = DFF // 256
FF2_CHUNKS = DFF2 // 256
MEM_HEADS = 4
RING = 3
UNIT = 2048

PARAM_ROWS = [("norm_mix_pre", 8), ("b_gate", 16), ("mu_rw", 14), ("w0", 4), ("a0", 4), ("k_k", 4),
              ("k_a", 4), ("r_k", 4), ("lnx_w", 4), ("lnx_b", 4), ("norm_ffn_pre", 8), ("conv_w_2", 12),
              ("g_conv_out_2", 4), ("g_attn_out_2", 4), ("g_mix_2", 8), ("g_xattn_2", 8), ("g_mem_2", 8),
              ("g_mlp_2", 8)]
PCOL = {}
_at = 0
for _n, _k in PARAM_ROWS:
    PCOL[_n] = _at
    _at += _k
NPARAM = _at


def shape_constants():
    i = np.arange(P)[:, None]
    j = np.arange(P)[None, :]
    t = np.arange(SEQ)[None, :]
    parts, cols = {"f32": [], "f16": []}, {}

    def put(name, a, kind="f32"):
        at = sum(x.shape[1] for x in parts[kind])
        a = np.broadcast_to(a, (P, a.shape[1]))
        cols[name] = (at, at + a.shape[1])
        parts[kind].append(a)

    same = (i // CHUNK) == (j // CHUNK)
    put("ident", (i == j) * 1.0)
    put("tri", (i >= j) * 1.0)
    put("ones", np.ones((P, P)))
    put("blockones", same * 1.0)
    put("incl", (same & (i <= j)) * 1.0, "f16")
    put("strict", (same & (i < j)) * 1.0, "f16")
    for m in (1, 2, 4, 8, 16, 32):
        two = (i // (2 * m)) == (j // (2 * m))
        put(f"level{m}", (two & (i % (2 * m) < m) & (j % (2 * m) >= m)) * 1.0, "f16")
    ks = np.concatenate([(i < t), (i + P < t[:, P:])], 1)
    put("sb_neg", ks * -1.0, "f16")
    put("sb_add", np.where(ks, 0.0, -1e30))

    def count(q, s):
        d = q - s
        c = ((d >= 0) & (d <= 128)) * 1 + ((d >= 0) & (d % 4 == 0)) * 1 + ((d >= 0) & (d % 16 == 0)) * 1
        return np.where(c > 0, np.log(np.maximum(c, 1)), -1e30)

    put("dil", np.concatenate([count(i, j), count(i + P, t)], 1))
    put("reset", (t % CHUNK != 0) * 1.0, "f16")
    put("gather", np.concatenate([np.arange(NH)[None, :] == 2 * f + i // HD for f in range(NPAIR)], 1) * 1.0)
    put("spread", (i == np.arange(HW)[None, :] // HD) * 1.0)
    return (np.concatenate(parts["f32"], 1).astype(np.float32), np.concatenate(parts["f16"], 1).astype(np.float16), cols)


CONSTS, MASKS, CCOL = shape_constants()
NCONST, NMASK = CONSTS.shape[1], MASKS.shape[1]


def block_kernel(nc, A, out, dbg=None):
    f32 = mybir.dt.float32
    f32r = mybir.dt.float32r
    ALU = mybir.AluOpType
    ACT = mybir.ActivationFunctionType
    AX = mybir.AxisListType
    KB = 1024
    BASE = 16512

    ctx = ExitStack()
    with ctx:
        def at(name, kb, shape, dt=f32):
            return nc.alloc_sbuf_tensor_at(name, shape, dt, offset=BASE + int(kb * KB))

        sems = {}

        def sem(name):
            if name not in sems:
                sems[name] = ctx.enter_context(nc.semaphore(name))
            return sems[name]

        raw = [at(f"raw{i}", 8 * i, [P, UNIT]) for i in range(RING)]
        whi = [at(f"whi{i}", 24 + 16 * i, [P, UNIT], f32r) for i in range(RING)]
        wlo = [at(f"wlo{i}", 32 + 16 * i, [P, UNIT], f32r) for i in range(RING)]
        cst = at("cst", 72, [P, NCONST])
        msk = at("msk", 80, [P, NMASK], mybir.dt.float16)
        par = at("par", 84, [P, NPARAM])
        small = at("small", 84.5, [P, 128])
        XR = 85
        xres = at("xres", XR, [P, NT, D])
        A0 = 93
        xh = at("xh", A0, [P, KD, SEQ], f32r)
        xl = at("xl", A0 + 8, [P, KD, SEQ], f32r)
        W = 109
        gates = at("gates", W, [P, 16, SEQ])
        sboh = at("sboh", W + 16, [P, NPAIR, SEQ], f32r)
        sbol = at("sbol", W + 20, [P, NPAIR, SEQ], f32r)
        xn = at("xn", W + 24, [P, NT, D])
        rw = at("rw", W + 24, [P, 14, SEQ])
        eP = at("eP", W + 38, [P, NPAIR, SEQ])
        eN = at("eN", W + 42, [P, NPAIR, SEQ])
        eX = at("eX", W + 46, [P, NPAIR, SEQ])
        kk = at("kk", W + 50, [P, NPAIR, SEQ])
        sg = at("sg", W + 54, [P, NPAIR, SEQ])
        cs = at("cs", W + 58, [P, NPAIR, SEQ])
        ag = at("ag", W + 62, [P, NPAIR, SEQ])
        kq = at("kq", W + 66, [P, NPAIR, SEQ])
        sq = at("sq", W + 70, [P, NPAIR, SEQ])
        sk = at("sk", W + 74, [P, NPAIR, SEQ])
        sv = at("sv", W + 78, [P, NT, HW])
        st1 = [at(f"st1{i}", W + 82 + 6 * i, [P, 384]) for i in range(2)]
        st2 = [at(f"st2{i}", W + 83.5 + 6 * i, [P, 384]) for i in range(2)]
        st3 = [at(f"st3{i}", W + 85 + 6 * i, [P, 384]) for i in range(2)]
        st4 = [at(f"st4{i}", W + 86.5 + 6 * i, [P, 384]) for i in range(2)]
        lora = at("lora", W + 94, [P, HW])
        gup = at("gup", W + 96, [P, HW])
        stg = [at(f"stg{i}", XR + 2.0625 * i, [P, 2, SEQ + 1]) for i in range(2)]
        diff = at("diff", XR + 4.25, [P, 2, SEQ])
        Tm = at("Tm", W + 54, [P, NH, P])
        TT = at("TT", W + 58, [P, NH, P])
        Gm = at("Gm", W + 62, [P, NH, P])
        Xm = [at("Xm0", W + 66, [P, NH, P]), at("Xm1", W + 94, [P, NH, P])]
        XT = at("XT", W + 70, [P, NH, P])
        AK = at("AK", W + 74, [P, NH, P])
        RB = at("RB", W + 78, [P, NH, P])
        RK = at("RK", W + 82, [P, NH, P])
        St = at("St", W + 86, [P, 4, NPAIR, P])
        yT = at("yT", XR, [P, NPAIR, SEQ])
        dS = at("dS", XR + 4, [P, NPAIR, P])
        at_ = at("a_tok", A0, [P, HW])
        bt_ = at("b_tok", A0 + 2, [P, HW])
        kt_ = at("k_tok", A0 + 4, [P, HW])
        vt_ = at("v_tok", A0 + 6, [P, HW])
        WT = at("WT", A0 + 8, [P, NPAIR, P])
        AV = at("AV", A0 + 10, [P, HW])
        U0 = at("U0", A0 + 12, [P, HW])
        Uc = at("Uc", A0 + 14, [P, HW])
        yc = at("yc", W + 54, [P, NPAIR, SEQ])
        yq = at("yq", W + 58, [P, NPAIR, SEQ])
        bon = at("bon", XR, [P, NPAIR, SEQ])
        rkk = at("rkk", W + 78, [P, NPAIR, SEQ])
        grs = at("grs", W + 62, [NH, SEQ])
        orw = at("orw", W + 66, [P, NPAIR, SEQ])
        rwoh = at("rwoh", W + 70, [P, NPAIR, SEQ], f32r)
        rwol = at("rwol", W + 74, [P, NPAIR, SEQ], f32r)
        mh = at("mh", A0, [P, KD, SEQ], f32r)
        ml = at("ml", A0 + 8, [P, KD, SEQ], f32r)
        gmix = at("gmix", W + 38, [P, D])
        gffn = at("gffn", W + 42, [P, D])
        gfin = at("gfin", W + 46, [P, D])
        tmp = at("tmp", W + 16, [P, NT, D])
        junk = at("junk", W, [P, D])
        dg_ = at("dg", W + 24, [P, NT, P])
        dg = {n: dg_ for n in ("n1", "n2", "n3", "n4", "n5")}
        dg["mem"] = at("dg_mem", W + 25, [P, NT, P])
        dg["att"] = at("dg_att", W + 50, [P, NT, P])
        fa = [at(f"fa{i}", W + 54 + 2 * i, [P, 2 * SEQ]) for i in range(2)]
        fb = [at(f"fb{i}", W + 58 + 2 * i, [P, 2 * SEQ]) for i in range(2)]
        fh = [at(f"fh{i}", W + 62 + 2 * i, [P, 2, SEQ], f32r) for i in range(2)]
        fl = [at(f"fl{i}", W + 66 + 2 * i, [P, 2, SEQ], f32r) for i in range(2)]
        q2 = at("q2", W, [P, NPAIR, SEQ])
        k2 = at("k2", W + 4, [P, NPAIR, SEQ])
        v2 = at("v2", W + 8, [P, NT, HW])
        att = at("att", W + 12, [P, NT, HW])
        cv = at("cv", W + 16, [P, 3, NPAIR, SEQ])
        m2h = at("m2h", W + 28, [P, KD, SEQ], f32r)
        m2l = at("m2l", W + 36, [P, KD, SEQ], f32r)
        dz = [at(f"dz{i}", W + 50 + 4.5 * i, [P, 384]) for i in range(2)]
        dp = [at(f"dp{i}", W + 51.5 + 4.5 * i, [P, 384]) for i in range(2)]
        dq = [at(f"dq{i}", W + 53 + 4.5 * i, [P, 384]) for i in range(2)]
        km = at("km", W + 59, [P, KD, SEQ])
        crs = at("crs", W + 67, [P, SEQ])
        memh = at("memh", W + 71, [P, KD, SEQ], f32r)
        meml = at("meml", W + 79, [P, KD, SEQ], f32r)
        mem = at("mem", W + 87, [P, NT, D])
        vm = at("vm", W + 87, [P, NT, D])
        qm = at("qm", W, [P, KD, SEQ])
        mp = [at(f"mp{i}", W + 8 + 4 * i, [P, NT, SEQ]) for i in range(2)]
        mq = [at(f"mq{i}", W + 10 + 4 * i, [P, NT, SEQ]) for i in range(2)]
        omh = at("omh", W + 16, [P, KD, SEQ], f32r)
        oml = at("oml", W + 24, [P, KD, SEQ], f32r)
        EVENTS = {"sq": (["n1", "p1", "n2", "p2", "n3", "mem", "att", "n4", "n5", "fin"], 2),
                  "sd": (["n1", "p1", "n2", "p2", "n3", "mem", "att", "n4", "n5", "fin"], 2),
                  "x": (["n2", "n3", "n4", "n5", "fin"], 2),
                  "y": (["p1", "p2"], 2 * NT),
                  "dg": (["n1", "n2", "n3", "mem", "att", "n4", "n5"], NT),
                  "T": (["n1", "n2", "n3", "mem", "att", "n4", "n5"], KD),
                  "hi": (["n1", "n2", "n3", "mem", "att", "n4", "n5"], KD),
                  "xT": (["n1", "n2", "n3", "mem", "att", "n4", "n5"], KD)}

        def norm_sem(st, what):
            return sem("norm_" + what)

        def nth(st, what, n):
            order, each = EVENTS[what]
            before = order.index(st) * each
            if each == KD and "att" in order[:order.index(st)]:
                before -= KD - NPAIR
            return before + n

        PS = ctx.enter_context(nc.psum_tensor("PS", [P, 8 * 512], f32))

        def bank(b):
            return PS[:, b * 512:(b + 1) * 512]

        def C(name):
            a, b = CCOL[name]
            return cst[:, a:b]

        def M(name):
            a, b = CCOL[name]
            return msk[:, a:b]

        def par_col(name, i=0):
            c = PCOL[name] + i
            return par[:, c:c + 1]

        def col(i, n=1):
            return small[:, i:i + n]

        EPS, GEPS = 0, 1
        NORM = {n: 2 + 6 * i for i, n in enumerate(["n1", "p1", "n2", "p2", "n3", "mem", "att", "n4", "n5", "fin"])}
        DMX, DL, DRL = 62, 78, 94
        SQ2 = 126
        MMX, MSUM = 110, 118
        dec = at("dec", W + 98, [P, NPAIR, 4])

        def halves(ap, v, second):
            m = 2 ** v
            return ap.rearrange("p (a b) -> p a b", b=2 * m)[:, :, second * m:(second + 1) * m]

        units = []

        def cols_unit(w, c0, n=256):
            units.append((w[:, c0:c0 + n].rearrange("(k p) n -> p k n", p=P), n))
            return len(units) - 1

        def rows_unit(w, k0, k, c0=0, n=D):
            units.append((w[k0 * P:(k0 + k) * P, c0:c0 + n].rearrange("(k p) n -> p k n", p=P), n))
            return len(units) - 1

        w_in, w_in2, w_kv = A["w_in"][0], A["w_in_2"], A["w_kv_mem_2"]
        U_RW = [cols_unit(w_in, RW0 + c) for c in (1536, 512, 768, 0, 256, 1024, 1280)]
        RW_TILE = [12, 4, 6, 0, 2, 8, 10]
        U_QK = [cols_unit(w_in, 256 * c) for c in range(4)]
        U_V = [rows_unit(w_in, 4 * i, 4, 2 * HW, HW) for i in range(2)]
        U_G = [cols_unit(w_in, GATE0 + 256 * c) for c in range(8)]
        U_SO = [cols_unit(A["w_sb_out"][0], 512 * c, 512) for c in range(2)]
        U_RO = [cols_unit(A["w_rw_out"][0], 512 * c, 512) for c in range(2)]
        U_O = [rows_unit(A["w_o"][0], 2 * i, 2) for i in range(4)]
        U_F = {}
        for i in range(FF_CHUNKS + 1):
            if i < FF_CHUNKS:
                U_F["g", i] = cols_unit(A["w_ffn_gate"][0], 256 * i)
                U_F["u", i] = cols_unit(A["w_ffn_up"][0], 256 * i)
            if i:
                U_F["d", i - 1] = rows_unit(A["w_ffn_down"][0], 2 * (i - 1), 2)
        U_QK2 = [cols_unit(w_in2, 256 * c) for c in range(4)]
        U_V2 = [rows_unit(w_in2, 4 * i, 4, 2 * HW, HW) for i in range(2)]
        U_CV = [cols_unit(w_in2, 3 * HW + 256 * c) for c in range(6)]
        U_KM = [cols_unit(w_kv, 256 * c) for c in range(4)]
        U_VM = [rows_unit(w_kv, 2 * i, 2, D, D) for i in range(4)]
        U_O2 = [rows_unit(A["w_out_2"], 2 * i, 2) for i in range(4)]
        U_QM = [cols_unit(A["w_q_mem_2"], 256 * c) for c in range(4)]
        U_OM = [rows_unit(A["w_o_mem_2"], 2 * i, 2) for i in range(4)]
        U_M = {}
        for i in range(FF2_CHUNKS + 1):
            if i < FF2_CHUNKS:
                U_M["u", i] = cols_unit(A["w_up_2"], 256 * i)
            if i:
                U_M["d", i - 1] = rows_unit(A["w_down_2"], 2 * (i - 1), 2)
        NU = len(units)
        TILE_V, TILE_O, TILE_F, TILE_V2, TILE_VM, TILE_O2, TILE_OM, TILE_M = range(1, 9)
        FILL2 = U_CV + U_KM

        raw_loaded = [sem(f"raw_loaded{i}") for i in range(RING)]

        block = ctx.enter_context(nc.Block())

        @block.sync
        def _(sp):
            for t in range(NT):
                sp.dma_start(xres[:, t, :], A["x"][0, t * P:(t + 1) * P, :]).then_inc(sem(f"x_loaded{t}"), 16)
            for u, (src, n) in enumerate(units):
                s = u % RING
                if u >= RING:
                    sp.wait_ge(sem("unit_split"), u - RING + 1)
                sp.dma_start(raw[s][:].rearrange("p (k n) -> p k n", n=n), src).then_inc(raw_loaded[s], 16)
                if u == RING:
                    sp.dma_start(lora[0:HD, :], A["w_up"][0]).then_inc(sem("lora_loaded"), 16)
                    sp.dma_start(lora[HD:P, :], A["a_up"][0]).then_inc(sem("lora_loaded"), 16)
                    sp.dma_start(gup[:], A["g_up"][0]).then_inc(sem("lora_loaded"), 16)
                    sp.dma_start(cst[:, P:], A["consts"][:, P:]).then_inc(sem("cst_loaded"), 16)
                    sp.dma_start(msk[:], A["masks"]).then_inc(sem("msk_loaded"), 16)
                if u == U_O[0]:
                    sp.wait_ge(sem("yc_ready"), 2)
                    sp.dma_start(xres[:], A["x"][0].rearrange("(t p) n -> p t n", p=P)).then_inc(sem("x_loaded0"), 16)
                    sp.dma_start(gmix[:], A["norm_mix_post"].rearrange("a n -> (a n)").partition_broadcast(P)).then_inc(sem("gmix_loaded"), 16)
                    sp.dma_start(gffn[:], A["norm_ffn_post"].rearrange("a n -> (a n)").partition_broadcast(P)).then_inc(sem("gffn_loaded"), 16)
                    sp.dma_start(gfin[:], A["g_final_2"].partition_broadcast(P)).then_inc(sem("gfin_loaded"), 16)
                    sp.dma_start(mem[:], A["mem_2"][0].rearrange("(t p) n -> p t n", p=P)).then_inc(sem("mem_loaded"), 16)
            for tt in range(NT):
                sp.wait_ge(sem("result"), tt + 1)
                sp.dma_start(out[0, tt * P:(tt + 1) * P, :], xn[:, tt, :]).then_inc(sem("stored"), 16)
            sp.wait_ge(sem("stored"), 16 * NT)

        @block.tensor
        def _(pe):
            def mm(o, l, r, start, stop, **kw):
                return nc.tensor.matmul(o, l, r, start=start, stop=stop, **kw)

            def slot(h):
                return 4 * (h % 2) + h // 2

            def split(u, n):
                pe.wait_ge(sem("unit_split"), u + 1)
                return (whi[u % RING][:].rearrange("p (k n) -> p k n", n=n),
                        wlo[u % RING][:].rearrange("p (k n) -> p k n", n=n))

            def by_feature(u, hi, lo, b, st=None):
                n = units[u][1]
                kt = UNIT // n
                wh, wl = split(u, n)
                for f in range(n // P):
                    o = PS[:, b * 512 + f * SEQ:b * 512 + (f + 1) * SEQ]
                    for k in range(kt):
                        if st and f == 0:
                            pe.wait_ge(norm_sem(st, "xT"), nth(st, "xT", max(k + 1, 2)))
                        fs = slice(f * P, (f + 1) * P)
                        mm(o, wh[:, k, fs], hi[:, k, :], k == 0, False)
                        mm(o, wh[:, k, fs], lo[:, k, :], False, False)
                        last = mm(o, wl[:, k, fs], hi[:, k, :], False, k == kt - 1)
                last.then_inc(sem("units_used"), 1)

            def by_token(u, hi, lo, k0, b, first, end):
                n = units[u][1]
                kt = UNIT // n
                wh, wl = split(u, n)
                steps = [(k, t) for t in range(NT) for k in range(kt)] if end else [(k, t) for k in range(kt) for t in range(NT)]
                for k, t in steps:
                    ts = slice(t * P, (t + 1) * P)
                    for c in range(n // 512):
                        o = bank(b + t * (n // 512) + c)
                        ns = slice(c * 512, (c + 1) * 512)
                        mm(o, hi[:, k0 + k, ts], wh[:, k, ns], first and k == 0, False)
                        mm(o, hi[:, k0 + k, ts], wl[:, k, ns], False, False)
                        last = mm(o, lo[:, k0 + k, ts], wh[:, k, ns], False, end and k == kt - 1)
                    if end and (k, t) == (kt - 1, 0):
                        last.then_inc(sem("tile_done"), 1)
                last.then_inc(sem("units_used"), 1)

            def transpose_in(st, src, nf, b):
                for t in range(NT):
                    pe.wait_ge(norm_sem(st, "dg"), nth(st, "dg", t + 1))
                    for f in range(nf):
                        last = mm(PS[:, b * 512 + f * SEQ + t * P:b * 512 + f * SEQ + (t + 1) * P],
                                  src[:, t, f * P:(f + 1) * P], dg[st][:, t, :], True, True)
                        if t == NT - 1:
                            last.then_inc(norm_sem(st, "T"), 1)

            transpose_in("n1", xres, KD, 4)
            for i, u in enumerate(U_RW):
                if i >= 2:
                    pe.wait_ge(sem("out_evac"), i - 1)
                by_feature(u, xh, xl, i % 2, None if i else "n1")
                if i == 2:
                    pe.wait_ge(sem("lora_in"), 1)
                    pe.wait_ge(sem("lora_loaded"), 48)
                    for j in range(NPAIR):
                        mm(PS[:, 4 * 512 + j * SEQ:4 * 512 + (j + 1) * SEQ], lora[0:HD, j * P:(j + 1) * P],
                           rw[0:HD, 12, :], True, True)
                    for j in range(NPAIR):
                        last = mm(PS[:, 6 * 512 + j * SEQ:6 * 512 + (j + 1) * SEQ], lora[HD:P, j * P:(j + 1) * P],
                                  rw[HD:P, 12, :], True, True)
                    last.then_inc(sem("lora_out"), 1)
                if i == 4:
                    pe.wait_ge(sem("kk_sq"), 1)
                    pe.wait_ge(sem("lora_evac"), 1)
                    pe.wait_ge(sem("cst_loaded"), 16)
                    for j in range(NPAIR):
                        last = mm(PS[:, 4 * 512 + j * SEQ:4 * 512 + (j + 1) * SEQ], C("blockones"), kq[:, j, :], True, True)
                    last.then_inc(sem("kk_ss"), 1)
            for i, u in enumerate(U_QK):
                pe.wait_ge(sem("out_evac"), i + 6)
                by_feature(u, xh, xl, (i + 7) % 2)
            for i, u in enumerate(U_V):
                by_token(u, xh, xl, 4 * i, 2, i == 0, i == 1)
                if i == 0:
                    pe.wait_ge(sem("kk_sd"), 1)
                    for j in range(NPAIR):
                        mm(PS[:, 4 * 512 + j * SEQ:4 * 512 + (j + 1) * SEQ], gup[:, j * P:(j + 1) * P], rw[:, 13, :], True, True)
                    pe.wait_ge(sem("rkk"), 1)
                    for j in range(NPAIR):
                        last = mm(PS[:, 6 * 512 + j * SEQ:6 * 512 + (j + 1) * SEQ], C("blockones"), rkk[:, j, :], True, True)
                    last.then_inc(sem("bonus_mm"), 1)
            pe.wait_ge(sem("gn_pre"), 1)
            for i in range(NH + 1):
                r = slice(HD * (i % 2), HD * (i % 2) + HD)
                b = 4 + i % 2
                if i < NH:
                    if i == 0:
                        pe.wait_ge(sem("out_evac"), 11)
                    if i >= 2:
                        pe.wait_ge(sem("sb_arg_read"), i - 1)
                    mm(PS[:, b * 512:b * 512 + SEQ], sk[r, i // 2, 0:P], sq[r, i // 2, :], True, False, skip_group_check=True)
                    mm(PS[:, b * 512 + SEQ:b * 512 + 384], sk[r, i // 2, P:SEQ], sq[r, i // 2, P:SEQ], False, True, skip_group_check=True) \
                        .then_inc(sem("sb_z"), 1)
                    pe.wait_ge(sem("out_evac"), i + 10)
                    by_feature(U_G[i], xh, xl, (i + 11) % 2)
                    pe.wait_ge(sem("sb_lf"), i + 1)
                    mm(PS[:, b * 512:b * 512 + 384], C("tri"), st2[i % 2][:], False, False, skip_group_check=True)
                    mm(PS[:, b * 512 + P:b * 512 + SEQ], C("ones"), st2[i % 2][:, SEQ:384], False, True,
                       skip_group_check=True).then_inc(sem("sb_arg"), 1)
                if i >= 1:
                    h = i - 1
                    o = PS[HD * (h % 2):HD * (h % 2) + HD, (6 + h // 4) * 512 + (h // 2 % 2) * SEQ:
                           (6 + h // 4) * 512 + (h // 2 % 2) * SEQ + SEQ]
                    pe.wait_ge(sem("sb_w"), h + 1)
                    if h == 0:
                        pe.wait_ge(sem("sv_ready"), 2)
                    mm(o, sv[:, 0, h * HD:(h + 1) * HD], st4[h % 2][:, 0:SEQ], True, False, skip_group_check=True)
                    mm(o[:, P:SEQ], sv[:, 1, h * HD:(h + 1) * HD], st4[h % 2][:, SEQ:384], False, True,
                       skip_group_check=True).then_inc(sem("sb_o"), 1)

            pe.wait_ge(sem("rw_pre"), 1)
            for tt in range(NT):
                ts = slice(tt * P, (tt + 1) * P)
                if tt == 0:
                    pe.wait_ge(sem("sb_evac"), 4)
                else:
                    pe.wait_ge(sem("y_evac"), tt)
                    pe.wait_ge(sem("state"), 2 * tt + 1)
                for q, src in enumerate((eX, kk, eN, rw)):
                    for j in range(NPAIR):
                        s = src[:, 8 + j, ts] if q == 3 else src[:, j, ts]
                        last = nc.tensor.transpose(PS[:, (4 + q) * 512 + j * P:(4 + q) * 512 + (j + 1) * P], s, C("ident"))
                    last.then_inc(sem("tok_T"), 1)
                for q, (l, r) in enumerate(((kk, eX), (eN, eX), (kk, eP), (eN, eP))):
                    for g in range(2):
                        b = (2 * q + g) % 8
                        if q == 0 and g == 0:
                            pe.wait_ge(sem("out_evac"), 19)
                        if b >= 4:
                            pe.wait_ge(sem("tok_evac"), 4 * tt + b - 3)
                        p = slice(HD * g, HD * g + HD)
                        for e in range(4):
                            h = 2 * e + g
                            last = mm(PS[:, b * 512 + e * P:b * 512 + (e + 1) * P], l[p, h // 2, ts], r[p, h // 2, ts], True, True)
                        last.then_inc(sem("pair_mm"), 1)
                for g in range(2):
                    pe.wait_ge(sem("xm"), 12 * tt + g + 1)
                    pe.wait_ge(sem("pair_evac"), 8 * tt + 2)
                    for e in range(4):
                        last = nc.tensor.transpose(PS[:, g * 512 + e * P:g * 512 + (e + 1) * P], Xm[0][:, 4 * g + e, :], C("ident"))
                    last.then_inc(sem("inv_T1"), 1)
                for v in range(1, 6):
                    for g in range(2):
                        pe.wait_ge(sem("xm"), 12 * tt + 2 * v + g + 1)
                        pe.wait_ge(sem("inv_t"), 10 * tt + 2 * (v - 1) + g + 1)
                        if v == 1:
                            pe.wait_ge(sem("pair_evac"), 8 * tt + 8)
                        for e in range(4):
                            h = 4 * g + e
                            last = mm(PS[:, g * 512 + e * P:g * 512 + (e + 1) * P], Xm[v % 2][:, h, :], Tm[:, h, :], True, True)
                        last.then_inc(sem("inv_g"), 1)
                    for g in range(2):
                        pe.wait_ge(sem("inv_g_evac"), 10 * tt + 2 * (v - 1) + g + 1)
                        pe.wait_ge(sem("inv_tt"), 12 * tt + 2 * (v - 1) + g + 1)
                        if v < 5:
                            for e in range(4):
                                mm(PS[:, (2 + g) * 512 + e * HD:(2 + g) * 512 + (e + 1) * HD], TT[:, 4 * g + e, :],
                                   halves(Gm[:, 4 * g + e, :], v, 0), True, True)
                        for e in range(4):
                            last = mm(PS[:, (4 + g) * 512 + e * HD:(4 + g) * 512 + (e + 1) * HD], Gm[:, 4 * g + e, :],
                                      halves(TT[:, 4 * g + e, :], v, 1), True, True)
                        last.then_inc(sem("inv_up"), 1)
                for h in range(NH):
                    o = PS[:, 7 * 512 + h * HD:7 * 512 + (h + 1) * HD]
                    last = mm(o, AK[:, slot(h), :], vt_[:, h * HD:(h + 1) * HD], True, True)
                last.then_inc(sem("av_mm"), 1)
                pe.wait_ge(sem("inv_tt"), 12 * tt + 12)
                for h in range(NH):
                    p = slice(HD * (h % 2), HD * (h % 2) + HD)
                    last = mm(PS[p, 6 * 512 + (h // 2) * P:6 * 512 + (h // 2 + 1) * P], at_[:, h * HD:(h + 1) * HD], TT[:, slot(h), :],
                              True, True, skip_group_check=True)
                last.then_inc(sem("wt_mm"), 1)
                pe.wait_ge(sem("av_evac"), tt + 1)
                for h in range(NH):
                    last = mm(PS[:, h * HD:(h + 1) * HD], TT[:, slot(h), :], AV[:, h * HD:(h + 1) * HD], True, True)
                last.then_inc(sem("u0_mm"), 1)
                pe.wait_ge(sem("wt_evac"), tt + 1)
                for c in range(2):
                    g = 2 * tt + c
                    rs_ = slice(CHUNK * c, CHUNK * c + CHUNK)
                    pe.wait_ge(sem("state"), g + 1)
                    for j in range(NPAIR):
                        last = mm(PS[rs_, 512 + j * P:512 + (j + 1) * P], WT[:, j, rs_], St[:, g, j, :], True, True,
                                  skip_group_check=True)
                    last.then_inc(sem("u_mm"), 1)
                    pe.wait_ge(sem("u_ready"), g + 1)
                    if g < 3:
                        for j in range(NPAIR):
                            o = PS[:, 2 * 512 + j * P:2 * 512 + (j + 1) * P]
                            js = slice(j * P, (j + 1) * P)
                            mm(o, bt_[rs_, js], Uc[rs_, js], True, False)
                            last = mm(o, kt_[rs_, js], vt_[rs_, js], False, True)
                        last.then_inc(sem("ds_mm"), 1)
                for j in range(NPAIR):
                    b0 = 3 * 512 + j * P
                    mm(PS[:, b0:b0 + CHUNK], St[:, 2 * tt, j, :], eP[:, j, tt * P:tt * P + CHUNK], True, False,
                       skip_group_check=True)
                    mm(PS[:, b0 + CHUNK:b0 + P], St[:, 2 * tt + 1, j, :], eP[:, j, tt * P + CHUNK:(tt + 1) * P], False, False,
                       skip_group_check=True)
                    for e in range(2):
                        h = 2 * j + e
                        o = PS[HD * e:HD * e + HD, b0:b0 + P]
                        mm(o, Uc[:, h * HD:(h + 1) * HD], RB[:, slot(h), :], False, False, skip_group_check=True)
                        last = mm(o, vt_[:, h * HD:(h + 1) * HD], RK[:, slot(h), :], False, True, skip_group_check=True)
                last.then_inc(sem("y_mm"), 1)

            pe.wait_ge(sem("y_evac"), 2)
            for j in range(NPAIR):
                last = mm(PS[:, 4 * 512 + j * SEQ:4 * 512 + (j + 1) * SEQ], C("blockones"), yT[:, j, :], True, True)
            last.then_inc(sem("y_sum"), 1)
            by_feature(U_SO[0], sboh, sbol, 0)
            pe.wait_ge(sem("y_sq"), 1)
            for j in range(NPAIR):
                last = mm(PS[0:NH, 6 * 512:6 * 512 + SEQ], C("gather")[:, NH * j:NH * (j + 1)], yq[:, j, :], j == 0, j == NPAIR - 1)
            last.then_inc(sem("y_ss"), 1)
            by_feature(U_SO[1], sboh, sbol, 2)
            pe.wait_ge(sem("y_rs"), 1)
            for j in range(NPAIR):
                last = mm(PS[:, 4 * 512 + j * SEQ:4 * 512 + (j + 1) * SEQ], C("spread")[0:NH, j * P:(j + 1) * P], grs[:], True, True)
            last.then_inc(sem("y_spread"), 1)
            pe.wait_ge(sem("rwo"), 1)
            for i in range(2):
                pe.wait_ge(sem("merge_a"), i + 1)
                by_feature(U_RO[i], rwoh, rwol, 2 * i)
            for i, u in enumerate(U_O):
                pe.wait_ge(sem("merged"), i // 2 + 1)
                by_token(u, mh, ml, 2 * i, 4, i == 0, i == 3)

            transpose_in("n2", xres, KD, 0)
            for i in range(FF_CHUNKS + 1):
                if i < FF_CHUNKS:
                    if i >= 2:
                        pe.wait_ge(sem("ff_out"), i - 1)
                    by_feature(U_F["g", i], xh, xl, 2 * (i % 2), None if i else "n2")
                    by_feature(U_F["u", i], xh, xl, 2 * (i % 2) + 1)
                if i:
                    pe.wait_ge(sem("ff_h"), i)
                    by_token(U_F["d", i - 1], fh[(i - 1) % 2], fl[(i - 1) % 2], 0, 4, i == 1, i == FF_CHUNKS)

            transpose_in("n3", xres, KD, 0)
            for i, u in enumerate(U_QK2):
                if i >= 2:
                    pe.wait_ge(sem("out2_evac"), i - 1)
                by_feature(u, xh, xl, i % 2, None if i else "n3")
            for i, u in enumerate(U_V2):
                by_token(u, xh, xl, 4 * i, 2, i == 0, i == 1)
            transpose_in("mem", mem, KD, 4)
            pe.wait_ge(norm_sem("mem", "xT"), nth("mem", "xT", KD))
            for i in range(NH + 2):
                if i < NH:
                    r = slice(HD * (i % 2), HD * (i % 2) + HD)
                    b = (4 + i % 2) * 512
                    if i == 0:
                        pe.wait_ge(sem("out2_evac"), 4)
                    if i >= 2:
                        pe.wait_ge(sem("d_z_read"), i - 1)
                    mm(PS[:, b:b + P], q2[r, i // 2, 0:P], k2[r, i // 2, 0:P], True, True)
                    mm(PS[:, b + P:b + 384], q2[r, i // 2, P:SEQ], k2[r, i // 2, :], True, True).then_inc(sem("d_z"), 1)
                pe.wait_ge(sem("out2_evac"), i + 3)
                if i < 6:
                    by_feature(FILL2[i], xh, xl, i % 2)
                else:
                    by_feature(FILL2[i], memh, meml, i % 2)
                if 1 <= i <= NH:
                    h = i - 1
                    pe.wait_ge(sem("d_p"), 2 * h + 2)
                    if h < 2:
                        pe.wait_ge(sem("v2_ready"), 2)
                    else:
                        pe.wait_ge(sem("d_q"), h - 1)
                    for c in range(3):
                        b = (2 + h % 2) * 512 + c * P
                        last = nc.tensor.transpose(PS[:, b:b + P], dp[h % 2][:, c * P:(c + 1) * P], C("ident"))
                    last.then_inc(sem("d_T"), 1)
                if i >= 2:
                    h = i - 2
                    pe.wait_ge(sem("d_q"), h + 1)
                    hs = slice(h * HD, (h + 1) * HD)
                    mm(bank(6)[:, hs], dq[h % 2][:, 0:P], v2[:, 0, hs], True, True)
                    mm(bank(7)[:, hs], dq[h % 2][:, P:SEQ], v2[:, 0, hs], True, False)
                    mm(bank(7)[:, hs], dq[h % 2][:, SEQ:384], v2[:, 1, hs], False, True).then_inc(sem("d_o"), 1)
            for i, u in enumerate(U_VM):
                by_token(u, memh, meml, 2 * i, 2, i == 0, i == 3)
                if i == 1:
                    pe.wait_ge(sem("c_sq"), 1)
                    pe.wait_ge(sem("out2_evac"), 14)
                    for j in range(NPAIR):
                        last = mm(PS[:, 0:SEQ], C("ones"), cv[:, 1, j, :], j == 0, j == NPAIR - 1)
                    last.then_inc(sem("c_ss"), 1)
                if i == 2:
                    transpose_in("att", att, NPAIR, 6)
            for i, u in enumerate(U_O2):
                if i < 2:
                    pe.wait_ge(norm_sem("att", "xT"), nth("att", "xT", NPAIR))
                else:
                    pe.wait_ge(sem("conv_xT"), NPAIR)
                if i == 0:
                    pe.wait_ge(sem("vm_ready"), 4)
                    pe.wait_ge(sem("c_sd"), 1)
                by_token(u, m2h, m2l, 2 * i, 0, i == 0, i == 3)

            transpose_in("n4", xres, KD, 4)
            for i, u in enumerate(U_QM):
                if i >= 2:
                    pe.wait_ge(sem("qm_evac"), i - 1)
                by_feature(u, xh, xl, i % 2, None if i else "n4")
            for i in range(MEM_HEADS + 2):
                if i < MEM_HEADS:
                    pe.wait_ge(sem("qm_evac"), min(i + 1, 4))
                    if i >= 2:
                        pe.wait_ge(sem("m_exp"), 2 * (i - 1))
                    for t in range(NT):
                        for e in range(2):
                            last = mm(PS[:, (2 + i % 2) * 512 + t * SEQ:(2 + i % 2) * 512 + (t + 1) * SEQ],
                                      qm[:, 2 * i + e, t * P:(t + 1) * P], km[:, 2 * i + e, :], e == 0, e == 1)
                    last.then_inc(sem("m_z"), 1)
                if 1 <= i <= MEM_HEADS:
                    h = i - 1
                    pe.wait_ge(sem("m_p"), h + 1)
                    if h >= 2:
                        pe.wait_ge(sem("m_q"), h - 1)
                    for mt in range(NT):
                        for t in range(NT):
                            b = (4 + h % 2) * 512 + mt * SEQ + t * P
                            last = nc.tensor.transpose(PS[:, b:b + P], mp[h % 2][:, t, mt * P:(mt + 1) * P], C("ident"))
                    last.then_inc(sem("m_T"), 1)
                if i >= 2:
                    h = i - 2
                    pe.wait_ge(sem("m_q"), h + 1)
                    if h >= 2:
                        pe.wait_ge(sem("om"), 2 * (h - 1))
                    for e in range(2):
                        for mt in range(NT):
                            last = mm(PS[:, (6 + h % 2) * 512 + e * SEQ:(6 + h % 2) * 512 + (e + 1) * SEQ],
                                      vm[:, mt, (2 * h + e) * P:(2 * h + e + 1) * P], mq[h % 2][:, mt, :], mt == 0, mt == 1)
                    last.then_inc(sem("m_o"), 1)
            for i, u in enumerate(U_OM):
                pe.wait_ge(sem("om"), 2 * (i + 1))
                by_token(u, omh, oml, 2 * i, 0, i == 0, i == 3)

            transpose_in("n5", xres, KD, 4)
            for i in range(FF2_CHUNKS + 1):
                if i < FF2_CHUNKS:
                    if i >= 4:
                        pe.wait_ge(sem("mlp_out"), i - 3)
                    by_feature(U_M["u", i], xh, xl, i % 4, None if i else "n5")
                if i:
                    pe.wait_ge(sem("mlp_h"), i)
                    by_token(U_M["d", i - 1], fh[(i - 1) % 2], fl[(i - 1) % 2], 0, 4, i == 1, i == FF2_CHUNKS)

        @block.gpsimd
        def _(pool):
            pool.wait_ge(sem("msk_loaded"), 16)
            for tt in range(NT):
                for v in range(6):
                    for g in range(2):
                        if g == 0:
                            pool.wait_ge(sem("pair_evac"), 8 * tt + 2)
                        if v == 2:
                            pool.wait_ge(sem("inv_tt"), 12 * tt + g + 1)
                            pool.wait_ge(sem("inv_T1"), 2 * tt + g + 1)
                        elif v > 2:
                            pool.wait_ge(sem("inv_g"), 10 * tt + 2 * (v - 3) + g + 1)
                        elif tt:
                            pool.wait_ge(sem("inv_g"), 10 * tt)
                        gs = slice(4 * g, 4 * g + 4)
                        nc.gpsimd.tensor_tensor(Xm[v % 2][:, gs, :], XT[:, gs, :],
                                                M(f"level{2 ** v}").unsqueeze(1).broadcast_to([P, 4, P]), ALU.mult) \
                            .then_inc(sem("xm"), 1)

        @block.scalar
        def _(act):
            chain = [0]

            def A_(o, i, f, **kw):
                return nc.scalar.activation(o, i, f, **kw)

            def link(ins):
                chain[0] += 1
                ins.then_inc(sem("act_chain"), 1)
                act.wait_ge(sem("act_chain"), chain[0])

            def hi(u):
                if u >= NU:
                    return
                act.wait_ge(raw_loaded[u % RING], 16 * (u // RING + 1))
                if u >= RING:
                    act.wait_ge(sem("units_used"), u - RING + 1)
                A_(whi[u % RING][:], raw[u % RING][:], ACT.Copy).then_inc(sem("hi_done"), 1)

            def after(u):
                hi(u + RING)
                act.wait_ge(sem("units_used"), u + 1)

            def root(st, t, width, bias):
                c = NORM[st]
                act.wait_ge(norm_sem(st, "sq"), nth(st, "sq", t + 1))
                A_(col(c + 2 + t), col(c + t), ACT.Sqrt, scale=1.0 / width, bias=bias).then_inc(norm_sem(st, "sd"), 1)

            def deviation(st, src, ready, width=D):
                c = NORM[st]
                for t in range(NT):
                    ready(t)
                    A_(junk[:, 0:width], src(t), ACT.Square, accum_out=col(c + t)).then_inc(norm_sem(st, "sq"), 1)
                    root(st, t, width, col(EPS))

            def round_T(st, g, dst, f0, nf, b):
                for f in range(nf):
                    act.wait_ge(norm_sem(st, "T"), nth(st, "T", f // 2 * 2 + 2))
                    A_(dst[:, f0 + f, :], PS[:, b * 512 + f * SEQ:b * 512 + (f + 1) * SEQ], ACT.Copy, scale=par_col(g, f)) \
                        .then_inc(norm_sem(st, "hi"), 1)

            act.dma_start(cst[:, 0:P], A["consts"][:, 0:P]).then_inc(sem("ident_loaded"), 16)
            act.dma_start(par[:], A["params"]).then_inc(sem("par_loaded"), 16)
            nc.scalar.preload_act_table_set("sqrt_and_others")
            act.wait_ge(sem("eps_set"), 1)
            deviation("n1", lambda t: xres[:, t, :], lambda t: act.wait_ge(sem(f"x_loaded{t}"), 16))
            hi(0)
            act.wait_ge(sem("par_loaded"), 16)
            round_T("n1", "norm_mix_pre", xh, 0, KD, 4)
            for u in range(1, RING):
                hi(u)
            for i, u in enumerate(U_RW):
                after(u)
                if i >= 2:
                    act.wait_ge(sem("mixed"), i - 1)
                else:
                    act.wait_ge(sem("stg_zero"), 1)
                A_(stg[i % 2][:, :, 1:SEQ + 1], bank(i % 2).rearrange("p (f t) -> p f t", f=2), ACT.Copy) \
                    .then_inc(sem("out_evac"), 1)
                if i == 1:
                    act.wait_ge(sem("mixed"), 1)
                    A_(rw[0:HD, 12, :], rw[0:HD, 12, :], ACT.Tanh)
                    A_(rw[:, 13, :], rw[:, 13, :], ACT.Sigmoid).then_inc(sem("lora_in"), 1)
                if i == 3:
                    act.wait_ge(sem("lora_out"), 1)
                    for j in range(NPAIR):
                        A_(sg[:, j, :], PS[:, 4 * 512 + j * SEQ:4 * 512 + (j + 1) * SEQ], ACT.Sigmoid, bias=par_col("w0", j))
                    for j in range(NPAIR):
                        last = A_(ag[:, j, :], PS[:, 6 * 512 + j * SEQ:6 * 512 + (j + 1) * SEQ], ACT.Sigmoid, bias=par_col("a0", j))
                    last.then_inc(sem("lora_evac"), 1)
                if i == 5:
                    act.wait_ge(sem("kk_ss"), 1)
                    A_(kq[:].rearrange("p j t -> p (j t)"), PS[:, 4 * 512:6 * 512], ACT.Sqrt).then_inc(sem("kk_sd"), 1)
            nc.scalar.preload_act_table_set("natural_log_exp_and_others")
            act.wait_ge(sem("cs"), 1)
            act.wait_ge(sem("k_mod"), 1)
            c0 = float(np.exp(-0.5))
            A_(eP[:], cs[:], ACT.Exp, scale=-c0)
            A_(eN[:], cs[:], ACT.Exp, scale=c0)
            A_(eX[:], sg[:], ACT.Exp, scale=-c0).then_inc(sem("decays"), 1)
            for i, u in enumerate(U_QK):
                after(u)
                dst = (sq, sk)[i // 2]
                A_(dst[:, 2 * (i % 2):2 * (i % 2) + 2, :], bank((i + 7) % 2).rearrange("p (f t) -> p f t", f=2), ACT.Copy,
                   scale=HD ** -0.5 if i < 2 else 1.0).then_inc(sem("out_evac"), 1)
            hi(U_V[0] + RING)
            after(U_V[1])
            for t in range(NT):
                A_(sv[:, t, :], bank(2 + t), ACT.Copy).then_inc(sem("sv_ready"), 1)
            for i in range(NH):
                b = (4 + i % 2) * 512
                s1, s2, s3, s4 = st1[i % 2], st2[i % 2], st3[i % 2], st4[i % 2]
                act.wait_ge(sem("sb_z"), i + 1)
                if i >= 2:
                    act.wait_ge(sem("sb_lf"), i - 1)
                link(A_(s1[:], PS[:, b:b + 384], ACT.Abs))
                link(A_(s1[:], s1[:], ACT.Exp, scale=-1.0))
                A_(s1[:], s1[:], ACT.Ln, bias=1.0).then_inc(sem("sb_ln"), 1)
                after(U_G[i])
                for f in range(2):
                    last = A_(gates[:, 2 * i + f, :], PS[:, ((i + 11) % 2) * 512 + f * SEQ:((i + 11) % 2) * 512 + (f + 1) * SEQ],
                              ACT.Identity, bias=par_col("b_gate", 2 * i + f))
                last.then_inc(sem("out_evac"), 1)
                act.wait_ge(sem("sb_arg_read"), i + 1)
                if i >= 2:
                    act.wait_ge(sem("sb_o"), i - 1)
                A_(s4[:], s3[:], ACT.Exp).then_inc(sem("sb_w"), 1)
            act.wait_ge(sem("sb_o"), NH)
            for j in range(2):
                A_(sboh[:, 2 * j:2 * j + 2, :], bank(6 + j).rearrange("p (f t) -> p f t", f=2), ACT.Copy).then_inc(sem("sbo_hi"), 1)
            act.wait_ge(sem("out_evac"), 19)
            A_(gates[:], gates[:], ACT.Sigmoid).then_inc(sem("gates_ready"), 1)
            for tt in range(NT):
                for q, dst in enumerate((at_, bt_, kt_, vt_)):
                    act.wait_ge(sem("tok_T"), 4 * tt + q + 1)
                    if q == 0 and tt == 0:
                        act.wait_ge(sem("units_used"), U_G[7] + 1)
                    A_(dst[:], bank(4 + q), ACT.Copy).then_inc(sem("tok_evac"), 1)
                for v in range(1, 6):
                    for g in range(2):
                        act.wait_ge(sem("inv_g"), 10 * tt + 2 * (v - 1) + g + 1)
                        A_(Gm[:, 4 * g:4 * g + 4, :], bank(g).rearrange("p (e t) -> p e t", e=4), ACT.Copy) \
                            .then_inc(sem("inv_g_evac"), 1)
                act.wait_ge(sem("av_mm"), tt + 1)
                A_(AV[:], bank(7), ACT.Copy).then_inc(sem("av_evac"), 1)
                act.wait_ge(sem("wt_mm"), tt + 1)
                A_(WT[:].rearrange("p j t -> p (j t)"), bank(6), ACT.Copy).then_inc(sem("wt_evac"), 1)
                act.wait_ge(sem("u0_mm"), tt + 1)
                A_(U0[:], bank(0), ACT.Copy).then_inc(sem("u0_evac"), 1)
                act.wait_ge(sem("y_mm"), tt + 1)
                A_(yT[:, :, tt * P:(tt + 1) * P], bank(3).rearrange("p (j t) -> p j t", j=NPAIR), ACT.Copy) \
                    .then_inc(sem("y_evac"), 1)
            act.wait_ge(sem("yc_ready"), 2)
            A_(yq[:], yc[:], ACT.Square).then_inc(sem("y_sq"), 1)
            hi(U_SO[0] + RING)
            act.wait_ge(sem("y_ss"), 1)
            A_(grs[:], PS[0:NH, 6 * 512:6 * 512 + SEQ], ACT.Sqrt, scale=1.0 / HD, bias=small[0:NH, GEPS:GEPS + 1]) \
                .then_inc(sem("y_sd"), 1)
            hi(U_SO[1] + RING)
            act.wait_ge(sem("orw"), 1)
            A_(rwoh[:], orw[:], ACT.Copy).then_inc(sem("rwo_hi"), 1)
            nc.scalar.preload_act_table_set("sqrt_and_others")
            for i, u in enumerate(U_RO):
                act.wait_ge(sem("merge_sum"), i + 1)
                A_(mh[:, 4 * i:4 * i + 4, :], gates[:, 4 * i:4 * i + 4, :], ACT.Copy).then_inc(sem("merged_hi"), 1)
                hi(u + RING)
            for u in U_O[:3]:
                hi(u + RING)

            def tile_ready(n, u, t):
                act.wait_ge(sem("units_used") if t else sem("tile_done"), u + 1 if t else n)

            def post(st, n, u, b):
                c = NORM[st]
                for t in range(NT):
                    tile_ready(n, u, t)
                    A_(junk[:, 0:512], bank(b + 2 * t), ACT.Square, accum_out=col(c + t)).then_inc(norm_sem(st, "sq"), 1)
                    act.wait_ge(norm_sem(st, "y"), nth(st, "y", 2 * t + 1))
                    link(A_(junk[:, 512:D], bank(b + 2 * t + 1), ACT.Square, accum_out=col(SQ2 + t)))
                    link(A_(col(SQ2 + t), col(SQ2 + t), ACT.Identity, scale=1.0 / D, bias=col(EPS)))
                    root(st, t, D, col(SQ2 + t))

            def pre(st, g, b):
                deviation(st, lambda t: xres[:, t, :], lambda t: act.wait_ge(norm_sem(st, "x"), nth(st, "x", t + 1)))
                round_T(st, g, xh, 0, KD, b)

            post("p1", TILE_O, U_O[3], 4)
            pre("n2", "norm_ffn_pre", 0)
            hi(U_O[3] + RING)
            for i in range(FF_CHUNKS):
                hi(U_F["g", i] + RING)
                act.wait_ge(sem("units_used"), U_F["u", i] + 1)
                if i >= 2:
                    act.wait_ge(sem("ff_out"), i - 1)
                A_(fa[i % 2][:], bank(2 * (i % 2)), ACT.Silu).then_inc(sem("ff_silu"), 1)
                if i == FF_CHUNKS - 1:
                    nc.scalar.preload_act_table_set("sqrt_and_others")
                act.wait_ge(sem("ff_out"), i + 1)
                if i >= 2:
                    act.wait_ge(sem("units_used"), U_F["d", i - 2] + 1)
                A_(fh[i % 2][:].rearrange("p f t -> p (f t)"), fb[i % 2][:], ACT.Copy).then_inc(sem("ff_hi"), 1)
                hi(U_F["u", i] + RING)
                if i:
                    hi(U_F["d", i - 1] + RING)
            post("p2", TILE_F, U_F["d", FF_CHUNKS - 1], 4)
            pre("n3", "g_mix_2", 0)
            hi(U_F["d", FF_CHUNKS - 1] + RING)
            act.wait_ge(sem("mem_loaded"), 16)
            deviation("mem", lambda t: mem[:, t, :], lambda t: None)
            for i, u in enumerate(U_QK2):
                after(u)
                dst = (q2, k2)[i // 2]
                A_(dst[:, 2 * (i % 2):2 * (i % 2) + 2, :], bank(i % 2).rearrange("p (f t) -> p f t", f=2), ACT.Copy) \
                    .then_inc(sem("out2_evac"), 1)
            hi(U_V2[0] + RING)
            after(U_V2[1])
            for t in range(NT):
                A_(v2[:, t, :], bank(2 + t), ACT.Copy).then_inc(sem("v2_ready"), 1)
            round_T("mem", "g_mem_2", memh, 0, KD, 4)
            for i in range(NH + 2):
                if i < NH:
                    if i >= 2:
                        act.wait_ge(sem("d_T"), i - 1)
                    act.wait_ge(sem("d_max"), i + 1)
                    A_(dp[i % 2][:, 0:P], dz[i % 2][:, 0:P], ACT.Exp, bias=col(DMX + i), accum_out=col(DL + i)) \
                        .then_inc(sem("d_p"), 1)
                    A_(dp[i % 2][:, P:384], dz[i % 2][:, P:384], ACT.Exp, bias=col(DMX + NH + i), accum_out=col(DL + NH + i)) \
                        .then_inc(sem("d_p"), 1)
                u = FILL2[i]
                after(u)
                dst = cv[:, i // 2, 2 * (i % 2):2 * (i % 2) + 2, :] if i < 6 else km[:, 2 * (i - 6):2 * (i - 6) + 2, :]
                A_(dst, bank(i % 2).rearrange("p (f t) -> p f t", f=2), ACT.Copy).then_inc(sem("out2_evac"), 1)
                if 1 <= i <= NH:
                    h = i - 1
                    act.wait_ge(sem("d_T"), h + 1)
                    if h >= 2:
                        act.wait_ge(sem("d_o"), h - 1)
                    A_(dq[h % 2][:], PS[:, (2 + h % 2) * 512:(2 + h % 2) * 512 + 384], ACT.Copy).then_inc(sem("d_q"), 1)
            act.wait_ge(sem("c_gated"), 1)
            A_(cv[:, 1], cv[:, 0], ACT.Square).then_inc(sem("c_sq"), 1)
            deviation("att", lambda t: att[:, t, :], lambda t: act.wait_ge(sem("att_raw"), t + 1), HW)
            for i in range(2):
                hi(U_VM[i] + RING)
            act.wait_ge(sem("c_ss"), 1)
            A_(crs[:], PS[:, 0:SEQ], ACT.Sqrt, scale=1.0 / HW, bias=col(EPS)).then_inc(sem("c_sd"), 1)
            hi(U_VM[2] + RING)
            for j in range(NPAIR):
                act.wait_ge(sem("conv_n"), j + 1)
                A_(m2h[:, 4 + j, :], cv[:, 0, j, :], ACT.Copy).then_inc(sem("conv_hi"), 1)
            round_T("att", "g_attn_out_2", m2h, 0, NPAIR, 6)
            after(U_VM[3])
            for t in range(NT):
                for c in range(2):
                    A_(vm[:, t, c * 512:(c + 1) * 512], bank(2 + 2 * t + c), ACT.Copy).then_inc(sem("vm_ready"), 1)
            nc.scalar.preload_act_table_set("sqrt_and_others")
            for u in U_O2[:3]:
                hi(u + RING)
            pre("n4", "g_xattn_2", 4)
            hi(U_O2[3] + RING)
            for i, u in enumerate(U_QM):
                after(u)
                A_(qm[:, 2 * i:2 * i + 2, :], bank(i % 2).rearrange("p (f t) -> p f t", f=2), ACT.Copy).then_inc(sem("qm_evac"), 1)
            for i in range(MEM_HEADS + 2):
                if i < MEM_HEADS:
                    act.wait_ge(sem("m_max"), i + 1)
                    if i >= 2:
                        act.wait_ge(sem("m_T"), i - 1)
                    for t in range(NT):
                        A_(mp[i % 2][:, t, :], PS[:, (2 + i % 2) * 512 + t * SEQ:(2 + i % 2) * 512 + (t + 1) * SEQ], ACT.Exp,
                           bias=col(MMX + 2 * i + t), scale=256 ** -0.5, accum_out=col(MSUM + 2 * i + t)) \
                            .then_inc(sem("m_exp"), 1)
                if 1 <= i <= MEM_HEADS:
                    h = i - 1
                    act.wait_ge(sem("m_T"), h + 1)
                    if h >= 2:
                        act.wait_ge(sem("m_o"), h - 1)
                    A_(mq[h % 2][:].rearrange("p m t -> p (m t)"), bank(4 + h % 2), ACT.Copy).then_inc(sem("m_q"), 1)
                if i >= 2:
                    h = i - 2
                    act.wait_ge(sem("m_o"), h + 1)
                    A_(omh[:, 2 * h:2 * h + 2, :], bank(6 + h % 2).rearrange("p (e t) -> p e t", e=2), ACT.Copy) \
                        .then_inc(sem("om_hi"), 1)
            nc.scalar.preload_act_table_set("sqrt_and_others")
            for u in U_OM[:3]:
                hi(u + RING)
            pre("n5", "g_mlp_2", 4)
            hi(U_OM[3] + RING)
            for i in range(FF2_CHUNKS):
                act.wait_ge(sem("units_used"), U_M["u", i] + 1)
                if i >= 2:
                    act.wait_ge(sem("mlp_sq"), i - 1)
                A_(fa[i % 2][:], bank(i % 4), ACT.Relu).then_inc(sem("mlp_out"), 1)
                act.wait_ge(sem("mlp_sq"), i + 1)
                if i >= 2:
                    act.wait_ge(sem("units_used"), U_M["d", i - 2] + 1)
                A_(fh[i % 2][:].rearrange("p f t -> p (f t)"), fb[i % 2][:], ACT.Copy).then_inc(sem("mlp_hi"), 1)
                hi(U_M["u", i] + RING)
                if i:
                    hi(U_M["d", i - 1] + RING)
            deviation("fin", lambda t: xres[:, t, :], lambda t: act.wait_ge(norm_sem("fin", "x"), nth("fin", "x", t + 1)))

        @block.vector
        def _(dve):
            V = nc.vector
            chain = [0]

            def link(ins):
                chain[0] += 1
                ins.then_inc(sem("dve_chain"), 1)
                dve.wait_ge(sem("dve_chain"), chain[0])

            def lo(u):
                if u >= NU:
                    return
                dve.wait_ge(sem("hi_done"), u + 1)
                V.tensor_tensor(wlo[u % RING][:], raw[u % RING][:], whi[u % RING][:].bitcast(f32), ALU.subtract) \
                    .then_inc(sem("unit_split"), 1)

            def diagonal(st):
                c = NORM[st]
                for t in range(NT):
                    dve.wait_ge(norm_sem(st, "sd"), nth(st, "sd", t + 1))
                    link(V.reciprocal(col(c + 4 + t), col(c + 2 + t)))
                    V.tensor_scalar(dg[st][:, t, :], C("ident"), col(c + 4 + t), None, ALU.mult).then_inc(norm_sem(st, "dg"), 1)

            def rest_T(st, g, hi_, lo_, f0, nf, b):
                for f in range(nf):
                    dve.wait_ge(norm_sem(st, "hi"), nth(st, "hi", f // 2 * 2 + 2))
                    V.scalar_tensor_tensor(out=lo_[:, f0 + f, :], in0=PS[:, b * 512 + f * SEQ:b * 512 + (f + 1) * SEQ],
                                           scalar=par_col(g, f), in1=hi_[:, f0 + f, :].bitcast(f32),
                                           op0=ALU.mult, op1=ALU.subtract).then_inc(norm_sem(st, "xT"), 1)

            V.memset(col(EPS), 1e-6)
            V.memset(col(GEPS), HD * 1e-5).then_inc(sem("eps_set"), 1)
            dve.wait_ge(sem("ident_loaded"), 16)
            diagonal("n1")
            lo(0)
            dve.wait_ge(sem("par_loaded"), 16)
            rest_T("n1", "norm_mix_pre", xh, xl, 0, KD, 4)
            for u in range(1, RING):
                lo(u)
            for i in range(2):
                last = V.memset(stg[i][:, :, 0:1], 0.0)
            last.then_inc(sem("stg_zero"), 1)
            for i, u in enumerate(U_RW):
                lo(u + RING)
                dve.wait_ge(sem("out_evac"), i + 1)
                s = stg[i % 2]
                if i:
                    dve.wait_ge(sem("mixed"), i)
                link(V.tensor_tensor(diff[:], s[:, :, 0:SEQ], s[:, :, 1:SEQ + 1], ALU.subtract))
                for f in range(2):
                    r = RW_TILE[i] + f
                    last = V.scalar_tensor_tensor(out=rw[:, r, :], in0=diff[:, f, :], scalar=par_col("mu_rw", r),
                                                  in1=s[:, f, 1:SEQ + 1], op0=ALU.mult, op1=ALU.add)
                last.then_inc(sem("mixed"), 1)
                if i == 2:
                    dve.wait_ge(sem("mixed"), 3)
                    for j in range(NPAIR):
                        last = V.tensor_scalar(kk[:, j, :], rw[:, 4 + j, :], par_col("k_k", j), None, ALU.mult)
                    link(last)
                    V.tensor_tensor(kq[:], kk[:], kk[:], ALU.mult).then_inc(sem("kk_sq"), 1)
                if i == 4:
                    dve.wait_ge(sem("lora_evac"), 1)
                    dve.wait_ge(sem("msk_loaded"), 16)
                    for j in range(NPAIR):
                        last = V.tensor_tensor_scan(cs[:, j, :], M("reset"), sg[:, j, :], 0.0, ALU.mult, ALU.add)
                    link(last)
                    V.tensor_tensor(sg[:], cs[:], sg[:], ALU.subtract).then_inc(sem("cs"), 1)
                if i == 5:
                    for j in range(NPAIR):
                        link(V.tensor_scalar(eP[:, j, :], ag[:, j, :], 1.0, par_col("k_a", j), ALU.subtract, ALU.mult))
                        last = V.scalar_tensor_tensor(out=rw[:, 4 + j, :], in0=eP[:, j, :], scalar=1.0, in1=rw[:, 4 + j, :],
                                                      op0=ALU.add, op1=ALU.mult)
                    last.then_inc(sem("k_mod"), 1)
                if i == 6:
                    dve.wait_ge(sem("k_mod"), 1)
                    for j in range(NPAIR):
                        last = V.scalar_tensor_tensor(out=rkk[:, j, :], in0=rw[:, j, :], scalar=par_col("r_k", j),
                                                      in1=rw[:, 4 + j, :], op0=ALU.mult, op1=ALU.mult)
                    last.then_inc(sem("rkk"), 1)
            dve.wait_ge(sem("kk_sd"), 1)
            lo(U_QK[0] + RING)
            link(V.tensor_scalar(kq[:], kq[:], 1e-12, None, ALU.max))
            link(V.reciprocal(kq[:], kq[:]))
            link(V.tensor_tensor(kk[:], kk[:], kq[:], ALU.mult))
            lo(U_QK[1] + RING)
            dve.wait_ge(sem("decays"), 1)
            V.tensor_copy(dec[:], eP[:].rearrange("p j (g c) -> p j g c", c=CHUNK)[:, :, :, CHUNK - 1])
            link(V.scalar_tensor_tensor(out=eX[:].rearrange("p j t -> p (j t)"), in0=kk[:].rearrange("p j t -> p (j t)"), scalar=-1.0,
                                        in1=eX[:].rearrange("p j t -> p (j t)"), op0=ALU.mult, op1=ALU.mult))
            link(V.tensor_tensor(kk[:], kk[:], ag[:], ALU.mult))
            lo(U_QK[2] + RING)
            link(V.tensor_tensor(kk[:], kk[:], eN[:], ALU.mult))
            dve.wait_ge(sem("mixed"), 7)
            V.tensor_tensor(eN[:], rw[:, 4:8, :], eN[:], ALU.mult)
            V.tensor_tensor(eP[:], rw[:, 0:4, :], eP[:], ALU.mult).then_inc(sem("rw_pre"), 1)
            lo(U_QK[3] + RING)
            lo(U_V[0] + RING)
            dve.wait_ge(sem("bonus_mm"), 1)
            dve.wait_ge(sem("rw_pre"), 1)
            for j in range(NPAIR):
                V.tensor_scalar(rw[:, j, :], PS[:, 4 * 512 + j * SEQ:4 * 512 + (j + 1) * SEQ], par_col("lnx_w", j), None, ALU.mult)
            for j in range(2):
                last = V.tensor_tensor(bon[:, 2 * j:2 * j + 2, :], bank(6 + j).rearrange("p (j t) -> p j t", j=2),
                                       rw[:, 8 + 2 * j:10 + 2 * j, :], ALU.mult)
            link(last)
            for j in range(NPAIR):
                last = V.scalar_tensor_tensor(out=rw[:, 4 + j, :], in0=bon[:, j, :], scalar=par_col("lnx_b", j),
                                              in1=PS[:, 4 * 512 + j * SEQ:4 * 512 + (j + 1) * SEQ], op0=ALU.add, op1=ALU.mult)
            last.then_inc(sem("gn_pre"), 1)
            lo(U_V[1] + RING)
            for i in range(NH):
                b = (4 + i % 2) * 512
                s1, s2, s3 = st1[i % 2], st2[i % 2], st3[i % 2]
                dve.wait_ge(sem("sb_ln"), i + 1)
                if i >= 2:
                    dve.wait_ge(sem("sb_arg"), i - 1)
                link(V.scalar_tensor_tensor(out=s2[:], in0=PS[:, b:b + 384], scalar=0.0, in1=s1[:], op0=ALU.max, op1=ALU.add))
                V.tensor_tensor(s2[:], s2[:], M("sb_neg"), ALU.mult).then_inc(sem("sb_lf"), 1)
                lo(U_G[i] + RING)
                dve.wait_ge(sem("sb_arg"), i + 1)
                if i >= 2:
                    dve.wait_ge(sem("sb_w"), i - 1)
                V.scalar_tensor_tensor(out=s3[:], in0=PS[:, b:b + 384], scalar=0.0, in1=C("sb_add"), op0=ALU.min, op1=ALU.add) \
                    .then_inc(sem("sb_arg_read"), 1)
            for j in range(2):
                dve.wait_ge(sem("sbo_hi"), j + 1)
                V.tensor_tensor(sbol[:, 2 * j:2 * j + 2, :], bank(6 + j).rearrange("p (f t) -> p f t", f=2),
                                sboh[:, 2 * j:2 * j + 2, :].bitcast(f32), ALU.subtract).then_inc(sem("sb_evac"), 2)

            def mask4(ap):
                return ap.unsqueeze(1).broadcast_to([P, 4, P])

            V.memset(St[:, 0], 0.0).then_inc(sem("state"), 1)
            for tt in range(NT):
                for q, (dst, m) in enumerate(((XT, "strict"), (AK, "strict"), (RB, "incl"), (RK, "incl"))):
                    for g in range(2):
                        dve.wait_ge(sem("pair_mm"), 8 * tt + 2 * q + g + 1)
                        if q == 0 and tt:
                            dve.wait_ge(sem("xm"), 12 * tt)
                        V.tensor_tensor(dst[:, 4 * g:4 * g + 4, :], bank(2 * q + g).rearrange("p (e t) -> p e t", e=4), mask4(M(m)),
                                        ALU.mult).then_inc(sem("pair_evac"), 1)
                        if q == 1 and g == 1:
                            for gg in range(2):
                                gs = slice(4 * gg, 4 * gg + 4)
                                dve.wait_ge(sem("xm"), 12 * tt + gg + 1)
                                V.tensor_tensor(TT[:, gs, :], Xm[0][:, gs, :], mask4(C("ident")), ALU.add).then_inc(sem("inv_tt"), 1)
                            for gg in range(2):
                                gs = slice(4 * gg, 4 * gg + 4)
                                dve.wait_ge(sem("inv_T1"), 2 * tt + gg + 1)
                                V.tensor_tensor(Tm[:, gs, :], bank(gg).rearrange("p (e t) -> p e t", e=4), mask4(C("ident")), ALU.add) \
                                    .then_inc(sem("inv_t"), 1)
                for v in range(1, 6):
                    for g in range(2):
                        gs = slice(4 * g, 4 * g + 4)
                        dve.wait_ge(sem("inv_up"), 10 * tt + 2 * (v - 1) + g + 1)
                        if v < 5:
                            part = halves(Tm[:, gs, :].rearrange("p e t -> p (e t)"), v, 0)
                            V.tensor_tensor(part, part, bank(2 + g)[:, 0:4 * HD].rearrange("p (a b) -> p a b", b=2 ** v), ALU.add) \
                                .then_inc(sem("inv_t"), 1)
                        part = halves(TT[:, gs, :].rearrange("p e t -> p (e t)"), v, 1)
                        V.tensor_tensor(part, part, bank(4 + g)[:, 0:4 * HD].rearrange("p (a b) -> p a b", b=2 ** v), ALU.add) \
                            .then_inc(sem("inv_tt"), 1)
                for c in range(2):
                    g = 2 * tt + c
                    r = slice(CHUNK * c, CHUNK * c + CHUNK)
                    dve.wait_ge(sem("u_mm"), g + 1)
                    dve.wait_ge(sem("u0_evac"), tt + 1)
                    V.tensor_tensor(Uc[r, :], PS[r, 512:1024], U0[r, :], ALU.add).then_inc(sem("u_ready"), 1)
                    if g < 3:
                        dve.wait_ge(sem("ds_mm"), g + 1)
                        link(V.tensor_tensor(dS[:], bank(2).rearrange("p (j t) -> p j t", j=NPAIR), St[:, g], ALU.add))
                        for j in range(NPAIR):
                            last = V.scalar_tensor_tensor(out=St[:, g + 1, j, :], in0=dS[:, j, :], scalar=dec[:, j, g:g + 1],
                                                          in1=C("blockones"), op0=ALU.mult, op1=ALU.mult)
                        last.then_inc(sem("state"), 1)
            dve.wait_ge(sem("y_sum"), 1)
            for j in range(2):
                V.scalar_tensor_tensor(out=yc[:, 2 * j:2 * j + 2, :].rearrange("p j t -> p (j t)"), in0=bank(4 + j), scalar=-1.0 / HD,
                                       in1=yT[:, 2 * j:2 * j + 2, :].rearrange("p j t -> p (j t)"), op0=ALU.mult, op1=ALU.add) \
                    .then_inc(sem("yc_ready"), 1)
            lo(U_SO[0] + RING)
            dve.wait_ge(sem("gates_ready"), 1)

            def gate(i, u, base):
                dve.wait_ge(sem("units_used"), u + 1)
                for c in range(2):
                    g = gates[:, base + 4 * i + 2 * c:base + 4 * i + 2 * c + 2, :].rearrange("p f t -> p (f t)")
                    last = V.tensor_tensor(g, bank(2 * i + c), g, ALU.mult)
                return last

            dve.wait_ge(sem("y_sd"), 1)
            V.reciprocal(grs[:], grs[:]).then_inc(sem("y_rs"), 1)
            lo(U_SO[1] + RING)
            gate(0, U_SO[0], 0).then_inc(sem("merge_a"), 1)
            dve.wait_ge(sem("y_spread"), 1)
            link(V.tensor_tensor(yc[:].rearrange("p j t -> p (j t)"), yc[:].rearrange("p j t -> p (j t)"), PS[:, 4 * 512:6 * 512],
                                 ALU.mult))
            link(V.tensor_tensor(yc[:], yc[:], rw[:, 0:4, :], ALU.mult))
            V.tensor_tensor(orw[:], yc[:], rw[:, 4:8, :], ALU.add).then_inc(sem("orw"), 1)
            gate(1, U_SO[1], 0).then_inc(sem("merge_a"), 1)
            dve.wait_ge(sem("rwo_hi"), 1)
            V.tensor_tensor(rwol[:], orw[:], rwoh[:].bitcast(f32), ALU.subtract).then_inc(sem("rwo"), 1)
            for i, u in enumerate(U_RO):
                link(gate(i, u, 8))
                V.tensor_tensor(gates[:, 4 * i:4 * i + 4, :], gates[:, 4 * i:4 * i + 4, :], gates[:, 8 + 4 * i:12 + 4 * i, :], ALU.add) \
                    .then_inc(sem("merge_sum"), 1)
                lo(u + RING)
                dve.wait_ge(sem("merged_hi"), i + 1)
                V.tensor_tensor(ml[:, 4 * i:4 * i + 4, :], gates[:, 4 * i:4 * i + 4, :], mh[:, 4 * i:4 * i + 4, :].bitcast(f32),
                                ALU.subtract).then_inc(sem("merged"), 1)
            for u in U_O[:2]:
                lo(u + RING)

            def tile_ready(n, u, t):
                dve.wait_ge(sem("units_used") if t else sem("tile_done"), u + 1 if t else n)

            def post(st, n, u, gain, loaded, b, then):
                c = NORM[st]
                dve.wait_ge(sem(loaded), 16)
                dve.wait_ge(sem("x_loaded0"), 32)
                for t in range(NT):
                    tile_ready(n, u, t)
                    V.tensor_tensor(tmp[:, t, 512:D], bank(b + 2 * t + 1), gain[:, 512:D], ALU.mult).then_inc(norm_sem(st, "y"), 1)
                    dve.wait_ge(norm_sem(st, "sq"), nth(st, "sq", t + 1))
                    V.tensor_tensor(tmp[:, t, 0:512], bank(b + 2 * t), gain[:, 0:512], ALU.mult).then_inc(norm_sem(st, "y"), 1)
                    dve.wait_ge(norm_sem(st, "sd"), nth(st, "sd", t + 1))
                    link(V.reciprocal(col(c + 4 + t), col(c + 2 + t)))
                    dve.wait_ge(norm_sem(st, "y"), nth(st, "y", 2 * t + 2))
                    V.scalar_tensor_tensor(out=xres[:, t, :], in0=tmp[:, t, :], scalar=col(c + 4 + t), in1=xres[:, t, :],
                                           op0=ALU.mult, op1=ALU.add).then_inc(norm_sem(then, "x"), 1)

            def residual(n, u, b, then):
                for t in range(NT):
                    tile_ready(n, u, t)
                    V.tensor_tensor(xres[:, t, :], xres[:, t, :], PS[:, b * 512 + t * D:b * 512 + (t + 1) * D], ALU.add) \
                        .then_inc(norm_sem(then, "x"), 1)

            def pre(st, g, b, u):
                diagonal(st)
                if u != U_F["d", FF_CHUNKS - 1]:
                    lo(u - 1 + RING)
                rest_T(st, g, xh, xl, 0, KD, b)
                lo(u + RING)

            post("p1", TILE_O, U_O[3], gmix, "gmix_loaded", 4, "n2")
            pre("n2", "norm_ffn_pre", 0, U_O[3])
            for i in range(FF_CHUNKS):
                lo(U_F["g", i] + RING)
                dve.wait_ge(sem("ff_silu"), i + 1)
                if i >= 2:
                    dve.wait_ge(sem("ff_hi"), i - 1)
                V.tensor_tensor(fb[i % 2][:], fa[i % 2][:], bank(2 * (i % 2) + 1), ALU.mult).then_inc(sem("ff_out"), 1)
                dve.wait_ge(sem("ff_hi"), i + 1)
                V.tensor_tensor(fl[i % 2][:].rearrange("p f t -> p (f t)"), fb[i % 2][:],
                                fh[i % 2][:].rearrange("p f t -> p (f t)").bitcast(f32), ALU.subtract).then_inc(sem("ff_h"), 1)
                lo(U_F["u", i] + RING)
                if i:
                    lo(U_F["d", i - 1] + RING)
            post("p2", TILE_F, U_F["d", FF_CHUNKS - 1], gffn, "gffn_loaded", 4, "n3")
            pre("n3", "g_mix_2", 0, U_F["d", FF_CHUNKS - 1])
            diagonal("mem")
            for u in U_QK2 + U_V2:
                lo(u + RING)
            rest_T("mem", "g_mem_2", memh, meml, 0, KD, 4)
            for i in range(NH + 2):
                if i < NH:
                    b = (4 + i % 2) * 512
                    z = dz[i % 2]
                    dve.wait_ge(sem("d_z"), i + 1)
                    if i >= 2:
                        dve.wait_ge(sem("d_p"), 2 * (i - 1))
                    V.scalar_tensor_tensor(out=z[:], in0=PS[:, b:b + 384], scalar=HD ** -0.5, in1=C("dil"), op0=ALU.mult, op1=ALU.add) \
                        .then_inc(sem("d_z_read"), 1)
                    dve.wait_ge(sem("d_z_read"), i + 1)
                    V.tensor_reduce(out=col(DMX + i), in_=z[:, 0:P], axis=AX.X, op=ALU.max, negate=True)
                    V.tensor_reduce(out=col(DMX + NH + i), in_=z[:, P:384], axis=AX.X, op=ALU.max, negate=True) \
                        .then_inc(sem("d_max"), 1)
                lo(FILL2[i] + RING)
                if i == 6:
                    dve.wait_ge(sem("out2_evac"), 10)
                    link(V.tensor_tensor(cv[:, 1], cv[:, 1], cv[:, 2], ALU.mult))
                    for j in range(NPAIR):
                        last = V.tensor_scalar(cv[:, 2, j, :], cv[:, 1, j, :], par_col("conv_w_2", 8 + j), None, ALU.mult)
                    link(last)
                    for tap in (1, 0):
                        sh = 2 - tap
                        for j in range(NPAIR):
                            last = V.scalar_tensor_tensor(out=cv[:, 2, j, sh:SEQ], in0=cv[:, 1, j, 0:SEQ - sh],
                                                          scalar=par_col("conv_w_2", 4 * tap + j), in1=cv[:, 2, j, sh:SEQ],
                                                          op0=ALU.mult, op1=ALU.add)
                        link(last)
                    V.tensor_tensor(cv[:, 0], cv[:, 0], cv[:, 2], ALU.mult).then_inc(sem("c_gated"), 1)
            dve.wait_ge(sem("d_o"), NH)
            dve.wait_ge(sem("d_p"), 2 * NH)
            link(V.reciprocal(col(DRL, 16), col(DL, 16)))
            for t in range(NT):
                V.tensor_tensor(att[:, t, :].rearrange("p (h e) -> p h e", h=NH), bank(6 + t).rearrange("p (h e) -> p h e", h=NH),
                                col(DRL + NH * t, NH).unsqueeze(2).broadcast_to([P, NH, HD]), ALU.mult).then_inc(sem("att_raw"), 1)
            diagonal("att")
            for i in range(2):
                lo(U_VM[i] + RING)
            dve.wait_ge(sem("c_sd"), 1)
            link(V.reciprocal(crs[:], crs[:]))
            lo(U_VM[2] + RING)
            for j in range(NPAIR):
                V.scalar_tensor_tensor(out=cv[:, 0, j, :], in0=cv[:, 0, j, :], scalar=par_col("g_conv_out_2", j), in1=crs[:],
                                       op0=ALU.mult, op1=ALU.mult).then_inc(sem("conv_n"), 1)
            for j in range(NPAIR):
                dve.wait_ge(sem("conv_hi"), j + 1)
                V.tensor_tensor(m2l[:, 4 + j, :], cv[:, 0, j, :], m2h[:, 4 + j, :].bitcast(f32), ALU.subtract) \
                    .then_inc(sem("conv_xT"), 1)
            rest_T("att", "g_attn_out_2", m2h, m2l, 0, NPAIR, 6)
            lo(U_VM[3] + RING)
            for u in U_O2[:2]:
                lo(u + RING)
            residual(TILE_O2, U_O2[3], 0, "n4")
            pre("n4", "g_xattn_2", 4, U_O2[3])
            for u in U_QM:
                lo(u + RING)
            for i in range(MEM_HEADS + 2):
                if i < MEM_HEADS:
                    dve.wait_ge(sem("m_z"), i + 1)
                    link(V.tensor_reduce(out=col(MMX + 2 * i, 2), in_=bank(2 + i % 2).rearrange("p (t m) -> p t m", t=2), axis=AX.X,
                                         op=ALU.max, negate=True))
                    V.tensor_scalar(col(MMX + 2 * i, 2), col(MMX + 2 * i, 2), 256 ** -0.5, None, ALU.mult).then_inc(sem("m_max"), 1)
                    dve.wait_ge(sem("m_exp"), 2 * i + 2)
                    link(V.reciprocal(col(MSUM + 2 * i, 2), col(MSUM + 2 * i, 2)))
                    for t in range(NT):
                        last = V.tensor_scalar(mp[i % 2][:, t, :], mp[i % 2][:, t, :], col(MSUM + 2 * i + t), None, ALU.mult)
                    last.then_inc(sem("m_p"), 1)
                if i >= 2:
                    h = i - 2
                    dve.wait_ge(sem("om_hi"), h + 1)
                    V.tensor_tensor(oml[:, 2 * h:2 * h + 2, :], bank(6 + h % 2).rearrange("p (e t) -> p e t", e=2),
                                    omh[:, 2 * h:2 * h + 2, :].bitcast(f32), ALU.subtract).then_inc(sem("om"), 2)
            for u in U_OM[:2]:
                lo(u + RING)
            residual(TILE_OM, U_OM[3], 0, "n5")
            pre("n5", "g_mlp_2", 4, U_OM[3])
            for i in range(FF2_CHUNKS):
                dve.wait_ge(sem("mlp_out"), i + 1)
                if i >= 2:
                    dve.wait_ge(sem("mlp_hi"), i - 1)
                V.tensor_tensor(fb[i % 2][:], fa[i % 2][:], fa[i % 2][:], ALU.mult).then_inc(sem("mlp_sq"), 1)
                dve.wait_ge(sem("mlp_hi"), i + 1)
                V.tensor_tensor(fl[i % 2][:].rearrange("p f t -> p (f t)"), fb[i % 2][:],
                                fh[i % 2][:].rearrange("p f t -> p (f t)").bitcast(f32), ALU.subtract).then_inc(sem("mlp_h"), 1)
                lo(U_M["u", i] + RING)
                if i:
                    lo(U_M["d", i - 1] + RING)
            residual(TILE_M, U_M["d", FF2_CHUNKS - 1], 4, "fin")
            c = NORM["fin"]
            dve.wait_ge(sem("gfin_loaded"), 16)
            for t in range(NT):
                dve.wait_ge(norm_sem("fin", "sd"), nth("fin", "sd", t + 1))
                link(V.reciprocal(col(c + 4 + t), col(c + 2 + t)))
                V.scalar_tensor_tensor(out=xn[:, t, :], in0=xres[:, t, :], scalar=col(c + 4 + t), in1=gfin[:],
                                       op0=ALU.mult, op1=ALU.mult).then_inc(sem("result"), 1)


_INS = ["x", "w_in", "w_up", "a_up", "g_up", "w_sb_out", "w_rw_out", "w_o", "norm_mix_post", "w_ffn_gate", "w_ffn_up",
        "w_ffn_down", "norm_ffn_post", "mem_2", "w_in_2", "w_out_2", "w_q_mem_2", "w_kv_mem_2", "w_o_mem_2", "w_up_2",
        "w_down_2", "g_final_2"]


def kernel(**inputs):
    import numpy as _np
    import concourse.bacc as _bacc
    from concourse import mybir as _mybir
    from concourse.bass_utils import run_bass_kernel_spmd as _run

    nc = _bacc.Bacc("TRN2", target_bir_lowering=False, num_devices=1)
    arrays, A = {}, {}
    given = {n: _np.ascontiguousarray(inputs[n]) for n in _INS}
    rows = [_np.ascontiguousarray(inputs[n]).reshape(k, P) for n, k in PARAM_ROWS]
    given["params"] = _np.ascontiguousarray(_np.concatenate(rows, 0).T)
    given["consts"], given["masks"] = CONSTS, MASKS
    for name, a in given.items():
        arrays[f"in_{name}_dram"] = a
        A[name] = nc.dram_tensor(f"in_{name}_dram", a.shape, _mybir.dt.from_np(a.dtype), kind="ExternalInput").ap()
    out = nc.dram_tensor("out_0_dram", (1, SEQ, D), _mybir.dt.float32, kind="ExternalOutput").ap()
    block_kernel(nc, A, out)
    r = _run(nc, [arrays], core_ids=[0])
    return r.results[0]["out_0_dram"]
```

```python
import concourse.bass as bass
from concourse import mybir
from contextlib import ExitStack
import numpy as np

P = 128
SEQ = 256
NT = SEQ // P
D = 1024
KD = D // P
HW = 512
NPAIR = HW // P
HD = 64
NH = HW // HD
CHUNK = 64
RW0 = 3 * HW
GATE0 = RW0 + 3 * HW + 256
DFF = ((8 * D + 3 * 256 - 1) // (3 * 256)) * 256
DFF2 = 4 * D
FF_CHUNKS = DFF // 256
FF2_CHUNKS = DFF2 // 256
MEM_HEADS = 4
RING = 3
UNIT = 2048

PARAM_ROWS = [("norm_mix_pre", 8), ("b_gate", 16), ("mu_rw", 14), ("w0", 4), ("a0", 4), ("k_k", 4),
              ("k_a", 4), ("r_k", 4), ("lnx_w", 4), ("lnx_b", 4), ("norm_ffn_pre", 8), ("conv_w_2", 12),
              ("g_conv_out_2", 4), ("g_attn_out_2", 4), ("g_mix_2", 8), ("g_xattn_2", 8), ("g_mem_2", 8),
              ("g_mlp_2", 8)]
PCOL = {}
_at = 0
for _n, _k in PARAM_ROWS:
    PCOL[_n] = _at
    _at += _k
NPARAM = _at


def shape_constants():
    i = np.arange(P)[:, None]
    j = np.arange(P)[None, :]
    t = np.arange(SEQ)[None, :]
    parts, cols = {"f32": [], "f16": []}, {}

    def put(name, a, kind="f32"):
        at = sum(x.shape[1] for x in parts[kind])
        a = np.broadcast_to(a, (P, a.shape[1]))
        cols[name] = (at, at + a.shape[1])
        parts[kind].append(a)

    same = (i // CHUNK) == (j // CHUNK)
    put("ident", (i == j) * 1.0)
    put("tri", (i >= j) * 1.0)
    put("ones", np.ones((P, P)))
    put("blockones", same * 1.0)
    put("incl", (same & (i <= j)) * 1.0, "f16")
    put("strict", (same & (i < j)) * 1.0, "f16")
    for m in (1, 2, 4, 8, 16, 32):
        two = (i // (2 * m)) == (j // (2 * m))
        put(f"level{m}", (two & (i % (2 * m) < m) & (j % (2 * m) >= m)) * 1.0, "f16")
    ks = np.concatenate([(i < t), (i + P < t[:, P:])], 1)
    put("sb_neg", ks * -1.0, "f16")
    put("sb_add", np.where(ks, 0.0, -1e30))

    def count(q, s):
        d = q - s
        c = ((d >= 0) & (d <= 128)) * 1 + ((d >= 0) & (d % 4 == 0)) * 1 + ((d >= 0) & (d % 16 == 0)) * 1
        return np.where(c > 0, np.log(np.maximum(c, 1)), -1e30)

    put("dil", np.concatenate([count(i, j), count(i + P, t)], 1))
    put("reset", (t % CHUNK != 0) * 1.0, "f16")
    put("gather", np.concatenate([np.arange(NH)[None, :] == 2 * f + i // HD for f in range(NPAIR)], 1) * 1.0)
    put("spread", (i == np.arange(HW)[None, :] // HD) * 1.0)
    return (np.concatenate(parts["f32"], 1).astype(np.float32), np.concatenate(parts["f16"], 1).astype(np.float16), cols)


CONSTS, MASKS, CCOL = shape_constants()
NCONST, NMASK = CONSTS.shape[1], MASKS.shape[1]


def block_kernel(nc, A, out, dbg=None):
    f32 = mybir.dt.float32
    f32r = mybir.dt.float32r
    ALU = mybir.AluOpType
    ACT = mybir.ActivationFunctionType
    AX = mybir.AxisListType
    KB = 1024
    BASE = 16512

    ctx = ExitStack()
    with ctx:
        def at(name, kb, shape, dt=f32):
            return nc.alloc_sbuf_tensor_at(name, shape, dt, offset=BASE + int(kb * KB))

        sems = {}

        def sem(name):
            if name not in sems:
                sems[name] = ctx.enter_context(nc.semaphore(name))
            return sems[name]

        raw = [at(f"raw{i}", 8 * i, [P, UNIT]) for i in range(RING)]
        whi = [at(f"whi{i}", 24 + 16 * i, [P, UNIT], f32r) for i in range(RING)]
        wlo = [at(f"wlo{i}", 32 + 16 * i, [P, UNIT], f32r) for i in range(RING)]
        cst = at("cst", 72, [P, NCONST])
        msk = at("msk", 80, [P, NMASK], mybir.dt.float16)
        par = at("par", 84, [P, NPARAM])
        small = at("small", 84.5, [P, 128])
        XR = 85
        xres = at("xres", XR, [P, NT, D])
        A0 = 93
        xh = at("xh", A0, [P, KD, SEQ], f32r)
        xl = at("xl", A0 + 8, [P, KD, SEQ], f32r)
        W = 109
        gates = at("gates", W, [P, 16, SEQ])
        sboh = at("sboh", W + 16, [P, NPAIR, SEQ], f32r)
        sbol = at("sbol", W + 20, [P, NPAIR, SEQ], f32r)
        xn = at("xn", W + 24, [P, NT, D])
        rw = at("rw", W + 24, [P, 14, SEQ])
        eP = at("eP", W + 38, [P, NPAIR, SEQ])
        eN = at("eN", W + 42, [P, NPAIR, SEQ])
        eX = at("eX", W + 46, [P, NPAIR, SEQ])
        kk = at("kk", W + 50, [P, NPAIR, SEQ])
        sg = at("sg", W + 54, [P, NPAIR, SEQ])
        cs = at("cs", W + 58, [P, NPAIR, SEQ])
        ag = at("ag", W + 62, [P, NPAIR, SEQ])
        kq = at("kq", W + 66, [P, NPAIR, SEQ])
        krs = at("krs", W + 94, [NH, SEQ])
        sq = at("sq", W + 70, [P, NPAIR, SEQ])
        sk = at("sk", W + 74, [P, NPAIR, SEQ])
        sv = at("sv", W + 78, [P, NT, HW])
        st1 = [at(f"st1{i}", W + 82 + 6 * i, [P, 384]) for i in range(2)]
        st2 = [at(f"st2{i}", W + 83.5 + 6 * i, [P, 384]) for i in range(2)]
        st3 = [at(f"st3{i}", W + 85 + 6 * i, [P, 384]) for i in range(2)]
        st4 = [at(f"st4{i}", W + 86.5 + 6 * i, [P, 384]) for i in range(2)]
        lora = at("lora", W + 94, [P, HW])
        gup = at("gup", W + 96, [P, HW])
        stg = [at(f"stg{i}", XR + 2.0625 * i, [P, 2, SEQ + 1]) for i in range(2)]
        diff = at("diff", XR + 4.25, [P, 2, SEQ])
        Tm = at("Tm", W + 54, [P, NH, P])
        TT = at("TT", W + 58, [P, NH, P])
        Gm = [at("Gm0", W + 62, [P, NH, P]), at("Gm1", A0 + 10, [P, NH, P])]
        Xm = [at("Xm0", W + 66, [P, NH, P]), at("Xm1", W + 94, [P, NH, P])]
        XT = at("XT", W + 70, [P, NH, P])
        AK = at("AK", W + 74, [P, NH, P])
        RB = at("RB", W + 78, [P, NH, P])
        RK = at("RK", W + 82, [P, NH, P])
        St = at("St", W + 86, [P, 4, NPAIR, P])
        yT = at("yT", XR, [P, NPAIR, SEQ])
        dS = at("dS", XR + 4, [P, NPAIR, P])
        at_ = at("a_tok", A0, [P, HW])
        bt_ = at("b_tok", A0 + 2, [P, HW])
        kt_ = at("k_tok", A0 + 4, [P, HW])
        vt_ = at("v_tok", A0 + 6, [P, HW])
        WT = at("WT", A0 + 8, [P, NPAIR, P])
        AV = at("AV", A0 + 10, [P, HW])
        U0 = at("U0", A0 + 12, [P, HW])
        Uc = at("Uc", A0 + 14, [P, HW])
        yc = at("yc", W + 46, [P, NPAIR, SEQ])
        yq = at("yq", W + 42, [P, NPAIR, P])
        bon = at("bon", XR, [P, NPAIR, SEQ])
        rkk = at("rkk", W + 78, [P, NPAIR, SEQ])
        grs = at("grs", W + 36, [NH, SEQ])
        rwoh = at("rwoh", W + 32, [P, NPAIR, SEQ], f32r)
        rwol = at("rwol", W + 50, [P, NPAIR, SEQ], f32r)
        mh = at("mh", A0, [P, KD, SEQ], f32r)
        ml = at("ml", A0 + 8, [P, KD, SEQ], f32r)
        gmix = at("gmix", W + 38, [P, D])
        gffn = at("gffn", W + 42, [P, D])
        gfin = at("gfin", W + 46, [P, D])
        tmp = at("tmp", W + 16, [P, NT, D])
        junk = at("junk", W + 54, [P, D])
        dg_ = at("dg", W + 24, [P, NT, P])
        dg = {n: dg_ for n in ("n1", "n2", "n3", "n4", "n5")}
        dg["mem"] = at("dg_mem", W + 25, [P, NT, P])
        dg["att"] = at("dg_att", W + 50, [P, NT, P])
        fa = [at(f"fa{i}", W + 0 + 2 * i, [P, 2 * SEQ]) for i in range(2)]
        fb = [at(f"fb{i}", W + 4 + 2 * i, [P, 2 * SEQ]) for i in range(2)]
        fh = [at(f"fh{i}", W + 8 + 2 * i, [P, 2, SEQ], f32r) for i in range(2)]
        fl = [at(f"fl{i}", W + 12 + 2 * i, [P, 2, SEQ], f32r) for i in range(2)]
        q2 = at("q2", W, [P, NPAIR, SEQ])
        k2 = at("k2", W + 4, [P, NPAIR, SEQ])
        v2 = at("v2", W + 8, [P, NT, HW])
        att = at("att", W + 12, [P, NT, HW])
        cv = at("cv", W + 16, [P, 3, NPAIR, SEQ])
        m2h = at("m2h", W + 28, [P, KD, SEQ], f32r)
        m2l = at("m2l", W + 36, [P, KD, SEQ], f32r)
        dz = [at(f"dz{i}", W + 50 + 4.5 * i, [P, 384]) for i in range(2)]
        dp = [at(f"dp{i}", W + 51.5 + 4.5 * i, [P, 384]) for i in range(2)]
        dq = [at(f"dq{i}", W + 53 + 4.5 * i, [P, 384]) for i in range(2)]
        km = at("km", W + 59, [P, KD, SEQ])
        crs = at("crs", W + 67, [P, SEQ])
        memh = at("memh", W + 71, [P, KD, SEQ], f32r)
        meml = at("meml", W + 79, [P, KD, SEQ], f32r)
        mem = at("mem", W + 87, [P, NT, D])
        vm = at("vm", W + 87, [P, NT, D])
        qm = at("qm", W, [P, KD, SEQ])
        mp = [at(f"mp{i}", W + 8 + 4 * i, [P, NT, SEQ]) for i in range(2)]
        mq = [at(f"mq{i}", W + 10 + 4 * i, [P, NT, SEQ]) for i in range(2)]
        omh = at("omh", W + 16, [P, KD, SEQ], f32r)
        oml = at("oml", W + 24, [P, KD, SEQ], f32r)
        ORDER = ["n1", "mem", "p1", "n2", "p2", "n3", "att", "n4", "n5", "fin"]
        HALVES = ("p1", "n2", "p2", "n3", "n4", "n5", "fin")
        TURNED = ("n1", "mem", "n2", "n3", "att", "n4", "n5")
        EVENTS = {"sq": {n: 2 * NT if n in HALVES else NT for n in ORDER},
                  "sd": {n: NT for n in ORDER},
                  "x": {n: 2 * NT for n in HALVES if n[0] != "p"},
                  "y": {n: 2 * NT for n in ("p1", "p2")},
                  "dg": {n: NT for n in TURNED}}
        for n in ("T", "hi", "xT"):
            EVENTS[n] = {n: NPAIR if n == "att" else KD for n in TURNED}

        def norm_sem(st, what):
            return sem("norm_" + what)

        def nth(st, what, n):
            return sum(EVENTS[what].get(o, 0) for o in ORDER[:ORDER.index(st)]) + n

        PS = ctx.enter_context(nc.psum_tensor("PS", [P, 8 * 512], f32))

        def bank(b):
            return PS[:, b * 512:(b + 1) * 512]

        def C(name):
            a, b = CCOL[name]
            return cst[:, a:b]

        def M(name):
            a, b = CCOL[name]
            return msk[:, a:b]

        def par_col(name, i=0):
            c = PCOL[name] + i
            return par[:, c:c + 1]

        def col(i, n=1):
            return small[:, i:i + n]

        EPS, GEPS = 0, 1
        NORM = {n: 2 + 6 * i for i, n in enumerate(["n1", "p1", "n2", "p2", "n3", "mem", "att", "n4", "n5", "fin"])}
        DMX, DL, DRL = 62, 78, 94
        SQ2 = 126
        MMX, MSUM = 110, 118
        dec = at("dec", W + 98, [P, NPAIR, 4])

        def halves(ap, v, second):
            m = 2 ** v
            return ap.rearrange("p (a b) -> p a b", b=2 * m)[:, :, second * m:(second + 1) * m]

        units = []

        def cols_unit(w, c0, n=256):
            units.append((lambda s: w[:, bass.ds(c0 + s, n)].rearrange("(k p) n -> p k n", p=P), n))
            return len(units) - 1

        def rows_unit(w, k0, k, c0=0, n=D):
            units.append((lambda s: w[bass.ds(k0 * P + s, k * P), c0:c0 + n].rearrange("(k p) n -> p k n", p=P), n))
            return len(units) - 1

        w_in, w_in2, w_kv = A["w_in"][0], A["w_in_2"], A["w_kv_mem_2"]
        U_RW = [cols_unit(w_in, RW0 + c) for c in (1536, 512, 768, 0, 256, 1024, 1280)]
        RW_TILE = [12, 4, 6, 0, 2, 8, 10]
        U_QK = [cols_unit(w_in, 256 * c) for c in range(4)]
        U_V = [rows_unit(w_in, 4 * i, 4, 2 * HW, HW) for i in range(2)]
        U_G = [cols_unit(w_in, GATE0 + 256 * c) for c in range(8)]
        U_SO = [cols_unit(A["w_sb_out"][0], 512 * c, 512) for c in range(2)]
        U_RO = [cols_unit(A["w_rw_out"][0], 512 * c, 512) for c in range(2)]
        U_O = [rows_unit(A["w_o"][0], 2 * i, 2) for i in range(4)]
        U_KM = [cols_unit(w_kv, 0)]
        U_F = {}
        for i in range(FF_CHUNKS + 1):
            if i < FF_CHUNKS:
                U_F["g", i] = cols_unit(A["w_ffn_gate"][0], 256 * i)
                U_F["u", i] = cols_unit(A["w_ffn_up"][0], 256 * i)
            if i:
                U_F["d", i - 1] = rows_unit(A["w_ffn_down"][0], 2 * (i - 1), 2)
        U_KM += [cols_unit(w_kv, 256)]
        U_QK2 = [cols_unit(w_in2, 256 * c) for c in range(4)]
        U_V2 = [rows_unit(w_in2, 4 * i, 4, 2 * HW, HW) for i in range(2)]
        U_CV = [cols_unit(w_in2, 3 * HW + 256 * c) for c in range(6)]
        U_KM += [cols_unit(w_kv, 256 * c) for c in (2, 3)]
        U_VM = [rows_unit(w_kv, 2 * i, 2, D, D) for i in range(4)]
        O2_TILE = (0, 2, 4, 6)
        U_O2 = [rows_unit(A["w_out_2"], k, 2) for k in O2_TILE]
        U_QM = [cols_unit(A["w_q_mem_2"], 256 * c) for c in range(4)]
        U_OM = [rows_unit(A["w_o_mem_2"], 2 * i, 2) for i in range(4)]
        U_M = {}
        for i in range(FF2_CHUNKS + 1):
            if i < FF2_CHUNKS:
                U_M["u", i] = cols_unit(A["w_up_2"], 256 * i)
            if i:
                U_M["d", i - 1] = rows_unit(A["w_down_2"], 2 * (i - 1), 2)
        NU = len(units)
        PART_O, PART_F, PART_VM, PART_O2, PART_OM, PART_M = 1, 4, 8, 11, 14, 17
        FILL2 = U_CV + U_KM[2:]

        raw_loaded = [sem(f"raw_loaded{i}") for i in range(RING)]

        FF_BODY, FF_TURNS = 2, (FF_CHUNKS - 3) // 2
        FF2_BODY, FF2_TURNS = 6, (FF2_CHUNKS - 4) // 6
        FF_STEP, FF2_STEP = 3 * FF_BODY, 2 * FF2_BODY
        FF_FIRST, FF2_FIRST = U_F["g", 2], U_M["u", 2]

        VM_BANKS = (0, 1, 4, 5)

        block = ctx.enter_context(nc.Block())

        @block.sync
        def _(sp):
            for t in range(NT):
                sp.dma_start(xres[:, t, :], A["x"][0, t * P:(t + 1) * P, :]).then_inc(sem(f"x_loaded{t}"), 16)
            def load(u, n=0, step=0, shift=0):
                s = u % RING
                src, width = units[u]
                src = src(shift * n)
                if u == 0:
                    sp.dma_start(raw[0][:, 0:UNIT // 2].rearrange("p (k n) -> p k n", n=width), src[:, 0:KD // 2]).then_inc(sem("half_loaded"), 16)
                    sp.dma_start(raw[0][:, UNIT // 2:].rearrange("p (k n) -> p k n", n=width), src[:, KD // 2:]).then_inc(raw_loaded[0], 16)
                    return
                if u >= RING:
                    sp.wait_ge(sem("unit_split"), u - RING + 1 + step * n)
                sp.dma_start(raw[s][:].rearrange("p (k n) -> p k n", n=width), src).then_inc(raw_loaded[s], 16)

            for u in range(FF_FIRST):
                load(u)
                if u == RING:
                    sp.dma_start(lora[0:HD, :], A["w_up"][0]).then_inc(sem("lora_loaded"), 16)
                    sp.dma_start(lora[HD:P, :], A["a_up"][0]).then_inc(sem("lora_loaded"), 16)
                    sp.dma_start(gup[:], A["g_up"][0]).then_inc(sem("lora_loaded"), 16)
                    sp.dma_start(cst[:, P:], A["consts"][:, P:]).then_inc(sem("cst_loaded"), 16)
                    sp.dma_start(msk[:], A["masks"]).then_inc(sem("msk_loaded"), 16)
                if u == U_O[1]:
                    sp.wait_ge(sem("rwo"), NT)
                    sp.dma_start(mem[:], A["mem_2"][0].rearrange("(t p) n -> p t n", p=P)).then_inc(sem("mem_loaded"), 16)
                    sp.dma_start(xres[:], A["x"][0].rearrange("(t p) n -> p t n", p=P)).then_inc(sem("x_loaded0"), 16)
                    sp.dma_start(gmix[:], A["norm_mix_post"].rearrange("a n -> (a n)").partition_broadcast(P)).then_inc(sem("gmix_loaded"), 16)
                    sp.dma_start(gffn[:], A["norm_ffn_post"].rearrange("a n -> (a n)").partition_broadcast(P)).then_inc(sem("gffn_loaded"), 16)
                    sp.dma_start(gfin[:], A["g_final_2"].partition_broadcast(P)).then_inc(sem("gfin_loaded"), 16)
            with sp.Fori(0, FF_TURNS) as n:
                for k in range(FF_STEP):
                    load(FF_FIRST + k, n, FF_STEP, 256 * FF_BODY)
            for u in range(FF_FIRST + FF_TURNS * FF_STEP, FF2_FIRST):
                load(u)
            with sp.Fori(0, FF2_TURNS) as n:
                for k in range(FF2_STEP):
                    load(FF2_FIRST + k, n, FF2_STEP, 256 * FF2_BODY)
            for u in range(FF2_FIRST + FF2_TURNS * FF2_STEP, NU):
                load(u)
            for i in range(2 * NT):
                sp.wait_ge(sem("result"), i + 1)
                cs_ = slice(512 * (i % 2), 512 * (i % 2) + 512)
                sp.dma_start(out[0, i // 2 * P:(i // 2 + 1) * P, cs_], xn[:, i // 2, cs_]).then_inc(sem("stored"), 16)
            sp.wait_ge(sem("stored"), 16 * 2 * NT)

        @block.tensor
        def _(pe):
            def mm(o, l, r, start, stop, **kw):
                return nc.tensor.matmul(o, l, r, start=start, stop=stop, **kw)

            def slot(h):
                return 4 * (h % 2) + h // 2

            def split(u, n, later=0):
                if u:
                    pe.wait_ge(sem("unit_split"), u + 1 + later)
                else:
                    pe.wait_ge(sem("half_split"), 1)
                return (whi[u % RING][:].rearrange("p (k n) -> p k n", n=n),
                        wlo[u % RING][:].rearrange("p (k n) -> p k n", n=n))

            def by_feature(u, hi, lo, b, st=None, between=None, later=0):
                n = units[u][1]
                kt = UNIT // n
                wh, wl = split(u, n, later)
                for f in range(n // P):
                    o = PS[:, b * 512 + f * SEQ:b * 512 + (f + 1) * SEQ]
                    for k in range(kt):
                        if st and f == 0:
                            pe.wait_ge(norm_sem(st, "xT"), nth(st, "xT", max(k + 1, 2)))
                            if u == 0 and k == kt // 2:
                                pe.wait_ge(sem("unit_split"), 1)
                        fs = slice(f * P, (f + 1) * P)
                        mm(o, wh[:, k, fs], hi[:, k, :], k == 0, False)
                        mm(o, wh[:, k, fs], lo[:, k, :], False, False)
                        last = mm(o, wl[:, k, fs], hi[:, k, :], False, k == kt - 1)
                    if between and f == 1:
                        between()
                last.then_inc(sem("units_used"), 1)

            def by_token(u, hi, lo, k0, b, first, end, later=0):
                n = units[u][1]
                kt = UNIT // n
                wh, wl = split(u, n, later)
                nc_ = n // 512
                if end:
                    steps = [(k, t, c) for t in range(NT) for c in range(nc_) for k in range(kt)]
                else:
                    steps = [(k, t, c) for k in range(kt) for t in range(NT) for c in range(nc_)]
                for k, t, c in steps:
                    ts = slice(t * P, (t + 1) * P)
                    o = bank(b[t * nc_ + c] if isinstance(b, tuple) else b + t * nc_ + c)
                    ns = slice(c * 512, (c + 1) * 512)
                    mm(o, hi[:, k0 + k, ts], wh[:, k, ns], first and k == 0, False)
                    mm(o, hi[:, k0 + k, ts], wl[:, k, ns], False, False)
                    last = mm(o, lo[:, k0 + k, ts], wh[:, k, ns], False, end and k == kt - 1)
                    if end and k == kt - 1 and (t, c) != (NT - 1, nc_ - 1):
                        last.then_inc(sem("part_done"), 1)
                last.then_inc(sem("units_used"), 1)

            def transpose_in(st, src, nf, b, filler=0):
                for t in range(NT):
                    pe.wait_ge(norm_sem(st, "dg"), nth(st, "dg", t + 1))
                    for f in range(nf):
                        if filler and f == 6:
                            pe.wait_ge(sem("km_evac"), filler)
                        last = mm(PS[:, b * 512 + f * SEQ + t * P:b * 512 + f * SEQ + (t + 1) * P],
                                  src[:, t, f * P:(f + 1) * P], dg[st][:, t, :], True, True)
                        if t == NT - 1:
                            last.then_inc(norm_sem(st, "T"), 1)

            transpose_in("n1", xres, KD, 4)
            for i, u in enumerate(U_RW):
                if i >= 2:
                    pe.wait_ge(sem("out_evac"), i - 1)
                by_feature(u, xh, xl, i % 2, None if i else "n1")
                if i == 2:
                    pe.wait_ge(sem("lora_in"), 1)
                    pe.wait_ge(sem("lora_loaded"), 48)
                    for j in range(NPAIR):
                        mm(PS[:, 4 * 512 + j * SEQ:4 * 512 + (j + 1) * SEQ], lora[0:HD, j * P:(j + 1) * P],
                           rw[0:HD, 12, :], True, True)
                    for j in range(NPAIR):
                        last = mm(PS[:, 6 * 512 + j * SEQ:6 * 512 + (j + 1) * SEQ], lora[HD:P, j * P:(j + 1) * P],
                                  rw[HD:P, 12, :], True, True)
                    last.then_inc(sem("lora_out"), 1)
                if i == 4:
                    pe.wait_ge(sem("kk_sq"), 1)
                    pe.wait_ge(sem("lora_evac"), 1)
                    pe.wait_ge(sem("cst_loaded"), 16)
                    for j in range(NPAIR):
                        last = mm(PS[0:NH, 4 * 512:4 * 512 + SEQ], C("gather")[:, NH * j:NH * (j + 1)], kq[:, j, :], j == 0,
                                  j == NPAIR - 1)
                    last.then_inc(sem("kk_ss"), 1)
            for i, u in enumerate(U_QK):
                pe.wait_ge(sem("out_evac"), i + 6)
                by_feature(u, xh, xl, (i + 7) % 2)
                if i == 0:
                    pe.wait_ge(sem("kk_rs"), 1)
                    for j in range(NPAIR):
                        last = mm(PS[:, 4 * 512 + j * SEQ:4 * 512 + (j + 1) * SEQ], C("spread")[0:NH, j * P:(j + 1) * P], krs[:],
                                  True, True)
                    last.then_inc(sem("kk_spread"), 1)
            for i, u in enumerate(U_V):
                by_token(u, xh, xl, 4 * i, 2, i == 0, i == 1)
                if i == 0:
                    pe.wait_ge(sem("kk_unit"), 1)
                    for j in range(NPAIR):
                        mm(PS[:, 4 * 512 + j * SEQ:4 * 512 + (j + 1) * SEQ], gup[:, j * P:(j + 1) * P], rw[:, 13, :], True, True)
                    pe.wait_ge(sem("rkk"), 1)
                    for j in range(NPAIR):
                        last = mm(PS[:, 6 * 512 + j * SEQ:6 * 512 + (j + 1) * SEQ], C("blockones"), rkk[:, j, :], True, True)
                    last.then_inc(sem("bonus_mm"), 1)
            def tokens(tt, qs):
                ts = slice(tt * P, (tt + 1) * P)
                for q in qs:
                    src = (eX, kk, eN, rw)[q]
                    for j in range(NPAIR):
                        s = src[:, 8 + j, ts] if q == 3 else src[:, j, ts]
                        last = nc.tensor.transpose(PS[:, (4 + q) * 512 + j * P:(4 + q) * 512 + (j + 1) * P], s, C("ident"))
                    last.then_inc(sem("tok_T"), 1)

            def pairs(tt, qs):
                ts = slice(tt * P, (tt + 1) * P)
                for q in qs:
                    l, r = ((kk, eX), (eN, eX), (kk, eP), (eN, eP))[q]
                    for g in range(2):
                        b = 2 * q + g
                        if tt == 0 and b < 2:
                            pe.wait_ge(sem("out_evac"), 19 - b)
                        if tt and b == 2:
                            pe.wait_ge(sem("state"), 1 + NPAIR * 2 * tt)
                        if tt and b == 3:
                            pe.wait_ge(sem("y_evac"), tt)
                        if b >= 4:
                            pe.wait_ge(sem("tok_evac"), 4 * tt + b - 3)
                        p = slice(HD * g, HD * g + HD)
                        for e in range(4):
                            h = 2 * e + g
                            last = mm(PS[:, b * 512 + e * P:b * 512 + (e + 1) * P], l[p, h // 2, ts], r[p, h // 2, ts], True, True)
                        last.then_inc(sem("pair_mm"), 1)

            def y_sum(tt):
                pe.wait_ge(sem("y_evac"), tt + 1)
                if tt:
                    pe.wait_ge(sem("wt_evac"), tt + 1)
                for j in range(NPAIR):
                    last = mm(PS[:, 6 * 512 + j * P:6 * 512 + (j + 1) * P], C("blockones"), yT[:, j, tt * P:(tt + 1) * P], True, True)
                last.then_inc(sem("y_sum"), 1)

            def y_squares(tt):
                pe.wait_ge(sem("y_sq"), tt + 1)
                if tt:
                    pe.wait_ge(sem("av_evac"), tt + 1)
                for j in range(NPAIR):
                    last = mm(PS[0:NH, 7 * 512:7 * 512 + P], C("gather")[:, NH * j:NH * (j + 1)], yq[:, j, :], j == 0, j == NPAIR - 1)
                last.then_inc(sem("y_ss"), 1)

            def y_spread(tt):
                pe.wait_ge(sem("y_rs"), tt + 1)
                for j in range(NPAIR):
                    last = mm(PS[:, 6 * 512 + j * P:6 * 512 + (j + 1) * P], C("spread")[0:NH, j * P:(j + 1) * P],
                              grs[:, tt * P:(tt + 1) * P], True, True)
                last.then_inc(sem("y_spread"), 1)

            pe.wait_ge(sem("gn_pre"), 1)
            for i in range(NH + 1):
                r = slice(HD * (i % 2), HD * (i % 2) + HD)
                b = 4 + i % 2
                if i < NH:
                    if i == 0:
                        pe.wait_ge(sem("out_evac"), 11)
                    if i >= 2:
                        pe.wait_ge(sem("sb_arg_read"), i - 1)
                    mm(PS[:, b * 512:b * 512 + SEQ], sk[r, i // 2, 0:P], sq[r, i // 2, :], True, False, skip_group_check=True)
                    mm(PS[:, b * 512 + SEQ:b * 512 + 384], sk[r, i // 2, P:SEQ], sq[r, i // 2, P:SEQ], False, True, skip_group_check=True) \
                        .then_inc(sem("sb_z"), 1)
                    pe.wait_ge(sem("out_evac"), i + 10)
                    by_feature(U_G[i], xh, xl, (i + 11) % 2)
                    pe.wait_ge(sem("sb_lf"), i + 1)
                    mm(PS[:, b * 512:b * 512 + 384], C("tri"), st2[i % 2][:], False, False, skip_group_check=True)
                    mm(PS[:, b * 512 + P:b * 512 + SEQ], C("ones"), st2[i % 2][:, SEQ:384], False, True,
                       skip_group_check=True).then_inc(sem("sb_arg"), 1)
                if i == NH:
                    pe.wait_ge(sem("rw_pre"), 1)
                    pairs(0, (0, 1))
                    pe.wait_ge(sem("sb_arg_read"), NH)
                    tokens(0, (0, 1))
                if i >= 1:
                    h = i - 1
                    o = PS[HD * (h % 2):HD * (h % 2) + HD, (6 + h // 4) * 512 + (h // 2 % 2) * SEQ:
                           (6 + h // 4) * 512 + (h // 2 % 2) * SEQ + SEQ]
                    pe.wait_ge(sem("sb_w"), h + 1)
                    if h == 0:
                        pe.wait_ge(sem("sv_ready"), 2)
                    mm(o, sv[:, 0, h * HD:(h + 1) * HD], st4[h % 2][:, 0:SEQ], True, False, skip_group_check=True)
                    mm(o[:, P:SEQ], sv[:, 1, h * HD:(h + 1) * HD], st4[h % 2][:, SEQ:384], False, True,
                       skip_group_check=True).then_inc(sem("sb_o"), 1)

            for tt in range(NT):
                if tt:
                    pairs(tt, (0, 1))
                    tokens(tt, (0, 1))
                for g in range(2):
                    pe.wait_ge(sem("xm"), 12 * tt + g + 1)
                    pe.wait_ge(sem("pair_evac"), 8 * tt + 2)
                    for e in range(4):
                        last = nc.tensor.transpose(PS[:, g * 512 + e * P:g * 512 + (e + 1) * P], Xm[0][:, 4 * g + e, :], C("ident"))
                    last.then_inc(sem("inv_T1"), 1)
                pairs(tt, (2,))
                if tt == 0:
                    pe.wait_ge(sem("sb_evac"), 4)
                tokens(tt, (2, 3))
                pairs(tt, (3,))
                for v in range(1, 6):
                    for g in range(2):
                        pe.wait_ge(sem("xm"), 12 * tt + 2 * v + g + 1)
                        pe.wait_ge(sem("inv_t"), 10 * tt + 2 * (v - 1) + g + 1)
                        for e in range(4):
                            h = 4 * g + e
                            last = mm(PS[:, g * 512 + e * HD:g * 512 + (e + 1) * HD], Xm[v % 2][:, h, :],
                                      halves(Tm[:, h, :], v, 0), True, True)
                        last.then_inc(sem("inv_g"), 1)
                    for g in range(2):
                        if v == 1:
                            pe.wait_ge(sem("pair_evac"), 8 * tt + 5 + g)
                        pe.wait_ge(sem("inv_g_evac"), 10 * tt + 2 * (v - 1) + g + 1)
                        pe.wait_ge(sem("inv_tt"), 12 * tt + 2 * (v - 1) + g + 1)
                        pe.wait_ge(sem("g_zero"), 5 * tt + v)
                        if v < 5:
                            for e in range(4):
                                mm(PS[:, (2 + g) * 512 + e * HD:(2 + g) * 512 + (e + 1) * HD], TT[:, 4 * g + e, :],
                                   halves(Gm[v % 2][:, 4 * g + e, :], v, 0), True, True)
                        for e in range(4):
                            last = mm(PS[:, (4 + g) * 512 + e * HD:(4 + g) * 512 + (e + 1) * HD], Gm[v % 2][:, 4 * g + e, :],
                                      halves(TT[:, 4 * g + e, :], v, 1), True, True)
                        last.then_inc(sem("inv_up"), 1)
                    if v == 1:
                        pe.wait_ge(sem("pair_evac"), 8 * tt + 8)
                    if tt and v in (2, 3, 4):
                        (y_sum, y_squares, y_spread)[v - 2](tt - 1)
                if tt:
                    pe.wait_ge(sem("y_done"), tt)
                for h in range(NH):
                    o = PS[:, 7 * 512 + h * HD:7 * 512 + (h + 1) * HD]
                    last = mm(o, AK[:, slot(h), :], vt_[:, h * HD:(h + 1) * HD], True, True)
                last.then_inc(sem("av_mm"), 1)
                pe.wait_ge(sem("inv_tt"), 12 * tt + 12)
                for h in range(NH):
                    p = slice(HD * (h % 2), HD * (h % 2) + HD)
                    last = mm(PS[p, 6 * 512 + (h // 2) * P:6 * 512 + (h // 2 + 1) * P], at_[:, h * HD:(h + 1) * HD], TT[:, slot(h), :],
                              True, True, skip_group_check=True)
                last.then_inc(sem("wt_mm"), 1)
                pe.wait_ge(sem("av_evac"), tt + 1)
                for h in range(NH):
                    last = mm(PS[:, h * HD:(h + 1) * HD], TT[:, slot(h), :], AV[:, h * HD:(h + 1) * HD], True, True)
                last.then_inc(sem("u0_mm"), 1)
                pe.wait_ge(sem("wt_evac"), tt + 1)

                def y_values(heads):
                    for h in heads:
                        mm(PS[HD * (h % 2):HD * (h % 2) + HD, 3 * 512 + (h // 2) * P:3 * 512 + (h // 2 + 1) * P],
                           vt_[:, h * HD:(h + 1) * HD], RK[:, slot(h), :], False, False, skip_group_check=True)

                for c in range(2):
                    g = 2 * tt + c
                    rs_ = slice(CHUNK * c, CHUNK * c + CHUNK)
                    for j in range(NPAIR):
                        pe.wait_ge(sem("state"), 1 + NPAIR * (g - 1) + j + 1 if g else 1)
                        last = mm(PS[rs_, 512 + j * P:512 + (j + 1) * P], WT[:, j, rs_], St[:, g, j, :], True, True,
                                  skip_group_check=True)
                    last.then_inc(sem("u_mm"), 1)
                    if c == 0:
                        for j in range(NPAIR):
                            mm(PS[:, 3 * 512 + j * P:3 * 512 + j * P + CHUNK], St[:, g, j, :], eP[:, j, g * CHUNK:(g + 1) * CHUNK],
                               j == 0, False, skip_group_check=True)
                        y_values(range(2))
                    else:
                        for j in range(NPAIR):
                            mm(PS[:, 3 * 512 + j * P + CHUNK:3 * 512 + (j + 1) * P], St[:, g, j, :],
                               eP[:, j, g * CHUNK:(g + 1) * CHUNK], False, False, skip_group_check=True)
                    pe.wait_ge(sem("u_ready"), g + 1)
                    if g < 3:
                        for j in range(NPAIR):
                            o = PS[:, 2 * 512 + j * P:2 * 512 + (j + 1) * P]
                            js = slice(j * P, (j + 1) * P)
                            mm(o, bt_[rs_, js], Uc[rs_, js], True, False)
                            last = mm(o, kt_[rs_, js], vt_[rs_, js], False, True)
                        last.then_inc(sem("ds_mm"), 1)
                    if c == 0:
                        y_values(range(2, NH))
                for h in range(NH):
                    last = mm(PS[HD * (h % 2):HD * (h % 2) + HD, 3 * 512 + (h // 2) * P:3 * 512 + (h // 2 + 1) * P],
                              Uc[:, h * HD:(h + 1) * HD], RB[:, slot(h), :], False, h == NH - 1, skip_group_check=True)
                last.then_inc(sem("y_mm"), 1)

            y_sum(1)
            by_feature(U_SO[0], sboh, sbol, 0, None, lambda: y_squares(1))
            y_spread(1)
            by_feature(U_SO[1], sboh, sbol, 2)
            pe.wait_ge(sem("rwo"), NT)
            for i in range(2):
                pe.wait_ge(sem("merge_a"), i + 1)
                by_feature(U_RO[i], rwoh, rwol, 2 * i)
            for i, u in enumerate(U_O):
                pe.wait_ge(sem("merged"), i // 2 + 1)
                by_token(u, mh, ml, 2 * i, 4, i == 0, i == 3)
                if i == 1:
                    pe.wait_ge(sem("merge_sum"), 2)
                    transpose_in("mem", mem, KD, 0)

            pe.wait_ge(norm_sem("mem", "xT"), nth("mem", "xT", KD))
            by_feature(U_KM[0], memh, meml, 3)
            transpose_in("n2", xres, KD, 0, 1)
            def ffn(i, n=0):
                later = FF_STEP * n
                if i < FF_CHUNKS:
                    if i >= 2:
                        pe.wait_ge(sem("ff_out"), i - 1 + FF_BODY * n)
                    by_feature(U_F["g", i], xh, xl, 2 * (i % 2), None if i else "n2", None, later)
                    by_feature(U_F["u", i], xh, xl, 2 * (i % 2) + 1, None, None, later)
                if i:
                    pe.wait_ge(sem("ff_h"), i + FF_BODY * n)
                    by_token(U_F["d", i - 1], fh[(i - 1) % 2], fl[(i - 1) % 2], 0, 4, i == 1, i == FF_CHUNKS, later)

            ffn(0)
            ffn(1)
            with pe.Fori(0, FF_TURNS) as n:
                for k in range(FF_BODY):
                    ffn(2 + k, n)
            for i in range(2 + FF_TURNS * FF_BODY, FF_CHUNKS + 1):
                ffn(i)

            by_feature(U_KM[1], memh, meml, 3)
            transpose_in("n3", xres, KD, 0, 2)
            for i, u in enumerate(U_QK2):
                if i >= 2:
                    pe.wait_ge(sem("out2_evac"), i - 1)
                by_feature(u, xh, xl, i % 2, None if i else "n3")
            for i, u in enumerate(U_V2):
                by_token(u, xh, xl, 4 * i, 2, i == 0, i == 1)
            def turn(h):
                pe.wait_ge(sem("d_p"), 2 * h + 2)
                if h < 2:
                    pe.wait_ge(sem("v2_ready"), 2)
                else:
                    pe.wait_ge(sem("d_q"), h - 1)
                for c in range(3):
                    b = (2 + h % 2) * 512 + c * P
                    last = nc.tensor.transpose(PS[:, b:b + P], dp[h % 2][:, c * P:(c + 1) * P], C("ident"))
                last.then_inc(sem("d_T"), 1)

            def head_out(h):
                pe.wait_ge(sem("d_q"), h + 1)
                hs = slice(h * HD, (h + 1) * HD)
                mm(bank(6)[:, hs], dq[h % 2][:, 0:P], v2[:, 0, hs], True, True)
                mm(bank(7)[:, hs], dq[h % 2][:, P:SEQ], v2[:, 0, hs], True, False)
                mm(bank(7)[:, hs], dq[h % 2][:, SEQ:384], v2[:, 1, hs], False, True).then_inc(sem("d_o"), 1)

            for i in range(NH):
                r = slice(HD * (i % 2), HD * (i % 2) + HD)
                b = (4 + i % 2) * 512
                if i == 0:
                    pe.wait_ge(sem("out2_evac"), 4)
                if i >= 2:
                    pe.wait_ge(sem("d_z_read"), i - 1)
                mm(PS[:, b:b + P], q2[r, i // 2, 0:P], k2[r, i // 2, 0:P], True, True)
                mm(PS[:, b + P:b + 384], q2[r, i // 2, P:SEQ], k2[r, i // 2, :], True, True).then_inc(sem("d_z"), 1)
                pe.wait_ge(sem("out2_evac"), i + 3)
                if i < 6:
                    by_feature(FILL2[i], xh, xl, i % 2)
                else:
                    by_feature(FILL2[i], memh, meml, i % 2)
                if i >= 1:
                    turn(i - 1)
                if i >= 2:
                    head_out(i - 2)
            turn(NH - 1)
            pe.wait_ge(sem("out2_evac"), 12)
            pe.wait_ge(sem("d_z_read"), NH)
            by_token(U_VM[0], memh, meml, 0, VM_BANKS, True, False)
            head_out(NH - 2)
            head_out(NH - 1)
            by_token(U_VM[1], memh, meml, 2, VM_BANKS, False, False)
            transpose_in("att", att, NPAIR, 6)
            by_token(U_VM[2], memh, meml, 4, VM_BANKS, False, False)
            pe.wait_ge(sem("c_sq"), 1)
            pe.wait_ge(sem("d_q"), NH)
            for j in range(NPAIR):
                last = mm(PS[:, 2 * 512:2 * 512 + SEQ], C("ones"), cv[:, 1, j, :], j == 0, j == NPAIR - 1)
            last.then_inc(sem("c_ss"), 1)
            by_token(U_VM[3], memh, meml, 6, VM_BANKS, False, True)
            for i, u in enumerate(U_O2):
                if i < 2:
                    pe.wait_ge(norm_sem("att", "xT"), nth("att", "xT", NPAIR))
                else:
                    pe.wait_ge(sem("conv_xT"), NPAIR)
                if i == 0:
                    pe.wait_ge(sem("vm_ready"), 2)
                    pe.wait_ge(sem("c_sd"), 1)
                by_token(u, m2h, m2l, O2_TILE[i], 0, i == 0, i == 3)

            pe.wait_ge(sem("vm_ready"), 4)
            transpose_in("n4", xres, KD, 4)
            for i in range(2):
                by_feature(U_QM[i], xh, xl, i, None if i else "n4")

            def logits(h):
                pe.wait_ge(sem("qm_evac"), h + 1)
                if h >= 2:
                    pe.wait_ge(sem("m_exp"), 2 * (h - 1))
                for t in range(NT):
                    for e in range(2):
                        last = mm(PS[:, (2 + h % 2) * 512 + t * SEQ:(2 + h % 2) * 512 + (t + 1) * SEQ],
                                  qm[:, 2 * h + e, t * P:(t + 1) * P], km[:, 2 * h + e, :], e == 0, e == 1)
                last.then_inc(sem("m_z"), 1)

            def weights_T(h):
                pe.wait_ge(sem("m_p"), h + 1)
                if h >= 2:
                    pe.wait_ge(sem("m_q"), h - 1)
                for mt in range(NT):
                    for t in range(NT):
                        b = (4 + h % 2) * 512 + mt * SEQ + t * P
                        last = nc.tensor.transpose(PS[:, b:b + P], mp[h % 2][:, t, mt * P:(mt + 1) * P], C("ident"))
                last.then_inc(sem("m_T"), 1)

            def outputs(h):
                pe.wait_ge(sem("m_q"), h + 1)
                if h >= 2:
                    pe.wait_ge(sem("om"), 2 * (h - 1))
                for e in range(2):
                    for mt in range(NT):
                        last = mm(PS[:, (6 + h % 2) * 512 + e * SEQ:(6 + h % 2) * 512 + (e + 1) * SEQ],
                                  vm[:, mt, (2 * h + e) * P:(2 * h + e + 1) * P], mq[h % 2][:, mt, :], mt == 0, mt == 1)
                last.then_inc(sem("m_o"), 1)

            logits(0)
            by_feature(U_QM[2], xh, xl, 0)
            logits(1)
            weights_T(0)
            logits(2)
            by_feature(U_QM[3], xh, xl, 1)
            logits(3)
            for h in range(1, MEM_HEADS):
                weights_T(h)
                outputs(h - 1)
            outputs(MEM_HEADS - 1)
            for i, u in enumerate(U_OM):
                pe.wait_ge(sem("om"), 2 * (i + 1))
                by_token(u, omh, oml, 2 * i, 0, i == 0, i == 3)

            transpose_in("n5", xres, KD, 4)
            def mlp(i, n=0):
                later = FF2_STEP * n
                if i < FF2_CHUNKS:
                    if i >= 2:
                        pe.wait_ge(sem("mlp_out"), i - 1 + FF2_BODY * n)
                    by_feature(U_M["u", i], xh, xl, i % 2, None if i else "n5", None, later)
                if i:
                    pe.wait_ge(sem("mlp_h"), i + FF2_BODY * n)
                    by_token(U_M["d", i - 1], fh[(i - 1) % 2], fl[(i - 1) % 2], 0, 4, i == 1, i == FF2_CHUNKS, later)

            mlp(0)
            mlp(1)
            with pe.Fori(0, FF2_TURNS) as n:
                for k in range(FF2_BODY):
                    mlp(2 + k, n)
            for i in range(2 + FF2_TURNS * FF2_BODY, FF2_CHUNKS + 1):
                mlp(i)

        @block.gpsimd
        def _(pool):
            pool.wait_ge(sem("msk_loaded"), 16)
            for tt in range(NT):
                for v in range(6):
                    for g in range(2):
                        if g == 0:
                            pool.wait_ge(sem("pair_evac"), 8 * tt + 2)
                        if v == 2:
                            pool.wait_ge(sem("inv_tt"), 12 * tt + g + 1)
                            pool.wait_ge(sem("inv_T1"), 2 * tt + g + 1)
                        elif v > 2:
                            pool.wait_ge(sem("inv_g"), 10 * tt + 2 * (v - 3) + g + 1)
                        elif tt:
                            pool.wait_ge(sem("inv_g"), 10 * tt)
                        gs = slice(4 * g, 4 * g + 4)
                        nc.gpsimd.tensor_tensor(Xm[v % 2][:, gs, :], XT[:, gs, :],
                                                M(f"level{2 ** v}").unsqueeze(1).broadcast_to([P, 4, P]), ALU.mult) \
                            .then_inc(sem("xm"), 1)
                    if v:
                        if v > 2 or tt:
                            pool.wait_ge(sem("inv_up"), 10 * tt + 2 * max(v - 2, 0))
                        nc.gpsimd.memset(halves(Gm[v % 2][:].rearrange("p e t -> p (e t)"), v, 1), 0.0).then_inc(sem("g_zero"), 1)

        @block.scalar
        def _(act):
            chain = [0]

            def A_(o, i, f, **kw):
                return nc.scalar.activation(o, i, f, **kw)

            def link(ins):
                chain[0] += 1
                ins.then_inc(sem("act_chain"), 1)
                act.wait_ge(sem("act_chain"), chain[0])

            def hi(u, n=0, step=0):
                if u >= NU:
                    return
                act.wait_ge(raw_loaded[u % RING], 16 * (u // RING + 1) + 16 * (step // RING) * n)
                if u >= RING:
                    act.wait_ge(sem("units_used"), u - RING + 1 + step * n)
                A_(whi[u % RING][:], raw[u % RING][:], ACT.Copy).then_inc(sem("hi_done"), 1)

            def after(u):
                hi(u + RING)
                act.wait_ge(sem("units_used"), u + 1)

            def deviation(st, src, ready, width=D):
                c = NORM[st]
                for t in range(NT):
                    ready(t)
                    A_(junk[:, 0:width], src(t), ACT.Square, accum_out=col(c + t)).then_inc(norm_sem(st, "sq"), 1)
                    act.wait_ge(norm_sem(st, "sq"), nth(st, "sq", t + 1))
                    A_(col(c + 2 + t), col(c + t), ACT.Sqrt, scale=1.0 / width, bias=col(EPS)).then_inc(norm_sem(st, "sd"), 1)

            def part_ready(base, u, t, c):
                if (t, c) == (NT - 1, 1):
                    act.wait_ge(sem("units_used"), u + 1)
                else:
                    act.wait_ge(sem("part_done"), base + 2 * t + c + 1)

            def deviation_halves(st, src, ready):
                c = NORM[st]
                for t in range(NT):
                    ready(t, 0)
                    A_(junk[:, 0:512], src(t, 0), ACT.Square, accum_out=col(c + t)).then_inc(norm_sem(st, "sq"), 1)
                    act.wait_ge(norm_sem(st, "sq"), nth(st, "sq", 2 * t + 1))
                    link(A_(col(SQ2 + t), col(c + t), ACT.Identity, scale=1.0 / D, bias=col(EPS)))
                    ready(t, 1)
                    A_(junk[:, 512:D], src(t, 1), ACT.Square, accum_out=col(c + 4 + t)).then_inc(norm_sem(st, "sq"), 1)
                    act.wait_ge(norm_sem(st, "sq"), nth(st, "sq", 2 * t + 2))
                    A_(col(c + 2 + t), col(c + 4 + t), ACT.Sqrt, scale=1.0 / D, bias=col(SQ2 + t)).then_inc(norm_sem(st, "sd"), 1)

            def residual_deviation(st):
                deviation_halves(st, lambda t, h: xres[:, t, 512 * h:512 * h + 512],
                                 lambda t, h: act.wait_ge(norm_sem(st, "x"), nth(st, "x", 2 * t + h + 1)))

            def round_T(st, g, dst, f0, nf, b):
                for f in range(nf):
                    act.wait_ge(norm_sem(st, "T"), nth(st, "T", f // 2 * 2 + 2))
                    A_(dst[:, f0 + f, :], PS[:, b * 512 + f * SEQ:b * 512 + (f + 1) * SEQ], ACT.Copy, scale=par_col(g, f)) \
                        .then_inc(norm_sem(st, "hi"), 1)

            act.dma_start(cst[:, 0:P], A["consts"][:, 0:P]).then_inc(sem("ident_loaded"), 16)
            act.dma_start(par[:], A["params"]).then_inc(sem("par_loaded"), 16)
            nc.scalar.preload_act_table_set("sqrt_and_others")
            act.wait_ge(sem("eps_set"), 1)
            deviation("n1", lambda t: xres[:, t, :], lambda t: act.wait_ge(sem(f"x_loaded{t}"), 16))
            act.wait_ge(sem("half_loaded"), 16)
            A_(whi[0][:, 0:UNIT // 2], raw[0][:, 0:UNIT // 2], ACT.Copy).then_inc(sem("half_hi"), 1)
            act.wait_ge(raw_loaded[0], 16)
            A_(whi[0][:, UNIT // 2:], raw[0][:, UNIT // 2:], ACT.Copy).then_inc(sem("hi_done"), 1)
            act.wait_ge(sem("par_loaded"), 16)
            round_T("n1", "norm_mix_pre", xh, 0, KD, 4)
            for u in range(1, RING):
                hi(u)
            nc.scalar.preload_act_table_set("sigmoid_and_others")
            for i, u in enumerate(U_RW):
                after(u)
                if i >= 2:
                    act.wait_ge(sem("mixed"), i - 1)
                else:
                    act.wait_ge(sem("stg_zero"), 1)
                A_(stg[i % 2][:, :, 1:SEQ + 1], bank(i % 2).rearrange("p (f t) -> p f t", f=2), ACT.Copy) \
                    .then_inc(sem("out_evac"), 1)
                if i == 1:
                    act.wait_ge(sem("mixed"), 1)
                    A_(rw[0:HD, 12, :], rw[0:HD, 12, :], ACT.Tanh)
                    A_(rw[:, 13, :], rw[:, 13, :], ACT.Sigmoid).then_inc(sem("lora_in"), 1)
                if i == 3:
                    act.wait_ge(sem("lora_out"), 1)
                    for j in range(NPAIR):
                        A_(sg[:, j, :], PS[:, 4 * 512 + j * SEQ:4 * 512 + (j + 1) * SEQ], ACT.Sigmoid, bias=par_col("w0", j))
                    for j in range(NPAIR):
                        last = A_(ag[:, j, :], PS[:, 6 * 512 + j * SEQ:6 * 512 + (j + 1) * SEQ], ACT.Sigmoid, bias=par_col("a0", j))
                    last.then_inc(sem("lora_evac"), 1)
                if i == 5:
                    act.wait_ge(sem("kk_ss"), 1)
                    A_(krs[:], PS[0:NH, 4 * 512:4 * 512 + SEQ], ACT.Sqrt).then_inc(sem("kk_sd"), 1)
            nc.scalar.preload_act_table_set("natural_log_exp_and_others")
            act.wait_ge(sem("cs"), 1)
            act.wait_ge(sem("k_mod"), 1)
            c0 = float(np.exp(-0.5))
            A_(eP[:], cs[:], ACT.Exp, scale=-c0)
            A_(eN[:], cs[:], ACT.Exp, scale=c0)
            A_(eX[:], sg[:], ACT.Exp, scale=-c0).then_inc(sem("decays"), 1)
            for i, u in enumerate(U_QK):
                after(u)
                dst = (sq, sk)[i // 2]
                A_(dst[:, 2 * (i % 2):2 * (i % 2) + 2, :], bank((i + 7) % 2).rearrange("p (f t) -> p f t", f=2), ACT.Copy,
                   scale=HD ** -0.5 if i < 2 else 1.0).then_inc(sem("out_evac"), 1)
            hi(U_V[0] + RING)
            after(U_V[1])
            for t in range(NT):
                A_(sv[:, t, :], bank(2 + t), ACT.Copy).then_inc(sem("sv_ready"), 1)
            for i in range(NH):
                b = (4 + i % 2) * 512
                s1, s2, s3, s4 = st1[i % 2], st2[i % 2], st3[i % 2], st4[i % 2]
                act.wait_ge(sem("sb_z"), i + 1)
                if i >= 2:
                    act.wait_ge(sem("sb_lf"), i - 1)
                link(A_(s1[:], PS[:, b:b + 384], ACT.Abs))
                link(A_(s1[:], s1[:], ACT.Exp, scale=-1.0))
                A_(s1[:], s1[:], ACT.Ln, bias=1.0).then_inc(sem("sb_ln"), 1)
                if i:
                    hi(U_G[i - 1] + RING)
                act.wait_ge(sem("units_used"), U_G[i] + 1)
                for f in range(2):
                    last = A_(gates[:, 2 * i + f, :], PS[:, ((i + 11) % 2) * 512 + f * SEQ:((i + 11) % 2) * 512 + (f + 1) * SEQ],
                              ACT.Identity, bias=par_col("b_gate", 2 * i + f))
                last.then_inc(sem("out_evac"), 1)
                act.wait_ge(sem("sb_arg_read"), i + 1)
                if i >= 2:
                    act.wait_ge(sem("sb_o"), i - 1)
                A_(s4[:], s3[:], ACT.Exp).then_inc(sem("sb_w"), 1)
            hi(U_G[NH - 1] + RING)
            def tok_evac(tt, qs):
                for q in qs:
                    act.wait_ge(sem("tok_T"), 4 * tt + q + 1)
                    if q == 0 and tt == 0:
                        act.wait_ge(sem("units_used"), U_G[7] + 1)
                    A_((at_, bt_, kt_, vt_)[q][:], bank(4 + q), ACT.Copy).then_inc(sem("tok_evac"), 1)

            tok_evac(0, (0, 1))
            act.wait_ge(sem("sb_o"), NH)
            for j in range(2):
                A_(sboh[:, 2 * j:2 * j + 2, :], bank(6 + j).rearrange("p (f t) -> p f t", f=2), ACT.Copy).then_inc(sem("sbo_hi"), 1)

            def y_square(tt):
                act.wait_ge(sem("yc_ready"), tt + 1)
                A_(yq[:], yc[:, :, tt * P:(tt + 1) * P], ACT.Square).then_inc(sem("y_sq"), 1)

            def y_root(tt):
                act.wait_ge(sem("y_ss"), tt + 1)
                A_(grs[:, tt * P:(tt + 1) * P], PS[0:NH, 7 * 512:7 * 512 + P], ACT.Sqrt, scale=1.0 / HD,
                   bias=small[0:NH, GEPS:GEPS + 1]).then_inc(sem("y_sd"), 1)

            def y_round(tt):
                act.wait_ge(sem("y_done"), tt + 1)
                A_(rwoh[:, :, tt * P:(tt + 1) * P], yc[:, :, tt * P:(tt + 1) * P], ACT.Copy).then_inc(sem("rwo_hi"), 1)

            act.wait_ge(sem("out_evac"), 19)
            def gate_sigmoid(c):
                A_(gates[:, 4 * c:4 * c + 4, :], gates[:, 4 * c:4 * c + 4, :], ACT.Sigmoid).then_inc(sem("gates_ready"), 1)

            for tt in range(NT):
                if tt:
                    tok_evac(tt, (0, 1))
                tok_evac(tt, (2, 3))
                for v in range(1, 6):
                    for g in range(2):
                        act.wait_ge(sem("inv_g"), 10 * tt + 2 * (v - 1) + g + 1)
                        A_(halves(Gm[v % 2][:, 4 * g:4 * g + 4, :].rearrange("p e t -> p (e t)"), v, 0),
                           bank(g)[:, 0:4 * HD].rearrange("p (a b) -> p a b", b=2 ** v), ACT.Copy) \
                            .then_inc(sem("inv_g_evac"), 1)
                    if tt == 0 and v < 5:
                        gate_sigmoid(v - 1)
                    if tt == 0 and v == 5:
                        nc.scalar.preload_act_table_set("sqrt_and_others")
                    if tt and v in (3, 4):
                        (y_square, y_root)[v - 3](tt - 1)
                if tt:
                    y_round(tt - 1)
                act.wait_ge(sem("av_mm"), tt + 1)
                A_(AV[:], bank(7), ACT.Copy).then_inc(sem("av_evac"), 1)
                act.wait_ge(sem("wt_mm"), tt + 1)
                A_(WT[:].rearrange("p j t -> p (j t)"), bank(6), ACT.Copy).then_inc(sem("wt_evac"), 1)
                act.wait_ge(sem("u0_mm"), tt + 1)
                A_(U0[:], bank(0), ACT.Copy).then_inc(sem("u0_evac"), 1)
                act.wait_ge(sem("y_mm"), tt + 1)
                A_(yT[:, :, tt * P:(tt + 1) * P], bank(3).rearrange("p (j t) -> p j t", j=NPAIR), ACT.Copy) \
                    .then_inc(sem("y_evac"), 1)
            y_square(1)
            y_root(1)
            y_round(1)
            for u in U_SO:
                hi(u + RING)
            for i, u in enumerate(U_RO):
                act.wait_ge(sem("merge_sum"), i + 1)
                A_(mh[:, 4 * i:4 * i + 4, :], gates[:, 4 * i:4 * i + 4, :], ACT.Copy).then_inc(sem("merged_hi"), 1)
                hi(u + RING)
            act.wait_ge(sem("mem_loaded"), 16)
            deviation("mem", lambda t: mem[:, t, :], lambda t: None)
            for u in U_O[:2]:
                hi(u + RING)
            round_T("mem", "g_mem_2", memh, 0, KD, 0)
            hi(U_O[2] + RING)

            def post(st, base, u, b):
                deviation_halves(st, lambda t, c: bank(b + 2 * t + c), lambda t, c: part_ready(base, u, t, c))

            def pre(st, g, b, filler=0):
                residual_deviation(st)
                if filler:
                    act.wait_ge(sem("units_used"), U_KM[filler - 1] + 1)
                    A_(km[:, 2 * filler - 2:2 * filler, :], bank(3).rearrange("p (f t) -> p f t", f=2), ACT.Copy) \
                        .then_inc(sem("km_evac"), 1)
                round_T(st, g, xh, 0, KD, b)

            post("p1", PART_O, U_O[3], 4)
            pre("n2", "norm_ffn_pre", 0, 1)
            hi(U_O[3] + RING)
            hi(U_KM[0] + RING)
            def ffn(i, n=0):
                later = FF_BODY * n
                hi(U_F["g", i] + RING, n, FF_STEP)
                act.wait_ge(sem("units_used"), U_F["u", i] + 1 + FF_STEP * n)
                if i >= 2:
                    act.wait_ge(sem("ff_out"), i - 1 + later)
                A_(fa[i % 2][:], bank(2 * (i % 2)), ACT.Silu).then_inc(sem("ff_silu"), 1)
                if i == FF_CHUNKS - 1:
                    nc.scalar.preload_act_table_set("sqrt_and_others")
                act.wait_ge(sem("ff_out"), i + 1 + later)
                if i >= 2:
                    act.wait_ge(sem("units_used"), U_F["d", i - 2] + 1 + FF_STEP * n)
                A_(fh[i % 2][:].rearrange("p f t -> p (f t)"), fb[i % 2][:], ACT.Copy).then_inc(sem("ff_hi"), 1)
                hi(U_F["u", i] + RING, n, FF_STEP)
                if i:
                    hi(U_F["d", i - 1] + RING, n, FF_STEP)

            ffn(0)
            ffn(1)
            with act.Fori(0, FF_TURNS) as n:
                for k in range(FF_BODY):
                    ffn(2 + k, n)
            for i in range(2 + FF_TURNS * FF_BODY, FF_CHUNKS):
                ffn(i)
            post("p2", PART_F, U_F["d", FF_CHUNKS - 1], 4)
            pre("n3", "g_mix_2", 0, 2)
            hi(U_F["d", FF_CHUNKS - 1] + RING)
            hi(U_KM[1] + RING)
            for i, u in enumerate(U_QK2):
                after(u)
                dst = (q2, k2)[i // 2]
                A_(dst[:, 2 * (i % 2):2 * (i % 2) + 2, :], bank(i % 2).rearrange("p (f t) -> p f t", f=2), ACT.Copy) \
                    .then_inc(sem("out2_evac"), 1)
            hi(U_V2[0] + RING)
            after(U_V2[1])
            for t in range(NT):
                A_(v2[:, t, :], bank(2 + t), ACT.Copy).then_inc(sem("v2_ready"), 1)
            for i in range(NH + 1):
                if i < NH:
                    if i >= 2:
                        act.wait_ge(sem("d_T"), i - 1)
                    act.wait_ge(sem("d_max"), i + 1)
                    A_(dp[i % 2][:, 0:P], dz[i % 2][:, 0:P], ACT.Exp, bias=col(DMX + i), accum_out=col(DL + i)) \
                        .then_inc(sem("d_p"), 1)
                    A_(dp[i % 2][:, P:384], dz[i % 2][:, P:384], ACT.Exp, bias=col(DMX + NH + i), accum_out=col(DL + NH + i)) \
                        .then_inc(sem("d_p"), 1)
                    if i:
                        hi(FILL2[i - 1] + RING)
                if i < NH:
                    act.wait_ge(sem("units_used"), FILL2[i] + 1)
                    dst = cv[:, i // 2, 2 * (i % 2):2 * (i % 2) + 2, :] if i < 6 else km[:, 2 * (i - 4):2 * (i - 4) + 2, :]
                    A_(dst, bank(i % 2).rearrange("p (f t) -> p f t", f=2), ACT.Copy).then_inc(sem("out2_evac"), 1)
                if 1 <= i <= NH:
                    h = i - 1
                    act.wait_ge(sem("d_T"), h + 1)
                    if h >= 2:
                        act.wait_ge(sem("d_o"), h - 1)
                    A_(dq[h % 2][:], PS[:, (2 + h % 2) * 512:(2 + h % 2) * 512 + 384], ACT.Copy).then_inc(sem("d_q"), 1)
            hi(FILL2[NH - 1] + RING)
            nc.scalar.preload_act_table_set("sqrt_and_others")
            deviation("att", lambda t: att[:, t, :], lambda t: act.wait_ge(sem("att_raw"), t + 1), HW)
            hi(U_VM[0] + RING)
            act.wait_ge(sem("c_gated"), 1)
            A_(cv[:, 1], cv[:, 0], ACT.Square).then_inc(sem("c_sq"), 1)
            round_T("att", "g_attn_out_2", m2h, 0, NPAIR, 6)
            hi(U_VM[1] + RING)
            act.wait_ge(sem("c_ss"), 1)
            A_(crs[:], PS[:, 2 * 512:2 * 512 + SEQ], ACT.Sqrt, scale=1.0 / HW, bias=col(EPS)).then_inc(sem("c_sd"), 1)

            def values_evac(t):
                for c in range(2):
                    part_ready(PART_VM, U_VM[3], t, c)
                    A_(vm[:, t, c * 512:(c + 1) * 512], bank(VM_BANKS[2 * t + c]), ACT.Copy).then_inc(sem("vm_ready"), 1)

            values_evac(0)
            for j in range(NPAIR):
                act.wait_ge(sem("conv_n"), j + 1)
                A_(m2h[:, 4 + j, :], cv[:, 0, j, :], ACT.Copy).then_inc(sem("conv_hi"), 1)
            values_evac(1)
            hi(U_VM[2] + RING)
            hi(U_VM[3] + RING)
            nc.scalar.preload_act_table_set("sqrt_and_others")
            for u in U_O2[:3]:
                hi(u + RING)
            pre("n4", "g_xattn_2", 4)
            hi(U_O2[3] + RING)

            def queries(i):
                act.wait_ge(sem("units_used"), U_QM[i] + 1)
                A_(qm[:, 2 * i:2 * i + 2, :], bank(i % 2).rearrange("p (f t) -> p f t", f=2), ACT.Copy).then_inc(sem("qm_evac"), 1)
                if i < 3:
                    hi(U_QM[i] + RING)

            def exponents(h):
                act.wait_ge(sem("m_max"), h + 1)
                if h >= 2:
                    act.wait_ge(sem("m_T"), h - 1)
                for t in range(NT):
                    A_(mp[h % 2][:, t, :], PS[:, (2 + h % 2) * 512 + t * SEQ:(2 + h % 2) * 512 + (t + 1) * SEQ], ACT.Exp,
                       bias=col(MMX + 2 * h + t), scale=256 ** -0.5, accum_out=col(MSUM + 2 * h + t)) \
                        .then_inc(sem("m_exp"), 1)

            def weights_evac(h):
                act.wait_ge(sem("m_T"), h + 1)
                if h >= 2:
                    act.wait_ge(sem("m_o"), h - 1)
                A_(mq[h % 2][:].rearrange("p m t -> p (m t)"), bank(4 + h % 2), ACT.Copy).then_inc(sem("m_q"), 1)

            def outputs_hi(h):
                act.wait_ge(sem("m_o"), h + 1)
                A_(omh[:, 2 * h:2 * h + 2, :], bank(6 + h % 2).rearrange("p (e t) -> p e t", e=2), ACT.Copy) \
                    .then_inc(sem("om_hi"), 1)

            queries(0)
            nc.scalar.preload_act_table_set("exp_and_others")
            queries(1)
            exponents(0)
            queries(2)
            exponents(1)
            weights_evac(0)
            exponents(2)
            queries(3)
            exponents(3)
            for h in range(1, MEM_HEADS):
                weights_evac(h)
                outputs_hi(h - 1)
            outputs_hi(MEM_HEADS - 1)
            nc.scalar.preload_act_table_set("sqrt_and_others")
            for u in U_QM[3:] + U_OM[:3]:
                hi(u + RING)
            pre("n5", "g_mlp_2", 4)
            hi(U_OM[3] + RING)
            def mlp(i, n=0):
                later = FF2_BODY * n
                act.wait_ge(sem("units_used"), U_M["u", i] + 1 + FF2_STEP * n)
                if i >= 2:
                    act.wait_ge(sem("mlp_sq"), i - 1 + later)
                A_(fa[i % 2][:], bank(i % 2), ACT.Relu).then_inc(sem("mlp_out"), 1)
                act.wait_ge(sem("mlp_sq"), i + 1 + later)
                if i >= 2:
                    act.wait_ge(sem("units_used"), U_M["d", i - 2] + 1 + FF2_STEP * n)
                A_(fh[i % 2][:].rearrange("p f t -> p (f t)"), fb[i % 2][:], ACT.Copy).then_inc(sem("mlp_hi"), 1)
                hi(U_M["u", i] + RING, n, FF2_STEP)
                if i:
                    hi(U_M["d", i - 1] + RING, n, FF2_STEP)

            mlp(0)
            mlp(1)
            with act.Fori(0, FF2_TURNS) as n:
                for k in range(FF2_BODY):
                    mlp(2 + k, n)
            for i in range(2 + FF2_TURNS * FF2_BODY, FF2_CHUNKS):
                mlp(i)
            residual_deviation("fin")

        @block.vector
        def _(dve):
            V = nc.vector
            chain = [0]

            def link(ins):
                chain[0] += 1
                ins.then_inc(sem("dve_chain"), 1)
                dve.wait_ge(sem("dve_chain"), chain[0])

            def lo(u, n=0, step=0):
                if u >= NU:
                    return
                dve.wait_ge(sem("hi_done"), u + 1 + step * n)
                V.tensor_tensor(wlo[u % RING][:], raw[u % RING][:], whi[u % RING][:].bitcast(f32), ALU.subtract) \
                    .then_inc(sem("unit_split"), 1)

            def diagonal(st):
                c = NORM[st]
                for t in range(NT):
                    dve.wait_ge(norm_sem(st, "sd"), nth(st, "sd", t + 1))
                    link(V.reciprocal(col(c + 4 + t), col(c + 2 + t)))
                    V.tensor_scalar(dg[st][:, t, :], C("ident"), col(c + 4 + t), None, ALU.mult).then_inc(norm_sem(st, "dg"), 1)

            def rest_T(st, g, hi_, lo_, f0, nf, b):
                for f in range(nf):
                    dve.wait_ge(norm_sem(st, "hi"), nth(st, "hi", f // 2 * 2 + 2))
                    V.scalar_tensor_tensor(out=lo_[:, f0 + f, :], in0=PS[:, b * 512 + f * SEQ:b * 512 + (f + 1) * SEQ],
                                           scalar=par_col(g, f), in1=hi_[:, f0 + f, :].bitcast(f32),
                                           op0=ALU.mult, op1=ALU.subtract).then_inc(norm_sem(st, "xT"), 1)

            V.memset(col(EPS), 1e-6)
            V.memset(col(GEPS), HD * 1e-5).then_inc(sem("eps_set"), 1)
            dve.wait_ge(sem("ident_loaded"), 16)
            diagonal("n1")
            for half, ready, done in ((slice(0, UNIT // 2), "half_hi", "half_split"), (slice(UNIT // 2, UNIT), "hi_done", "unit_split")):
                dve.wait_ge(sem(ready), 1)
                V.tensor_tensor(wlo[0][:, half], raw[0][:, half], whi[0][:, half].bitcast(f32), ALU.subtract).then_inc(sem(done), 1)
            dve.wait_ge(sem("par_loaded"), 16)
            rest_T("n1", "norm_mix_pre", xh, xl, 0, KD, 4)
            for u in range(1, RING):
                lo(u)
            for i in range(2):
                last = V.memset(stg[i][:, :, 0:1], 0.0)
            last.then_inc(sem("stg_zero"), 1)
            for i, u in enumerate(U_RW):
                lo(u + RING)
                dve.wait_ge(sem("out_evac"), i + 1)
                s = stg[i % 2]
                if i:
                    dve.wait_ge(sem("mixed"), i)
                link(V.tensor_tensor(diff[:], s[:, :, 0:SEQ], s[:, :, 1:SEQ + 1], ALU.subtract))
                for f in range(2):
                    r = RW_TILE[i] + f
                    last = V.scalar_tensor_tensor(out=rw[:, r, :], in0=diff[:, f, :], scalar=par_col("mu_rw", r),
                                                  in1=s[:, f, 1:SEQ + 1], op0=ALU.mult, op1=ALU.add)
                last.then_inc(sem("mixed"), 1)
                if i == 2:
                    dve.wait_ge(sem("mixed"), 3)
                    for j in range(NPAIR):
                        last = V.tensor_scalar(kk[:, j, :], rw[:, 4 + j, :], par_col("k_k", j), None, ALU.mult)
                    link(last)
                    V.tensor_tensor(kq[:], kk[:], kk[:], ALU.mult).then_inc(sem("kk_sq"), 1)
                if i == 4:
                    dve.wait_ge(sem("lora_evac"), 1)
                    dve.wait_ge(sem("msk_loaded"), 16)
                    for j in range(NPAIR):
                        last = V.tensor_tensor_scan(cs[:, j, :], M("reset"), sg[:, j, :], 0.0, ALU.mult, ALU.add)
                    link(last)
                    V.tensor_tensor(sg[:], cs[:], sg[:], ALU.subtract).then_inc(sem("cs"), 1)
                if i == 5:
                    for j in range(NPAIR):
                        link(V.tensor_scalar(eP[:, j, :], ag[:, j, :], 1.0, par_col("k_a", j), ALU.subtract, ALU.mult))
                        last = V.scalar_tensor_tensor(out=rw[:, 4 + j, :], in0=eP[:, j, :], scalar=1.0, in1=rw[:, 4 + j, :],
                                                      op0=ALU.add, op1=ALU.mult)
                    last.then_inc(sem("k_mod"), 1)
                if i == 5:
                    dve.wait_ge(sem("kk_sd"), 1)
                    link(V.tensor_scalar(krs[:], krs[:], 1e-12, None, ALU.max))
                    V.reciprocal(krs[:], krs[:]).then_inc(sem("kk_rs"), 1)
                if i == 6:
                    dve.wait_ge(sem("k_mod"), 1)
                    for j in range(NPAIR):
                        last = V.scalar_tensor_tensor(out=rkk[:, j, :], in0=rw[:, j, :], scalar=par_col("r_k", j),
                                                      in1=rw[:, 4 + j, :], op0=ALU.mult, op1=ALU.mult)
                    last.then_inc(sem("rkk"), 1)
            lo(U_QK[0] + RING)
            dve.wait_ge(sem("kk_spread"), 1)
            V.tensor_tensor(kk[:].rearrange("p j t -> p (j t)"), kk[:].rearrange("p j t -> p (j t)"), PS[:, 4 * 512:6 * 512],
                                 ALU.mult).then_inc(sem("kk_unit"), 1)
            dve.wait_ge(sem("kk_unit"), 1)
            lo(U_QK[1] + RING)
            dve.wait_ge(sem("decays"), 1)
            V.tensor_copy(dec[:], eP[:].rearrange("p j (g c) -> p j g c", c=CHUNK)[:, :, :, CHUNK - 1])
            link(V.scalar_tensor_tensor(out=eX[:].rearrange("p j t -> p (j t)"), in0=kk[:].rearrange("p j t -> p (j t)"), scalar=-1.0,
                                        in1=eX[:].rearrange("p j t -> p (j t)"), op0=ALU.mult, op1=ALU.mult))
            link(V.tensor_tensor(kk[:], kk[:], ag[:], ALU.mult))
            lo(U_QK[2] + RING)
            link(V.tensor_tensor(kk[:], kk[:], eN[:], ALU.mult))
            dve.wait_ge(sem("mixed"), 7)
            V.tensor_tensor(eN[:], rw[:, 4:8, :], eN[:], ALU.mult)
            V.tensor_tensor(eP[:], rw[:, 0:4, :], eP[:], ALU.mult).then_inc(sem("rw_pre"), 1)
            lo(U_QK[3] + RING)
            lo(U_V[0] + RING)
            dve.wait_ge(sem("bonus_mm"), 1)
            dve.wait_ge(sem("rw_pre"), 1)
            for j in range(NPAIR):
                V.tensor_scalar(rw[:, j, :], PS[:, 4 * 512 + j * SEQ:4 * 512 + (j + 1) * SEQ], par_col("lnx_w", j), None, ALU.mult)
            for j in range(2):
                last = V.tensor_tensor(bon[:, 2 * j:2 * j + 2, :], bank(6 + j).rearrange("p (j t) -> p j t", j=2),
                                       rw[:, 8 + 2 * j:10 + 2 * j, :], ALU.mult)
            link(last)
            for j in range(NPAIR):
                last = V.scalar_tensor_tensor(out=rw[:, 4 + j, :], in0=bon[:, j, :], scalar=par_col("lnx_b", j),
                                              in1=PS[:, 4 * 512 + j * SEQ:4 * 512 + (j + 1) * SEQ], op0=ALU.add, op1=ALU.mult)
            last.then_inc(sem("gn_pre"), 1)
            lo(U_V[1] + RING)
            for i in range(NH):
                b = (4 + i % 2) * 512
                s1, s2, s3 = st1[i % 2], st2[i % 2], st3[i % 2]
                dve.wait_ge(sem("sb_ln"), i + 1)
                if i >= 2:
                    dve.wait_ge(sem("sb_arg"), i - 1)
                link(V.scalar_tensor_tensor(out=s2[:], in0=PS[:, b:b + 384], scalar=0.0, in1=s1[:], op0=ALU.max, op1=ALU.add))
                V.tensor_tensor(s2[:], s2[:], M("sb_neg"), ALU.mult).then_inc(sem("sb_lf"), 1)
                if i:
                    lo(U_G[i - 1] + RING)
                dve.wait_ge(sem("sb_arg"), i + 1)
                if i >= 2:
                    dve.wait_ge(sem("sb_w"), i - 1)
                V.scalar_tensor_tensor(out=s3[:], in0=PS[:, b:b + 384], scalar=0.0, in1=C("sb_add"), op0=ALU.min, op1=ALU.add) \
                    .then_inc(sem("sb_arg_read"), 1)
            def mask4(ap):
                return ap.unsqueeze(1).broadcast_to([P, 4, P])

            def pair_evac(tt, qs):
                for q in qs:
                    dst, m = ((XT, "strict"), (AK, "strict"), (RB, "incl"), (RK, "incl"))[q]
                    for g in range(2):
                        dve.wait_ge(sem("pair_mm"), 8 * tt + 2 * q + g + 1)
                        if q == 0 and tt:
                            dve.wait_ge(sem("xm"), 12 * tt)
                        V.tensor_tensor(dst[:, 4 * g:4 * g + 4, :], bank(2 * q + g).rearrange("p (e t) -> p e t", e=4), mask4(M(m)),
                                        ALU.mult).then_inc(sem("pair_evac"), 1)

            def y_center(tt):
                dve.wait_ge(sem("y_sum"), tt + 1)
                t = slice(tt * P, (tt + 1) * P)
                V.scalar_tensor_tensor(out=yc[:, :, t], in0=bank(6).rearrange("p (j t) -> p j t", j=NPAIR), scalar=-1.0 / HD,
                                       in1=yT[:, :, t], op0=ALU.mult, op1=ALU.add).then_inc(sem("yc_ready"), 1)

            def y_inverse(tt):
                dve.wait_ge(sem("y_sd"), tt + 1)
                t = slice(tt * P, (tt + 1) * P)
                V.reciprocal(grs[:, t], grs[:, t]).then_inc(sem("y_rs"), 1)

            def y_scale(tt):
                dve.wait_ge(sem("y_spread"), tt + 1)
                t = slice(tt * P, (tt + 1) * P)
                link(V.tensor_tensor(yc[:, :, t], yc[:, :, t], bank(6).rearrange("p (j t) -> p j t", j=NPAIR), ALU.mult))
                link(V.tensor_tensor(yc[:, :, t], yc[:, :, t], rw[:, 0:4, t], ALU.mult))
                V.tensor_tensor(yc[:, :, t], yc[:, :, t], rw[:, 4:8, t], ALU.add).then_inc(sem("y_done"), 1)

            def y_rest(tt):
                dve.wait_ge(sem("rwo_hi"), tt + 1)
                t = slice(tt * P, (tt + 1) * P)
                V.tensor_tensor(rwol[:, :, t], yc[:, :, t], rwoh[:, :, t].bitcast(f32), ALU.subtract).then_inc(sem("rwo"), 1)

            pair_evac(0, (0, 1))
            for j in range(2):
                dve.wait_ge(sem("sbo_hi"), j + 1)
                V.tensor_tensor(sbol[:, 2 * j:2 * j + 2, :], bank(6 + j).rearrange("p (f t) -> p f t", f=2),
                                sboh[:, 2 * j:2 * j + 2, :].bitcast(f32), ALU.subtract).then_inc(sem("sb_evac"), 2)

            for tt in range(NT):
                if tt:
                    pair_evac(tt, (0, 1))
                for g in range(2):
                    gs = slice(4 * g, 4 * g + 4)
                    dve.wait_ge(sem("xm"), 12 * tt + g + 1)
                    V.tensor_tensor(TT[:, gs, :], Xm[0][:, gs, :], mask4(C("ident")), ALU.add).then_inc(sem("inv_tt"), 1)
                for g in range(2):
                    gs = slice(4 * g, 4 * g + 4)
                    dve.wait_ge(sem("inv_T1"), 2 * tt + g + 1)
                    V.tensor_tensor(Tm[:, gs, :], bank(g).rearrange("p (e t) -> p e t", e=4), mask4(C("ident")), ALU.add) \
                        .then_inc(sem("inv_t"), 1)
                pair_evac(tt, (2, 3))
                if tt == 0:
                    V.memset(St[:, 0], 0.0).then_inc(sem("state"), 1)
                    lo(U_G[NH - 1] + RING)
                for v in range(1, 6):
                    for g in range(2):
                        gs = slice(4 * g, 4 * g + 4)
                        dve.wait_ge(sem("inv_up"), 10 * tt + 2 * (v - 1) + g + 1)
                        if v < 5:
                            part = halves(Tm[:, gs, :].rearrange("p e t -> p (e t)"), v, 0)
                            V.tensor_tensor(part, part, bank(2 + g)[:, 0:4 * HD].rearrange("p (a b) -> p a b", b=2 ** v), ALU.add) \
                                .then_inc(sem("inv_t"), 1)
                        part = halves(TT[:, gs, :].rearrange("p e t -> p (e t)"), v, 1)
                        V.tensor_tensor(part, part, bank(4 + g)[:, 0:4 * HD].rearrange("p (a b) -> p a b", b=2 ** v), ALU.add) \
                            .then_inc(sem("inv_tt"), 1)
                    if tt and v in (2, 3, 4):
                        (y_center, y_inverse, y_scale)[v - 2](tt - 1)
                if tt:
                    y_rest(tt - 1)
                for c in range(2):
                    g = 2 * tt + c
                    r = slice(CHUNK * c, CHUNK * c + CHUNK)
                    dve.wait_ge(sem("u_mm"), g + 1)
                    dve.wait_ge(sem("u0_evac"), tt + 1)
                    V.tensor_tensor(Uc[r, :], PS[r, 512:1024], U0[r, :], ALU.add).then_inc(sem("u_ready"), 1)
                    if g < 3:
                        dve.wait_ge(sem("ds_mm"), g + 1)
                        link(V.tensor_tensor(dS[:], bank(2).rearrange("p (j t) -> p j t", j=NPAIR), St[:, g], ALU.add))
                        for j in range(NPAIR):
                            V.scalar_tensor_tensor(out=St[:, g + 1, j, :], in0=dS[:, j, :], scalar=dec[:, j, g:g + 1],
                                                          in1=C("blockones"), op0=ALU.mult, op1=ALU.mult).then_inc(sem("state"), 1)
            y_center(1)
            y_inverse(1)
            y_scale(1)
            dve.wait_ge(sem("gates_ready"), 4)

            def gate(i, u, base):
                dve.wait_ge(sem("units_used"), u + 1)
                for c in range(2):
                    g = gates[:, base + 4 * i + 2 * c:base + 4 * i + 2 * c + 2, :].rearrange("p f t -> p (f t)")
                    last = V.tensor_tensor(g, bank(2 * i + c), g, ALU.mult)
                return last

            gate(0, U_SO[0], 0).then_inc(sem("merge_a"), 1)
            y_rest(1)
            lo(U_SO[0] + RING)
            gate(1, U_SO[1], 0).then_inc(sem("merge_a"), 1)
            lo(U_SO[1] + RING)
            for i, u in enumerate(U_RO):
                link(gate(i, u, 8))
                V.tensor_tensor(gates[:, 4 * i:4 * i + 4, :], gates[:, 4 * i:4 * i + 4, :], gates[:, 8 + 4 * i:12 + 4 * i, :], ALU.add) \
                    .then_inc(sem("merge_sum"), 1)
                dve.wait_ge(sem("merged_hi"), i + 1)
                V.tensor_tensor(ml[:, 4 * i:4 * i + 4, :], gates[:, 4 * i:4 * i + 4, :], mh[:, 4 * i:4 * i + 4, :].bitcast(f32),
                                ALU.subtract).then_inc(sem("merged"), 1)
                lo(u + RING)
            diagonal("mem")
            for u in U_O[:2]:
                lo(u + RING)
            rest_T("mem", "g_mem_2", memh, meml, 0, KD, 0)

            def part_ready(base, u, t, c):
                if (t, c) == (NT - 1, 1):
                    dve.wait_ge(sem("units_used"), u + 1)
                else:
                    dve.wait_ge(sem("part_done"), base + 2 * t + c + 1)

            def post(st, gain, loaded, b, then):
                n = NORM[st]
                dve.wait_ge(sem(loaded), 16)
                dve.wait_ge(sem("x_loaded0"), 32)
                for t in range(NT):
                    for c in range(2):
                        h = slice(512 * c, 512 * c + 512)
                        dve.wait_ge(norm_sem(st, "sq"), nth(st, "sq", 2 * t + c + 1))
                        V.tensor_tensor(tmp[:, t, h], bank(b + 2 * t + c), gain[:, h], ALU.mult).then_inc(norm_sem(st, "y"), 1)
                    dve.wait_ge(norm_sem(st, "sd"), nth(st, "sd", t + 1))
                    link(V.reciprocal(col(n + 4 + t), col(n + 2 + t)))
                    dve.wait_ge(norm_sem(st, "y"), nth(st, "y", 2 * t + 2))
                    for c in range(2):
                        h = slice(512 * c, 512 * c + 512)
                        V.scalar_tensor_tensor(out=xres[:, t, h], in0=tmp[:, t, h], scalar=col(n + 4 + t), in1=xres[:, t, h],
                                               op0=ALU.mult, op1=ALU.add).then_inc(norm_sem(then, "x"), 1)

            def residual(base, u, b, then):
                for t in range(NT):
                    for c in range(2):
                        h = slice(512 * c, 512 * c + 512)
                        part_ready(base, u, t, c)
                        V.tensor_tensor(xres[:, t, h], xres[:, t, h], bank(b + 2 * t + c), ALU.add).then_inc(norm_sem(then, "x"), 1)

            def pre(st, g, b, u):
                diagonal(st)
                if u != U_F["d", FF_CHUNKS - 1]:
                    lo(u - 1 + RING)
                rest_T(st, g, xh, xl, 0, KD, b)
                lo(u + RING)
                if u == U_O[3]:
                    lo(U_KM[0] + RING)
                if u == U_F["d", FF_CHUNKS - 1]:
                    lo(U_KM[1] + RING)

            post("p1", gmix, "gmix_loaded", 4, "n2")
            pre("n2", "norm_ffn_pre", 0, U_O[3])
            def ffn(i, n=0):
                later = FF_BODY * n
                lo(U_F["g", i] + RING, n, FF_STEP)
                dve.wait_ge(sem("ff_silu"), i + 1 + later)
                if i >= 2:
                    dve.wait_ge(sem("ff_hi"), i - 1 + later)
                V.tensor_tensor(fb[i % 2][:], fa[i % 2][:], bank(2 * (i % 2) + 1), ALU.mult).then_inc(sem("ff_out"), 1)
                dve.wait_ge(sem("ff_hi"), i + 1 + later)
                V.tensor_tensor(fl[i % 2][:].rearrange("p f t -> p (f t)"), fb[i % 2][:],
                                fh[i % 2][:].rearrange("p f t -> p (f t)").bitcast(f32), ALU.subtract).then_inc(sem("ff_h"), 1)
                lo(U_F["u", i] + RING, n, FF_STEP)
                if i:
                    lo(U_F["d", i - 1] + RING, n, FF_STEP)

            ffn(0)
            ffn(1)
            with dve.Fori(0, FF_TURNS) as n:
                for k in range(FF_BODY):
                    ffn(2 + k, n)
            for i in range(2 + FF_TURNS * FF_BODY, FF_CHUNKS):
                ffn(i)
            post("p2", gffn, "gffn_loaded", 4, "n3")
            pre("n3", "g_mix_2", 0, U_F["d", FF_CHUNKS - 1])
            for u in U_QK2 + U_V2:
                lo(u + RING)
            for i in range(NH):
                if i < NH:
                    b = (4 + i % 2) * 512
                    z = dz[i % 2]
                    dve.wait_ge(sem("d_z"), i + 1)
                    if i >= 2:
                        dve.wait_ge(sem("d_p"), 2 * (i - 1))
                    V.scalar_tensor_tensor(out=z[:], in0=PS[:, b:b + 384], scalar=HD ** -0.5, in1=C("dil"), op0=ALU.mult, op1=ALU.add) \
                        .then_inc(sem("d_z_read"), 1)
                    dve.wait_ge(sem("d_z_read"), i + 1)
                    V.tensor_reduce(out=col(DMX + i), in_=z[:, 0:P], axis=AX.X, op=ALU.max, negate=True)
                    V.tensor_reduce(out=col(DMX + NH + i), in_=z[:, P:384], axis=AX.X, op=ALU.max, negate=True) \
                        .then_inc(sem("d_max"), 1)
                if i:
                    lo(FILL2[i - 1] + RING)
            lo(FILL2[NH - 1] + RING)
            dve.wait_ge(sem("out2_evac"), 10)
            link(V.tensor_tensor(cv[:, 1], cv[:, 1], cv[:, 2], ALU.mult))
            for j in range(NPAIR):
                last = V.tensor_scalar(cv[:, 2, j, :], cv[:, 1, j, :], par_col("conv_w_2", 8 + j), None, ALU.mult)
            link(last)

            def tap(n):
                sh = 2 - n
                for j in range(NPAIR):
                    last = V.scalar_tensor_tensor(out=cv[:, 2, j, sh:SEQ], in0=cv[:, 1, j, 0:SEQ - sh],
                                                  scalar=par_col("conv_w_2", 4 * n + j), in1=cv[:, 2, j, sh:SEQ],
                                                  op0=ALU.mult, op1=ALU.add)
                link(last)

            dve.wait_ge(sem("d_o"), NH)
            dve.wait_ge(sem("d_p"), 2 * NH)
            link(V.reciprocal(col(DRL, 16), col(DL, 16)))
            for t in range(NT):
                V.tensor_tensor(att[:, t, :].rearrange("p (h e) -> p h e", h=NH), bank(6 + t).rearrange("p (h e) -> p h e", h=NH),
                                col(DRL + NH * t, NH).unsqueeze(2).broadcast_to([P, NH, HD]), ALU.mult).then_inc(sem("att_raw"), 1)
            tap(1)
            diagonal("att")
            tap(0)
            V.tensor_tensor(cv[:, 0], cv[:, 0], cv[:, 2], ALU.mult).then_inc(sem("c_gated"), 1)
            rest_T("att", "g_attn_out_2", m2h, m2l, 0, NPAIR, 6)
            for u in U_VM[:2]:
                lo(u + RING)
            dve.wait_ge(sem("c_sd"), 1)
            link(V.reciprocal(crs[:], crs[:]))
            for j in range(NPAIR):
                V.scalar_tensor_tensor(out=cv[:, 0, j, :], in0=cv[:, 0, j, :], scalar=par_col("g_conv_out_2", j), in1=crs[:],
                                       op0=ALU.mult, op1=ALU.mult).then_inc(sem("conv_n"), 1)
            for j in range(NPAIR):
                dve.wait_ge(sem("conv_hi"), j + 1)
                V.tensor_tensor(m2l[:, 4 + j, :], cv[:, 0, j, :], m2h[:, 4 + j, :].bitcast(f32), ALU.subtract) \
                    .then_inc(sem("conv_xT"), 1)
            lo(U_VM[2] + RING)
            lo(U_VM[3] + RING)
            for u in U_O2[:2]:
                lo(u + RING)
            residual(PART_O2, U_O2[3], 0, "n4")
            pre("n4", "g_xattn_2", 4, U_O2[3])
            for u in U_QM[:2]:
                lo(u + RING)
            for h in range(MEM_HEADS):
                dve.wait_ge(sem("m_z"), h + 1)
                link(V.tensor_reduce(out=col(MMX + 2 * h, 2), in_=bank(2 + h % 2).rearrange("p (t m) -> p t m", t=2), axis=AX.X,
                                     op=ALU.max, negate=True))
                V.tensor_scalar(col(MMX + 2 * h, 2), col(MMX + 2 * h, 2), 256 ** -0.5, None, ALU.mult).then_inc(sem("m_max"), 1)
                dve.wait_ge(sem("m_exp"), 2 * h + 2)
                link(V.reciprocal(col(MSUM + 2 * h, 2), col(MSUM + 2 * h, 2)))
                for t in range(NT):
                    last = V.tensor_scalar(mp[h % 2][:, t, :], mp[h % 2][:, t, :], col(MSUM + 2 * h + t), None, ALU.mult)
                last.then_inc(sem("m_p"), 1)
                if h == 1:
                    lo(U_QM[2] + RING)
            for h in range(MEM_HEADS):
                dve.wait_ge(sem("om_hi"), h + 1)
                V.tensor_tensor(oml[:, 2 * h:2 * h + 2, :], bank(6 + h % 2).rearrange("p (e t) -> p e t", e=2),
                                omh[:, 2 * h:2 * h + 2, :].bitcast(f32), ALU.subtract).then_inc(sem("om"), 2)
            for u in U_QM[3:] + U_OM[:2]:
                lo(u + RING)
            residual(PART_OM, U_OM[3], 0, "n5")
            pre("n5", "g_mlp_2", 4, U_OM[3])
            def mlp(i, n=0):
                later = FF2_BODY * n
                dve.wait_ge(sem("mlp_out"), i + 1 + later)
                if i >= 2:
                    dve.wait_ge(sem("mlp_hi"), i - 1 + later)
                V.tensor_tensor(fb[i % 2][:], fa[i % 2][:], fa[i % 2][:], ALU.mult).then_inc(sem("mlp_sq"), 1)
                dve.wait_ge(sem("mlp_hi"), i + 1 + later)
                V.tensor_tensor(fl[i % 2][:].rearrange("p f t -> p (f t)"), fb[i % 2][:],
                                fh[i % 2][:].rearrange("p f t -> p (f t)").bitcast(f32), ALU.subtract).then_inc(sem("mlp_h"), 1)
                lo(U_M["u", i] + RING, n, FF2_STEP)
                if i:
                    lo(U_M["d", i - 1] + RING, n, FF2_STEP)

            mlp(0)
            mlp(1)
            with dve.Fori(0, FF2_TURNS) as n:
                for k in range(FF2_BODY):
                    mlp(2 + k, n)
            for i in range(2 + FF2_TURNS * FF2_BODY, FF2_CHUNKS):
                mlp(i)
            residual(PART_M, U_M["d", FF2_CHUNKS - 1], 4, "fin")
            c = NORM["fin"]
            dve.wait_ge(sem("gfin_loaded"), 16)
            for t in range(NT):
                dve.wait_ge(norm_sem("fin", "sd"), nth("fin", "sd", t + 1))
                link(V.reciprocal(col(c + 4 + t), col(c + 2 + t)))
                for h in (slice(0, 512), slice(512, D)):
                    V.scalar_tensor_tensor(out=xn[:, t, h], in0=xres[:, t, h], scalar=col(c + 4 + t), in1=gfin[:, h],
                                           op0=ALU.mult, op1=ALU.mult).then_inc(sem("result"), 1)


_INS = ["x", "w_in", "w_up", "a_up", "g_up", "w_sb_out", "w_rw_out", "w_o", "norm_mix_post", "w_ffn_gate", "w_ffn_up",
        "w_ffn_down", "norm_ffn_post", "mem_2", "w_in_2", "w_out_2", "w_q_mem_2", "w_kv_mem_2", "w_o_mem_2", "w_up_2",
        "w_down_2", "g_final_2"]


def kernel(**inputs):
    import numpy as _np
    import concourse.bacc as _bacc
    from concourse import mybir as _mybir
    from concourse.bass_utils import run_bass_kernel_spmd as _run

    nc = _bacc.Bacc("TRN2", target_bir_lowering=False, num_devices=1)
    arrays, A = {}, {}
    given = {n: _np.ascontiguousarray(inputs[n]) for n in _INS}
    rows = [_np.ascontiguousarray(inputs[n]).reshape(k, P) for n, k in PARAM_ROWS]
    given["params"] = _np.ascontiguousarray(_np.concatenate(rows, 0).T)
    given["consts"], given["masks"] = CONSTS, MASKS
    for name, a in given.items():
        arrays[f"in_{name}_dram"] = a
        A[name] = nc.dram_tensor(f"in_{name}_dram", a.shape, _mybir.dt.from_np(a.dtype), kind="ExternalInput").ap()
    out = nc.dram_tensor("out_0_dram", (1, SEQ, D), _mybir.dt.float32, kind="ExternalOutput").ap()
    block_kernel(nc, A, out)
    r = _run(nc, [arrays], core_ids=[0])
    return r.results[0]["out_0_dram"]
```
